# Optimizing a Trainium2 kernel written in Bass

```python
import math
import jax, jax.numpy as jnp
from jax import lax
import numpy as np

D_MODEL = 1024
BATCH = 1
SEQ = 256
DEPTH = 2

GDN_HEADS = 4
GDN_DK = 64
GDN_DV = 64
GDN_QK_W = GDN_HEADS * GDN_DK
GDN_V_W = GDN_HEADS * GDN_DV
GDN_QKV_W = 2 * GDN_QK_W + GDN_V_W
GDN_CONV = 4
GDN_CHUNK = 64
S5_WIDTH = 256
S5_GROUP_CH = 16
S5_GROUPS = S5_WIDTH // S5_GROUP_CH
S5_STATE = 64
DIFF_HEADS = 4
DIFF_DQK = 64
DIFF_DV = 2 * DIFF_DQK
DIFF_QK_W = DIFF_HEADS * 2 * DIFF_DQK
DIFF_V_W = DIFF_HEADS * DIFF_DV
Q_BLOCK = 128
MIX_WIDTH = GDN_V_W + S5_WIDTH + DIFF_V_W
IN_SIZES = (GDN_QKV_W, GDN_V_W, GDN_HEADS, GDN_HEADS, S5_WIDTH, DIFF_QK_W, DIFF_QK_W, DIFF_V_W)
IN_WIDTH = sum(IN_SIZES)
PEER_HEADS = 8
PEER_DQ = 128
PEER_DHALF = PEER_DQ // 2
N_KEYS = 128
N_EXPERTS = N_KEYS * N_KEYS
PEER_TOPK = 16
PEER_BLOCK = 128
NORM_EPS = 1e-6

kernel_name = "hybrid_gdn_s5_diffattn_peer"

def rms_norm(x, gain):
    xf = x.astype(jnp.float32)
    y = xf * lax.rsqrt(jnp.mean(xf * xf, axis=-1, keepdims=True) + NORM_EPS)
    return (y * gain.astype(jnp.float32)).astype(x.dtype)

def l2_normalize(t):
    return t * lax.rsqrt(jnp.sum(t * t, axis=-1, keepdims=True) + 1e-6)

def chunk_gated_delta(q, k, v, g, beta):
    bn, seq, heads, dk = q.shape
    dv = v.shape[-1]
    nc = seq // GDN_CHUNK

    def chunks(t):
        t = t.reshape((bn, nc, GDN_CHUNK, heads) + t.shape[3:])
        return jnp.moveaxis(t, (1, 3), (0, 2))

    q = chunks(q * dk ** -0.5)
    k = chunks(k)
    v = chunks(v)
    beta = chunks(beta)
    g = jnp.cumsum(chunks(g), axis=-1)
    incl = jnp.tril(jnp.ones((GDN_CHUNK, GDN_CHUNK), bool))
    strict = jnp.tril(jnp.ones((GDN_CHUNK, GDN_CHUNK), bool), -1)
    decay = jnp.exp(jnp.where(incl, g[..., :, None] - g[..., None, :], -jnp.inf))
    kk = jnp.einsum('nbhid,nbhjd->nbhij', k, k)
    lower = jnp.where(strict, beta[..., :, None] * kk * decay, 0.0)
    eye = jnp.eye(GDN_CHUNK, dtype=jnp.float32)
    t_inv = lax.linalg.triangular_solve(eye + lower, jnp.broadcast_to(eye, lower.shape),
                                        left_side=True, lower=True)
    u = t_inv @ (v * beta[..., None])
    w = t_inv @ (k * (beta * jnp.exp(g))[..., None])
    qk = jnp.where(incl, jnp.einsum('nbhid,nbhjd->nbhij', q, k) * decay, 0.0)

    def step(state, inp):
        q_c, k_c, u_c, w_c, g_c, qk_c = inp
        v_new = u_c - w_c @ state
        out = (q_c * jnp.exp(g_c)[..., None]) @ state + qk_c @ v_new
        g_last = g_c[..., -1:]
        state = state * jnp.exp(g_last)[..., None] + jnp.einsum(
            'bhck,bhcv->bhkv', k_c * jnp.exp(g_last - g_c)[..., None], v_new)
        return state, out

    state0 = jnp.zeros((bn, heads, dk, dv), jnp.float32)
    _, out = lax.scan(step, state0, (q, k, u, w, g, qk))
    return jnp.moveaxis(out, (0, 2), (1, 3)).reshape(bn, seq, heads, dv)

def gdn_mixer(qkv, z, a, b, conv_w, a_log, dt_bias, norm_g):
    bn, seq, ch = qkv.shape
    qkv = jax.nn.silu(lax.conv_general_dilated(
        qkv, conv_w.astype(qkv.dtype)[:, None, :], (1,), [(GDN_CONV - 1, 0)],
        dimension_numbers=('NWC', 'WIO', 'NWC'), feature_group_count=ch))
    q, k, v = jnp.split(qkv.astype(jnp.float32), [GDN_QK_W, 2 * GDN_QK_W], axis=-1)
    q = l2_normalize(q.reshape(bn, seq, GDN_HEADS, GDN_DK))
    k = l2_normalize(k.reshape(bn, seq, GDN_HEADS, GDN_DK))
    v = v.reshape(bn, seq, GDN_HEADS, GDN_DV)
    beta = jax.nn.sigmoid(b.astype(jnp.float32))
    g = -jnp.exp(a_log.astype(jnp.float32)) * jax.nn.softplus(a.astype(jnp.float32) + dt_bias.astype(jnp.float32))
    o = chunk_gated_delta(q, k, v, g, beta)
    o = rms_norm(o, norm_g) * jax.nn.silu(z.astype(jnp.float32).reshape(bn, seq, GDN_HEADS, GDN_DV))
    return o.reshape(bn, seq, GDN_V_W).astype(z.dtype)

def _lin_combine(e1, e2):
    a1, b1 = e1
    a2, b2 = e2
    return a1 * a2, a2 * b1 + b2

def s5_mixer(u, lam_re, lam_im, b_re, b_im, c_re, c_im, d_skip, log_step, glu_w, glu_b):
    bn, seq, _ = u.shape
    uf = u.astype(jnp.float32)
    lam = lax.complex(lam_re.astype(jnp.float32), lam_im.astype(jnp.float32))
    step = jnp.exp(log_step.astype(jnp.float32))[:, None]
    a_bar = jnp.exp(lam * step)
    b_bar = ((a_bar - 1.0) / lam)[:, :, None] * lax.complex(b_re.astype(jnp.float32), b_im.astype(jnp.float32))
    bu = jnp.einsum('blgc,gnc->blgn', uf.reshape(bn, seq, S5_GROUPS, S5_GROUP_CH), b_bar)
    _, states = lax.associative_scan(_lin_combine, (jnp.broadcast_to(a_bar, bu.shape), bu), axis=1)
    c = lax.complex(c_re.astype(jnp.float32), c_im.astype(jnp.float32))
    y = jnp.einsum('blgn,gcn->blgc', states, c).real.reshape(bn, seq, S5_WIDTH) + d_skip.astype(jnp.float32) * uf
    y = jax.nn.gelu(y).astype(u.dtype)
    zg = y @ glu_w + glu_b
    z_val, z_gate = jnp.split(zg, 2, axis=-1)
    return z_val * jax.nn.sigmoid(z_gate)

def diff_attn_mixer(q, k, v, lq1, lk1, lq2, lk2, norm_g, lam_init):
    bn, seq, _ = q.shape
    q = q.reshape(bn, seq, DIFF_HEADS, 2, DIFF_DQK)
    k = k.reshape(bn, seq, DIFF_HEADS, 2, DIFF_DQK)
    vf = v.reshape(bn, seq, DIFF_HEADS, DIFF_DV).astype(jnp.float32)
    f32 = jnp.float32
    lam = (jnp.exp(jnp.sum(lq1.astype(f32) * lk1.astype(f32)))
           - jnp.exp(jnp.sum(lq2.astype(f32) * lk2.astype(f32))) + lam_init)
    nb = seq // Q_BLOCK
    q_blocks = q.reshape(bn, nb, Q_BLOCK, DIFF_HEADS, 2, DIFF_DQK).swapaxes(0, 1)
    scale = DIFF_DQK ** -0.5
    k_pos = jnp.arange(seq)

    def block(args):
        blk, qb = args
        s = jnp.einsum('bqhmd,bkhmd->bhmqk', qb, k).astype(f32) * scale
        q_pos = blk * Q_BLOCK + jnp.arange(Q_BLOCK)
        s = jnp.where(k_pos[None, :] <= q_pos[:, None], s, -jnp.inf)
        p = jax.nn.softmax(s, axis=-1)
        p_diff = p[:, :, 0] - lam * p[:, :, 1]
        return jnp.einsum('bhqk,bkhe->bqhe', p_diff, vf)

    o = lax.map(block, (jnp.arange(nb), q_blocks))
    o = o.swapaxes(0, 1).reshape(bn, seq, DIFF_HEADS, DIFF_DV)
    o = rms_norm(o, norm_g) * (1.0 - lam_init)
    return o.reshape(bn, seq, DIFF_V_W).astype(v.dtype)

def peer_ffn(x, wq, keys, u_tab, v_tab):
    bn, seq, dm = x.shape
    nb = seq // PEER_BLOCK
    xb = x.reshape(bn, nb, PEER_BLOCK, dm).swapaxes(0, 1)

    def block(xt):
        q = (xt @ wq).reshape(bn, PEER_BLOCK, PEER_HEADS, 2, PEER_DHALF)
        s = jnp.einsum('bthpd,hpnd->bthpn', q, keys).astype(jnp.float32)
        sv, si = lax.top_k(s, PEER_TOPK)
        cand_s = (sv[..., 0, :, None] + sv[..., 1, None, :]).reshape(bn, PEER_BLOCK, PEER_HEADS, PEER_TOPK * PEER_TOPK)
        cand_e = (si[..., 0, :, None] * N_KEYS + si[..., 1, None, :]).reshape(bn, PEER_BLOCK, PEER_HEADS, PEER_TOPK * PEER_TOPK)
        top_s, top_i = lax.top_k(cand_s, PEER_TOPK)
        expert = jnp.take_along_axis(cand_e, top_i, axis=-1)
        gate = jax.nn.softmax(top_s, axis=-1)
        act = jax.nn.gelu(jnp.einsum('bthkd,btd->bthk', u_tab[expert], xt).astype(jnp.float32))
        return jnp.einsum('bthk,bthkd->btd', (gate * act).astype(xt.dtype), v_tab[expert])

    y = lax.map(block, xb)
    return y.swapaxes(0, 1).reshape(bn, seq, dm)

def setup_inputs(seed: int = 0) -> dict:
    key = jax.random.key(seed)
    ks = iter(jax.random.split(key, 32))
    f32 = jnp.float32
    nrm = lambda shape, scale: scale * jax.random.normal(next(ks), shape, f32)
    unif = lambda shape, lo, hi: jax.random.uniform(next(ks), shape, f32, lo, hi)
    x = nrm((BATCH, SEQ, D_MODEL), 1.0)
    norm1_g = 1.0 + nrm((DEPTH, D_MODEL), 0.02)
    w_in = nrm((DEPTH, D_MODEL, IN_WIDTH), D_MODEL ** -0.5)
    gdn_conv_w = nrm((DEPTH, GDN_CONV, GDN_QKV_W), GDN_CONV ** -0.5)
    gdn_a_log = jnp.log(unif((DEPTH, GDN_HEADS), 1.0, 16.0))
    dt = jnp.exp(unif((DEPTH, GDN_HEADS), math.log(1e-3), math.log(1e-1)))
    gdn_dt_bias = dt + jnp.log(-jnp.expm1(-dt))
    gdn_norm_g = 1.0 + nrm((DEPTH, GDN_DV), 0.02)
    s5_lambda_re = -0.5 + nrm((DEPTH, S5_GROUPS, S5_STATE), 0.01)
    s5_lambda_im = math.pi * jnp.arange(S5_STATE, dtype=f32) + nrm((DEPTH, S5_GROUPS, S5_STATE), 0.01)
    s5_b_re = nrm((DEPTH, S5_GROUPS, S5_STATE, S5_GROUP_CH), (2 * S5_GROUP_CH) ** -0.5)
    s5_b_im = nrm((DEPTH, S5_GROUPS, S5_STATE, S5_GROUP_CH), (2 * S5_GROUP_CH) ** -0.5)
    s5_c_re = nrm((DEPTH, S5_GROUPS, S5_GROUP_CH, S5_STATE), (2 * S5_STATE) ** -0.5)
    s5_c_im = nrm((DEPTH, S5_GROUPS, S5_GROUP_CH, S5_STATE), (2 * S5_STATE) ** -0.5)
    s5_d = nrm((DEPTH, S5_WIDTH), 1.0)
    s5_log_step = unif((DEPTH, S5_GROUPS), math.log(1e-3), math.log(1e-1))
    s5_glu_w = nrm((DEPTH, S5_WIDTH, 2 * S5_WIDTH), S5_WIDTH ** -0.5)
    s5_glu_b = nrm((DEPTH, 2 * S5_WIDTH), 0.01)
    diff_lq1 = nrm((DEPTH, DIFF_DQK), 0.1)
    diff_lk1 = nrm((DEPTH, DIFF_DQK), 0.1)
    diff_lq2 = nrm((DEPTH, DIFF_DQK), 0.1)
    diff_lk2 = nrm((DEPTH, DIFF_DQK), 0.1)
    diff_norm_g = 1.0 + nrm((DEPTH, DIFF_DV), 0.02)
    w_out = nrm((DEPTH, MIX_WIDTH, D_MODEL), MIX_WIDTH ** -0.5)
    norm2_g = 1.0 + nrm((DEPTH, D_MODEL), 0.02)
    peer_wq = nrm((DEPTH, D_MODEL, PEER_HEADS * PEER_DQ), D_MODEL ** -0.5)
    peer_keys = nrm((DEPTH, PEER_HEADS, 2, N_KEYS, PEER_DHALF), PEER_DHALF ** -0.5)
    peer_u = nrm((DEPTH, N_EXPERTS, D_MODEL), D_MODEL ** -0.5)
    peer_v = nrm((DEPTH, N_EXPERTS, D_MODEL), PEER_HEADS ** -0.5)
    final_g = 1.0 + nrm((D_MODEL,), 0.02)
    return {"x": x, "norm1_g": norm1_g, "w_in": w_in, "gdn_conv_w": gdn_conv_w, "gdn_a_log": gdn_a_log,
            "gdn_dt_bias": gdn_dt_bias, "gdn_norm_g": gdn_norm_g, "s5_lambda_re": s5_lambda_re,
            "s5_lambda_im": s5_lambda_im, "s5_b_re": s5_b_re, "s5_b_im": s5_b_im, "s5_c_re": s5_c_re,
            "s5_c_im": s5_c_im, "s5_d": s5_d, "s5_log_step": s5_log_step, "s5_glu_w": s5_glu_w,
            "s5_glu_b": s5_glu_b, "diff_lq1": diff_lq1, "diff_lk1": diff_lk1, "diff_lq2": diff_lq2,
            "diff_lk2": diff_lk2, "diff_norm_g": diff_norm_g, "w_out": w_out, "norm2_g": norm2_g,
            "peer_wq": peer_wq, "peer_keys": peer_keys, "peer_u": peer_u, "peer_v": peer_v, "final_g": final_g}

def reference(x, norm1_g, w_in, gdn_conv_w, gdn_a_log, gdn_dt_bias, gdn_norm_g, s5_lambda_re, s5_lambda_im,
              s5_b_re, s5_b_im, s5_c_re, s5_c_im, s5_d, s5_log_step, s5_glu_w, s5_glu_b, diff_lq1, diff_lk1,
              diff_lq2, diff_lk2, diff_norm_g, w_out, norm2_g, peer_wq, peer_keys, peer_u, peer_v, final_g):
    split_at = np.cumsum(IN_SIZES)[:-1].tolist()
    h = x
    for layer in range(DEPTH):
        lam_init = 0.8 - 0.6 * math.exp(-0.3 * layer)
        hn = rms_norm(h, norm1_g[layer])
        proj = hn @ w_in[layer]
        qkv_a, z_a, a_a, b_a, u_s, q_c, k_c, v_c = jnp.split(proj, split_at, axis=-1)
        o_a = gdn_mixer(qkv_a, z_a, a_a, b_a, gdn_conv_w[layer], gdn_a_log[layer], gdn_dt_bias[layer],
                        gdn_norm_g[layer])
        o_b = s5_mixer(u_s, s5_lambda_re[layer], s5_lambda_im[layer], s5_b_re[layer], s5_b_im[layer],
                       s5_c_re[layer], s5_c_im[layer], s5_d[layer], s5_log_step[layer], s5_glu_w[layer],
                       s5_glu_b[layer])
        o_c = diff_attn_mixer(q_c, k_c, v_c, diff_lq1[layer], diff_lk1[layer], diff_lq2[layer], diff_lk2[layer],
                              diff_norm_g[layer], lam_init)
        h = h + jnp.concatenate([o_a, o_b, o_c], axis=-1) @ w_out[layer]
        h = h + peer_ffn(rms_norm(h, norm2_g[layer]), peer_wq[layer], peer_keys[layer], peer_u[layer], peer_v[layer])
    return rms_norm(h, final_g)


_drawn_inputs = setup_inputs


def setup_inputs(seed=0):
    import zlib

    import numpy as np

    out = dict(_drawn_inputs(seed))
    spreads = {}
    factors = {'gdn_norm_g': 2.908,
     's5_lambda_re': 200.0,
     's5_glu_b': 3.737,
     'final_g': 20.569,
     's5_lambda_im': 29.153,
     's5_b_re': 36.368,
     's5_b_im': 38.064,
     's5_c_re': 35.616,
     's5_c_im': 38.936,
     's5_log_step': 31.512,
     'diff_lk2': 2.794}
    for name, (base, spread) in spreads.items():
        noise = np.random.default_rng([zlib.crc32(name.encode()), seed]).standard_normal(out[name].shape)
        drawn = base * np.exp(spread * noise) if base else spread * noise
        out[name] = __import__('jax').numpy.asarray(drawn.astype(out[name].dtype))
    for name, factor in factors.items():
        out[name] = (out[name] * factor).astype(out[name].dtype)
    return out
```

```python
from contextlib import ExitStack

import numpy as np

import concourse.bass as bass
from concourse import mybir

P = 128
D = 1024
KT = D // P
SEQ = 256
TB = SEQ // P
DEPTH = 2
HEADS = 4
DK = 64
CONV = 4
QKV = 3 * HEADS * DK
CT = QKV // P
GROUPS, GCH, NSTATE = 16, 16, 64
MT = GROUPS * NSTATE // P
DV2 = 128
PH = 8
NKEY = 128
TOPK = 16
NEXP = NKEY * NKEY
EPS = 1e-6
BLK = 256
NEG = -1.0e30
LOWEST = -3.0e38

F32 = mybir.dt.float32
U32 = mybir.dt.uint32
ALU = mybir.AluOpType
ACT = mybir.ActivationFunctionType
AX = mybir.AxisListType.X

IN_COLS = {"u": 1032, "qkv0": 0, "qkv1": 256, "qkv2": 512, "z": 768,
           "v0": 2312, "v1": 2568, "q0": 1288, "q1": 1544, "k0": 1800, "k1": 2056}
BLOCKS = list(IN_COLS) + [f"out{i}" for i in range(4)] + [f"wq{i}" for i in range(4)]
NB = len(BLOCKS)
RING = 8
FILLS = ["u", "qkv0", "qkv1", "qkv2", "ab", "z", "v0", "v1", "q0", "q1", "k0", "k1"]


def fields(*pairs):
    at, out = 0, {}
    for name, n in pairs:
        out[name] = (at, at + n)
        at += n
    return out, at


COLS, NCOLS = fields(("g1", KT), ("conv", CT * CONV), ("lre", MT), ("lim", MT), ("lst", MT), ("dsk", 2),
                     ("wab", KT * 8), ("bre", 2 * P), ("bim", 2 * P), ("cre", MT * 32), ("cim", MT * 32),
                     ("glu", 2 * 512))
ROWS, NROWS = fields(("alog", HEADS), ("dt", HEADS), ("gng", DK), ("lq1", 64), ("lk1", 64), ("lq2", 64),
                     ("lk2", 64), ("dng", DV2), ("glb", 512), ("g2", D), ("laminit", 1), ("lamrest", 1),
                     ("expoff", 1), ("pad", 1))
LEVELS = 7
CST, NCST = fields(("ident", P), ("tri", P), ("negT", P), ("negq", P), ("lev", LEVELS * P), ("iota", TOPK))


class Signal:

    def __init__(self, sem, per_layer, start=0):
        self.sem, self.per_layer, self.start = sem, per_layer, start

    def __call__(self, layer, k):
        return self.sem, layer * self.per_layer + (k + self.start)


def build(nc, x, w_blocks, cols_d, rows_d, keys_d, u_tab, v_tab, cst_d, fin_d, out):
    with ExitStack() as ctx:
        _build(nc, ctx, x, w_blocks, cols_d, rows_d, keys_d, u_tab, v_tab, cst_d, fin_d, out)


def _build(nc, ctx, x, w_blocks, cols_d, rows_d, keys_d, u_tab, v_tab, cst_d, fin_d, out):
    def sb(name, shape, dt=F32):
        return ctx.enter_context(nc.sbuf_tensor(name, shape, dt))

    def signal(name, per_layer, start=0):
        return Signal(ctx.enter_context(nc.semaphore(name)), per_layer, start)

    h = sb("h", [P, TB, D])
    hn = sb("hn", [P, TB, D])
    hnT = sb("hnT", [P, KT, SEQ])
    cst = sb("cst", [P, NCST])
    rows = sb("rows", [P, NROWS])
    cols = sb("cols", [P, NCOLS])
    keysT = sb("keysT", [P, PH, NKEY])
    scores = sb("scores", [P, TB, PH, 2 * NKEY])
    small = sb("small", [P, 1024])
    big = sb("big", [P, 2 * 16 * 1024])

    def col(name):
        return cols[:, COLS[name][0]:COLS[name][1]]

    def row(name):
        return rows[:, ROWS[name][0]:ROWS[name][1]]

    def const(name):
        return cst[:, CST[name][0]:CST[name][1]]

    ident, tri, negT, negq = const("ident"), const("tri"), const("negT"), const("negq")
    lev = const("lev").rearrange("p (l i) -> p l i", l=LEVELS)
    iota = const("iota")

    wring = big[:, 0:16384].rearrange("p (s k c) -> p s k c", s=RING, k=KT)
    uring = big[:, 0:16384].rearrange("p (s d) -> p s d", s=TOPK)
    vring = big[:, 16384:32768].rearrange("p (s d) -> p s d", s=TOPK)
    taken = [16384]

    def scratch(n):
        a = taken[0]
        taken[0] += n
        assert taken[0] <= 32768, taken[0]
        return big[:, a:a + n]

    reg = scratch(6144)
    phase_c = reg[:, 0:2048].rearrange("p (m t) -> p m t", m=MT)
    phase_s = reg[:, 2048:4096].rearrange("p (m t) -> p m t", m=MT)
    cz_re = reg[:, 4096:5120].rearrange("p (m c) -> p m c", m=MT)
    cz_im = reg[:, 5120:6144].rearrange("p (m c) -> p m c", m=MT)
    raw = scratch(1554).rearrange("p (c t) -> p c t", c=CT)
    convd = scratch(1536).rearrange("p (c t) -> p c t", c=CT)
    nat = scratch(1536).rearrange("p (b c) -> p b c", b=TB)
    zbuf = scratch(512).rearrange("p (b c) -> p b c", b=TB)
    vbuf = scratch(1024).rearrange("p (b c) -> p b c", b=TB)
    qT = scratch(1024).rearrange("p (c t) -> p c t", c=4)
    kT = scratch(1024).rearrange("p (c t) -> p c t", c=4)
    uT = scratch(512).rearrange("p (c t) -> p c t", c=2)
    kb = scratch(512).rearrange("p (b c) -> p b c", b=TB)
    flat_raw = big[:, 16384 + 6144:16384 + 6144 + 1554]
    places = [reg[:, 512 * i:512 * i + 512] for i in range(12)] + [flat_raw[:, 0:512], flat_raw[:, 512:1024]]
    mats = [[m.rearrange("p (h i) -> p h i", h=HEADS) for m in places[7 * c:7 * c + 7]] for c in range(TB)]
    dec, LT, ML, TI, TIT, XM, QK = (
        [mats[c][i] for c in range(TB)] for i in range(7))
    keyT = [convd[:, 3 * c:3 * c + 3, :].rearrange("p k (g t) -> p k g t", g=2) for c in range(TB)]
    sreg = scores[:, :, :, :].rearrange("p b h n -> p (b h n)")
    s5a = sreg[:, 0:1024]
    s5b = sreg[:, 1024:2048]
    s5st = sreg[:, 2048:3072].rearrange("p (b r t) -> p b r t", b=2, r=2)
    s5y = sreg[:, 3072:3584].rearrange("p (c t) -> p c t", c=2)
    s5w = sreg[:, 3584:4096].rearrange("p (c t) -> p c t", c=2)
    prob1 = sreg[:, 0:2048].rearrange("p (h m k) -> p h m k", h=HEADS, m=2)
    prob0 = sreg[:, 2048:3072].rearrange("p (h m k) -> p h m k", h=HEADS, m=2)
    pT1 = sreg[:, 3072:4096].rearrange("p (h c q) -> p h c q", h=HEADS, c=2)
    pT0 = nat[:, :, 0:256].rearrange("p b (g q) -> p b g q", g=2)
    qpT = big[:, 16384:16384 + 2048].rearrange("p (h t) -> p h t", h=PH)
    glu_t = uT
    kd = kb[:, 0, :]
    unew = zbuf
    sel = hnT[:, :, :].rearrange("p k t -> p (k t)")
    scur = sel[:, 0:256].rearrange("p (a n) -> p a n", a=2)
    scur2 = sel[:, 256:512].rearrange("p (a n) -> p a n", a=2)
    cand = sel[:, 512:768]
    cand2 = sel[:, 768:1024]
    onehot = sel[:, 1024:1536].rearrange("p (a k n) -> p a k n", a=2, k=TOPK)
    diag = sel[:, 1536:2048].rearrange("p (r c) -> p r c", r=4)

    sm = [0]

    def tiny(n, dt=F32):
        a = sm[0]
        sm[0] += n
        assert sm[0] <= 1024
        return small[:, a:a + n] if dt == F32 else small[:, a:a + n].bitcast(dt)

    ss, rstd, expoff = tiny(2), tiny(2), tiny(1)
    (stp, xr, th, zz, em1, kk_, s2, c2, t0, t1, t2, sin1, cosm1, are, aim, kre, kim, mag) = (tiny(8) for _ in range(18))
    pw = [(tiny(8), tiny(8)), (tiny(8), tiny(8))]
    convh = tiny(24)
    ab = tiny(16).rearrange("p (b c) -> p b c", b=TB)
    beta = tiny(8).rearrange("p (b c) -> p b c", b=TB)
    gg = tiny(8).rearrange("p (b c) -> p b c", b=TB)
    ga, gb_, ea = tiny(8).rearrange("p (b c) -> p b c", b=TB), tiny(8).rearrange("p (b c) -> p b c", b=TB), tiny(4)
    gc = tiny(8).rearrange("p (b c) -> p b c", b=TB)
    eg = tiny(8).rearrange("p (b c) -> p b c", b=TB)
    qkn = tiny(16).rearrange("p (b c) -> p b c", b=TB)
    gss = tiny(8).rearrange("p (b c) -> p b c", b=TB)
    lam, lsum = tiny(1), tiny(2)
    mx, zsum, rz, lrz = tiny(16), tiny(16), tiny(16), tiny(8)
    dss = tiny(8)
    sv = [tiny(32).rearrange("p (a k) -> p a k", a=2) for _ in range(1)][0]
    si = tiny(32, U32).rearrange("p (a k) -> p a k", a=2)
    sif = tiny(32).rearrange("p (a k) -> p a k", a=2)
    tv, tp = tiny(16), tiny(16, U32)
    ab_u = tiny(32, U32).rearrange("p (a k) -> p a k", a=2)
    ab_f = tiny(32).rearrange("p (a k) -> p a k", a=2)
    eij = tiny(32).rearrange("p (a k) -> p a k", a=2)
    ids = tiny(32, U32).rearrange("p (b k) -> p b k", b=TB)
    nmax, gz = tiny(2), tiny(2)
    gate = tiny(32).rearrange("p (b k) -> p b k", b=TB)
    dots = tiny(32).rearrange("p (b k) -> p b k", b=TB)
    ge = tiny(32).rearrange("p (a k) -> p a k", a=2)
    gt = tiny(32).rearrange("p (b k) -> p b k", b=TB)
    pk = tiny(32).rearrange("p (b k) -> p b k", b=TB)

    ps = ctx.enter_context(nc.psum_tensor("ps", [P, 8, 512], F32))

    def bank(i):
        return ps[:, i, :]

    cst_in = signal("cst_in", 0)
    x_in = signal("x_in", 0)
    params_in = signal("params_in", 3 * 16)
    slot_blocks = [len(range(s, NB, RING)) for s in range(RING)]
    w_in = [signal(f"w_in{s}", 16 * slot_blocks[s]) for s in range(RING)]
    w_used = signal("w_used", NB)
    u_in = [signal(f"u_in{k}", 16 * PH * TB) for k in range(TOPK)]
    v_in = [signal(f"v_in{k}", 16 * PH * TB) for k in range(TOPK)]
    fin_in = signal("fin_in", 0)
    out_done = signal("out_done", 0)

    h_ready = signal("h_ready", 1, start=1)
    ss_ready = signal("ss_ready", 2)
    inv_ready = signal("inv_ready", 2)
    rstd_ready = signal("rstd_ready", 2)
    hn_ready = signal("hn_ready", 2)
    tr_done = signal("tr_done", 12)
    trT_ready = signal("trT_ready", 12)
    fill_done = signal("fill_done", len(FILLS))
    fill_act = signal("fill_act", len(FILLS))
    pads_ready = signal("pads_ready", 1)
    step_ready = signal("step_ready", 1)
    half_angle = signal("half_angle", 1)
    sines_ready = signal("sines_ready", 1)
    cz_ready = signal("cz_ready", 1)
    bu_done = signal("bu_done", MT)
    bu_used = signal("bu_used", MT)
    state_ready = signal("state_ready", MT)
    y_acc = signal("y_acc", MT)
    y_arg = signal("y_arg", 1)
    y_tanh = signal("y_tanh", 1)
    yT_ready = signal("yT_ready", 1)
    glu_done = signal("glu_done", 2)
    glu_pre = signal("glu_pre", 2)
    glu_tanh = signal("glu_tanh", 2)
    s5_out = signal("s5_out", 1)
    a_pre = signal("a_pre", 1)
    a_exp = signal("a_exp", 1)
    a_ln = signal("a_ln", 1)
    g_ready = signal("g_ready", 1)
    gcum_done = signal("gcum_done", 1)
    dec_pre = signal("dec_pre", TB)
    dec_ready = signal("dec_ready", TB)
    conv_done = signal("conv_done", CT)
    conv_tanh = signal("conv_tanh", CT)
    silu_ready = signal("silu_ready", CT)
    nat_done = signal("nat_done", TB)
    nat_ready = signal("nat_ready", TB)
    qk_inv = signal("qk_inv", 1)
    qk_root = signal("qk_root", 1)
    qkb_ready = signal("qkb_ready", TB)
    keyT_done = signal("keyT_done", TB)
    keyT_ready = signal("keyT_ready", TB)
    kk_done = signal("kk_done", TB)
    t1T_ready = signal("t1T_ready", TB)
    t1_done = signal("t1_done", TB)
    t_ready = signal("t_ready", TB * LEVELS)
    x_done = signal("x_done", TB * (LEVELS - 1))
    x_ready = signal("x_ready", TB * (LEVELS - 1))
    upd_done = signal("upd_done", TB * (LEVELS - 1))
    rhs_ready = signal("rhs_ready", TB)
    vnew_done = signal("vnew_done", TB)
    vnew_ready = signal("vnew_ready", TB)
    kd_ready = signal("kd_ready", 1)
    state_done = signal("state_done", 1)
    sbd_ready = signal("sbd_ready", 1)
    inter_done = signal("inter_done", 1)
    gout_done = signal("gout_done", TB)
    go_inv = signal("go_inv", 1)
    go_root = signal("go_root", 1)
    z_tanh = signal("z_tanh", 1)
    gdn_out = signal("gdn_out", 1)
    lam_sum = signal("lam_sum", 1)
    lam_exp = signal("lam_exp", 1)
    att_done = signal("att_done", TB)
    att_max = signal("att_max", TB)
    att_exp = signal("att_exp", TB)
    pd_ready = signal("pd_ready", TB)
    pT_done = signal("pT_done", TB)
    pT_ready = signal("pT_ready", TB)
    ao_done = signal("ao_done", TB)
    ao_inv = signal("ao_inv", 1)
    ao_root = signal("ao_root", 1)
    mix_ready = signal("mix_ready", 1)
    proj_done = signal("proj_done", 4)
    resid = signal("resid", 4)
    pq_done = signal("pq_done", 4)
    pq_ready = signal("pq_ready", 4)
    sc_done = signal("sc_done", 4)
    sc_ready = signal("sc_ready", 4)
    xy_ready = signal("xy_ready", 2)
    y_init = signal("y_init", 1)
    NG = PH * TB
    params_free = signal("params_free", 1, start=1)
    ids_ready = signal("ids_ready", NG)
    top_ready = signal("top_ready", NG)
    gexp_ready = signal("gexp_ready", NG)
    dot_done = signal("dot_done", NG * TOPK, start=TOPK)
    gelu_arg = signal("gelu_arg", NG)
    gelu_tanh = signal("gelu_tanh", NG)
    p_ready = signal("p_ready", NG)
    diag_ready = signal("diag_ready", NG * TOPK)
    v_used = signal("v_used", NG * TOPK, start=TOPK)
    pool_gate = signal("pool_gate", 0)
    final_ss = signal("final_ss", 0)
    final_inv = signal("final_inv", 0)
    final_root = signal("final_root", 0)
    final_ready = signal("final_ready", 0)

    block = ctx.enter_context(nc.Block())

    def nat_tanh(j):
        return nat[:, :, :].rearrange("p b c -> p (b c)")[:, j * SEQ:(j + 1) * SEQ]

    @block.sync
    def _(sp):
        sp.dma_start(cst[:, :], cst_d).then_inc(cst_in.sem, 16)
        sp.dma_start(h[:, :, :], x.rearrange("o (b p) d -> p (o b) d", p=P)).then_inc(x_in.sem, 16)
        with sp.Fori(0, DEPTH) as layer:
            sp.wait_ge(*params_free(layer, 0))
            sp.dma_start(cols[:, :], cols_d[bass.ds(layer, 1), :, :].rearrange("o p c -> p (o c)")).then_inc(params_in.sem, 16)
            sp.dma_start(rows[:, :], rows_d[bass.ds(layer, 1), :, :].rearrange("o p c -> p (o c)")).then_inc(params_in.sem, 16)
            sp.dma_start(keysT[:, :, :].rearrange("p h n -> p (h n)"),
                         keys_d[bass.ds(layer, 1), :, :].rearrange("o p c -> p (o c)")).then_inc(params_in.sem, 16)
            for n in range(NB):
                if n == 0:
                    sp.wait_ge(*dot_done(layer, 0))
                elif n >= RING:
                    sp.wait_ge(*w_used(layer, n - RING + 1))
                sp.dma_start(wring[:, n % RING, :, :].rearrange("p k c -> p (k c)"),
                             w_blocks[bass.ds(layer * NB + n, 1), :, :].rearrange("o p c -> p (o c)")
                             ).then_inc(w_in[n % RING].sem, 16)
        sp.wait_ge(*params_free(DEPTH, 0))
        sp.dma_start(row("g2"), fin_d).then_inc(fin_in.sem, 16)
        sp.wait_ge(final_ready.sem, 1)
        sp.dma_start(out.rearrange("o (b p) d -> p (o b) d", p=P), hn[:, :, :]).then_inc(out_done.sem, 16)
        sp.wait_ge(out_done.sem, 16)

    @block.tensor
    def _(pe):
        def mm(o, a, b, start=True, stop=True):
            return nc.tensor.matmul(o, a, b, start=start, stop=stop, skip_group_check=True)

        def turn(o, a):
            return nc.tensor.transpose(o, a, ident)

        def turn_tokens(src, banks, ready):
            for b in range(4):
                if ready is not None:
                    ready(b)
                for k in range(2):
                    for t in range(TB):
                        ins = turn(bank(banks[b])[:, (2 * k + t) * P:(2 * k + t + 1) * P],
                                   src[:, t, (2 * b + k) * P:(2 * b + k + 1) * P])
                ins.then_inc(tr_done.sem, 1)

        def block_in(layer, n):
            pe.wait_ge(*w_in[n % RING](layer, 16 * (n // RING + 1)))

        def fill_wait(layer, f):
            prev = f - 4
            if prev >= 0:
                pe.wait_ge(*fill_act(layer, prev + 1))

        def fill(layer, f):
            name = FILLS[f]
            o = bank(4 + f % 4)
            fill_wait(layer, f)
            if name == "ab":
                for t in range(TB):
                    for k in range(KT):
                        ins = mm(o[:, 8 * t:8 * t + 8], hnT[:, k, t * P:(t + 1) * P],
                                 col("wab").rearrange("p (k c) -> p k c", k=KT)[:, k, :], k == 0, k == KT - 1)
                ins.then_inc(fill_done.sem, 1)
                return
            n = BLOCKS.index(name)
            w = wring[:, n % RING, :, :]
            block_in(layer, n)
            for j in range(2):
                for k in range(KT):
                    if name[0] in "zv":
                        ins = mm(o[:, j * 256:(j + 1) * 256], hnT[:, k, j * P:(j + 1) * P], w[:, k, :],
                                 k == 0, k == KT - 1)
                    else:
                        ins = mm(o[:, j * 256:(j + 1) * 256], w[:, k, j * P:(j + 1) * P], hnT[:, k, :],
                                 k == 0, k == KT - 1)
            ins.then_inc(fill_done.sem, 1)
            pe.wait_ge(*fill_done(layer, f + 1))
            pe.sem_inc(w_used.sem, 1)

        def bu(layer, m):
            if m >= 3:
                pe.wait_ge(*bu_used(layer, m - 2))
            r = slice(32 * (m % 4), 32 * (m % 4) + 32)
            for i, name in enumerate(("bre", "bim")):
                ins = mm(bank(m % 3)[:, 256 * i:256 * i + 256],
                         col(name).rearrange("p (c n) -> p c n", c=2)[r, m // 4, :], uT[r, m // 4, :])
            ins.then_inc(bu_done.sem, 1)

        def y_part(layer, m):
            pe.wait_ge(*state_ready(layer, m + 1))
            if m == 0:
                pe.wait_ge(*cz_ready(layer, 1))
            for i, cz in enumerate((cz_re, cz_im)):
                ins = mm(bank(3)[:, 256 * (m // 4):256 * (m // 4) + 256], cz[:, m, :], s5st[:, m % 2, i, :],
                         m % 4 == 0 and i == 0, m % 4 == 3 and i == 1)
            ins.then_inc(y_acc.sem, 1)

        pe.wait_ge(cst_in.sem, 16)
        pe.sem_inc(v_used.sem, TOPK)
        with pe.Fori(0, DEPTH) as layer:
            pe.wait_ge(*hn_ready(layer, 1))
            turn_tokens(hn, (4, 5, 6, 7), None)
            pe.wait_ge(*params_in(layer, 48))
            pe.wait_ge(*trT_ready(layer, 4))
            fill(layer, 0)
            pe.wait_ge(*fill_act(layer, 1))
            for m in range(3):
                bu(layer, m)
            for f in range(1, len(FILLS)):
                fill(layer, f)
                m = f - 4
                if 0 <= m < MT:
                    y_part(layer, m)
                    if m + 3 < MT:
                        bu(layer, m + 3)
            pe.wait_ge(*yT_ready(layer, 1))
            for t in range(TB):
                for k in range(2):
                    ins = mm(bank(t), s5w[:, k, t * P:(t + 1) * P],
                             col("glu").rearrange("p (k n) -> p k n", k=2)[:, k, :], k == 0, k == 1)
                ins.then_inc(glu_done.sem, 1)
            pe.wait_ge(*g_ready(layer, 1))
            pe.wait_ge(*y_tanh(layer, 1))
            for c in range(TB):
                for hd in range(HEADS):
                    mm(bank(2 + c)[:, hd * P:(hd + 1) * P], XM[c][:, hd, :], tri)
            pe.wait_ge(*fill_act(layer, len(FILLS)))
            for c in range(TB):
                ins = mm(bank(4)[:, 4 * c:4 * c + 4], tri, gg[:, c, :])
            ins.then_inc(gcum_done.sem, 1)
            for c in range(TB):
                for j in range(CT):
                    if c == 0:
                        pe.wait_ge(*silu_ready(layer, j + 1))
                    if c == 0 and j == 0:
                        pe.wait_ge(*dec_pre(layer, 1))
                    o = bank(4 + 2 * c + j // 4)
                    ins = turn(o[:, (j % 4) * P:(j % 4 + 1) * P], convd[:, j, c * P:(c + 1) * P])
                ins.then_inc(nat_done.sem, 1)
            for c in range(TB):
                pe.wait_ge(*qkb_ready(layer, c + 1))
                pe.wait_ge(*nat_ready(layer, c + 1))
                for kind in range(3):
                    for g in range(2):
                        src = (nat[:, c, kind * 256 + g * P:kind * 256 + (g + 1) * P] if kind < 2
                               else kb[:, c, g * P:(g + 1) * P])
                        i = 2 * kind + g
                        ins = turn(bank(4 + 2 * c + i // 4)[:, (i % 4) * P:(i % 4 + 1) * P], src)
                ins.then_inc(keyT_done.sem, 1)
            for c in range(TB):
                pe.wait_ge(*keyT_ready(layer, c + 1))
                if c == 0:
                    pe.wait_ge(*glu_pre(layer, 2))
                pe.wait_ge(*keyT_ready(layer, TB))
                for hd in range(HEADS):
                    r = slice(64 * (hd % 2), 64 * (hd % 2) + 64)
                    k_ = keyT[c][r, 1, hd // 2, :]
                    o = bank(4 * c + hd % 2)
                    g = hd // 2
                    mm(o[:, g * P:(g + 1) * P], k_, keyT[c][r, 2, g, :])
                    ins = mm(o[:, 256 + g * P:256 + (g + 1) * P], k_, keyT[c][r, 0, g, :])
                ins.then_inc(kk_done.sem, 1)
            for c in range(TB):
                pe.wait_ge(*t1T_ready(layer, c + 1))
                if c == 0:
                    pe.wait_ge(*dec_pre(layer, 2))
                for hd in range(HEADS):
                    ins = turn(bank(4 * c + 2)[:, hd * P:(hd + 1) * P], TIT[c][:, hd, :])
                ins.then_inc(t1_done.sem, 1)
            for lv in range(1, LEVELS):
                for c in range(TB):
                    pe.wait_ge(*t_ready(layer, TB * (lv - 1) + c + 1))
                    for hd in range(HEADS):
                        ins = mm(bank(4 * c)[:, hd * P:(hd + 1) * P], ML[c][:, hd, :], TI[c][:, hd, :])
                    ins.then_inc(x_done.sem, 1)
                for c in range(TB):
                    pe.wait_ge(*x_ready(layer, TB * (lv - 1) + c + 1))
                    for hd in range(HEADS):
                        ins = mm(bank(4 * c + 1)[:, hd * P:(hd + 1) * P], XM[c][:, hd, :], TIT[c][:, hd, :])
                        if lv < LEVELS - 1:
                            ins = mm(bank(4 * c + 2)[:, hd * P:(hd + 1) * P], TIT[c][:, hd, :], XM[c][:, hd, :])
                    ins.then_inc(upd_done.sem, 1)

            def solve(c, rhs):
                for hd in range(HEADS):
                    ins = mm(bank(4 * c)[:, hd * DK:(hd + 1) * DK], TIT[c][:, hd, :], rhs[:, hd * DK:(hd + 1) * DK])
                ins.then_inc(vnew_done.sem, 1)

            def inside(c):
                for hd in range(HEADS):
                    ins = mm(bank(4 * c + 2)[:, hd * DK:(hd + 1) * DK], QK[c][:, hd, :],
                             unew[:, c, hd * DK:(hd + 1) * DK])
                ins.then_inc(gout_done.sem, 1)

            pe.wait_ge(*rhs_ready(layer, 1))
            pe.wait_ge(*t_ready(layer, TB * LEVELS))
            solve(0, nat[:, 0, 512:768])
            pe.wait_ge(*vnew_ready(layer, 1))
            pe.wait_ge(*kd_ready(layer, 1))
            for g in range(2):
                ins = mm(bank(3)[:, g * P:(g + 1) * P], kd[:, g * P:(g + 1) * P], unew[:, 0, g * P:(g + 1) * P])
            ins.then_inc(state_done.sem, 1)
            inside(0)
            pe.wait_ge(*sbd_ready(layer, 1))
            for i, kind in enumerate((2, 0)):
                for g in range(2):
                    ins = mm(bank(7)[:, 256 * i + g * P:256 * i + (g + 1) * P], keyT[1][:, kind, g, :],
                             XM[0][:, g, :])
            ins.then_inc(inter_done.sem, 1)
            pe.wait_ge(*rhs_ready(layer, 2))
            solve(1, nat[:, 1, 512:768])
            pe.wait_ge(*vnew_ready(layer, 2))
            inside(1)

            pe.wait_ge(*gdn_out(layer, 1))
            for t in range(TB):
                nk = (t + 1) * P
                for hd in range(HEADS):
                    for m in range(2):
                        r = slice(64 * m, 64 * m + 64)
                        o = ps[:, m if t == 0 else 2 + 2 * m + hd // 2, (hd * nk) % 512:(hd * nk) % 512 + nk]
                        ins = mm(o, qT[r, hd, t * P:(t + 1) * P], kT[r, hd, 0:nk])
                ins.then_inc(att_done.sem, 1)
            for t in range(TB):
                pe.wait_ge(*pd_ready(layer, t + 1))
                for hd in range(HEADS):
                    for kb_ in range(t + 1):
                        p_ = (prob0 if t == 0 else prob1)[:, hd, 0, kb_ * P:(kb_ + 1) * P]
                        i = hd * (t + 1) + kb_
                        ins = turn((bank(6) if t == 0 else ps[:, 2:4, :].rearrange("p b n -> p (b n)"))[:, i * P:(i + 1) * P], p_)
                ins.then_inc(pT_done.sem, 1)
            for t in range(TB):
                pe.wait_ge(*pT_ready(layer, t + 1))
                for hd in range(HEADS):
                    for kb_ in range(t + 1):
                        lhs = pT0[:, hd // 2, hd % 2, :] if t == 0 else pT1[:, hd, kb_, :]
                        ins = mm(bank(7 if t == 0 else 5)[:, hd * P:(hd + 1) * P], lhs,
                                 vbuf[:, kb_, hd * P:(hd + 1) * P], kb_ == 0, kb_ == t)
                ins.then_inc(ao_done.sem, 1)

            pe.wait_ge(*mix_ready(layer, 1))
            turn_tokens(hn, (0, 1, 2, 3), None)
            pe.wait_ge(*trT_ready(layer, 8))
            for i in range(4):
                n = BLOCKS.index(f"out{i}")
                block_in(layer, n)
                for t in range(TB):
                    for k in range(KT):
                        ins = mm(bank(4 + i)[:, 256 * t:256 * t + 256], hnT[:, k, t * P:(t + 1) * P],
                                 wring[:, n % RING, k, :], k == 0, k == KT - 1)
                ins.then_inc(proj_done.sem, 1)
                pe.wait_ge(*proj_done(layer, i + 1))
                pe.sem_inc(w_used.sem, 1)
            pe.wait_ge(*hn_ready(layer, 2))
            turn_tokens(hn, (0, 1, 2, 3), None)
            pe.wait_ge(*trT_ready(layer, 12))
            for i in range(4):
                n = BLOCKS.index(f"wq{i}")
                block_in(layer, n)
                for j in range(2):
                    for k in range(KT):
                        ins = mm(bank(4 + i)[:, 256 * j:256 * j + 256], wring[:, n % RING, k, j * P:(j + 1) * P],
                                 hnT[:, k, :], k == 0, k == KT - 1)
                ins.then_inc(pq_done.sem, 1)
                pe.wait_ge(*pq_done(layer, i + 1))
                pe.sem_inc(w_used.sem, 1)
            pe.wait_ge(*pq_ready(layer, 4))
            for i in range(4):
                t, hg = i // 2, i % 2
                if i >= 2:
                    pe.wait_ge(*sc_ready(layer, i - 1))
                for j in range(4):
                    for a in range(2):
                        r = slice(64 * a, 64 * a + 64)
                        ins = mm(bank(2 * (i % 2) + a)[:, j * P:(j + 1) * P],
                                 qpT[r, 4 * hg + j, t * P:(t + 1) * P], keysT[r, 4 * hg + j, :])
                ins.then_inc(sc_done.sem, 1)
            for t in range(TB):
                for j in range(2):
                    ins = mm(bank(4 + 2 * t + j), ident, h[:, t, 512 * j:512 * j + 512])
            ins.then_inc(y_init.sem, 1)
            with pe.Fori(0, PH) as head:
                for t in range(TB):
                    for k in range(TOPK):
                        n = head * (TB * TOPK) + (t * TOPK + k)
                        pe.wait_ge(*v_in[k](layer, (head * TB + t) * 16 + 16))
                        pe.wait_ge(*diag_ready(layer, n + 1))
                        for j in range(2):
                            ins = mm(bank(4 + 2 * t + j), diag[:, k % 4, :], vring[:, k, 512 * j:512 * j + 512],
                                     False, True)
                        ins.then_inc(v_used.sem, 1)

    @block.vector
    def _(dve):
        V = nc.vector
        fence = V.drain

        def norm_tokens(layer, which):
            dve.wait_ge(*ss_ready(layer, which))
            V.tensor_scalar(rstd, ss, 1.0 / D, EPS, ALU.mult, ALU.add)
            fence()
            V.reciprocal(rstd, rstd).then_inc(inv_ready.sem, 1)
            dve.wait_ge(*rstd_ready(layer, which))

        def bc(a, shape):
            return a.broadcast_to(shape)

        dve.wait_ge(cst_in.sem, 16)
        dve.wait_ge(x_in.sem, 16)
        dve.sem_inc(h_ready.sem, 1)
        dve.sem_inc(dot_done.sem, TOPK)
        dve.sem_inc(params_free.sem, 1)
        with dve.Fori(0, DEPTH) as layer:
            norm_tokens(layer, 1)
            for t in range(TB):
                ins = V.tensor_scalar(hn[:, t, :], h[:, t, :], rstd[:, t:t + 1], None, ALU.mult)
            ins.then_inc(hn_ready.sem, 1)

            V.memset(raw[:, :, 0:3], 0.0).then_inc(pads_ready.sem, 1)
            dve.wait_ge(*params_in(layer, 48))
            V.tensor_scalar(convh, col("conv"), 0.5, None, ALU.mult)
            dve.wait_ge(*step_ready(layer, 1))
            V.tensor_tensor(xr, col("lre"), stp, ALU.mult)
            V.tensor_tensor(th, col("lim"), stp, ALU.mult)
            fence()
            V.tensor_scalar(xr, xr, -80.0, 80.0, ALU.max, ALU.min)
            magic = 12582912.0
            V.tensor_scalar(kk_, th, float(1.0 / (2.0 * np.pi)), magic, ALU.mult, ALU.add)
            fence()
            V.tensor_scalar(zz, xr, 1.0 / 128.0, None, ALU.mult)
            V.tensor_scalar(kk_, kk_, magic, None, ALU.subtract)
            fence()
            turn_parts = (6.28125, 0.0019340515136718750, 2.0 * np.pi - 6.28125 - 0.0019340515136718750)
            V.tensor_scalar(em1, zz, 1.0 / 9.0, 1.0, ALU.mult, ALU.add)
            for i, part in enumerate(turn_parts):
                V.scalar_tensor_tensor(th, kk_, -float(part), th, ALU.mult, ALU.add)
                fence()
            V.tensor_scalar(th, th, -float(np.float32(3.1415925)), float(np.float32(3.1415925)), ALU.max, ALU.min)
            fence()
            V.scalar_tensor_tensor(c2, th, -1.0, th, ALU.mult, ALU.max)
            V.tensor_scalar(s2, th, 0.5, None, ALU.mult)
            fence()
            V.tensor_scalar(c2, c2, -0.5, float(np.float32(np.pi / 2)), ALU.mult, ALU.add).then_inc(half_angle.sem, 1)
            for n in range(8, 0, -1):
                V.tensor_tensor(em1, em1, zz, ALU.mult)
                fence()
                if n > 1:
                    V.tensor_scalar(em1, em1, 1.0 / n, 1.0, ALU.mult, ALU.add)
                    fence()
            for _ in range(7):
                V.scalar_tensor_tensor(em1, em1, 2.0, em1, ALU.add, ALU.mult)
                fence()
            V.tensor_scalar(mag, em1, 1.0, None, ALU.add)
            dve.wait_ge(*sines_ready(layer, 1))
            V.scalar_tensor_tensor(sin1, s2, 2.0, c2, ALU.mult, ALU.mult)
            V.scalar_tensor_tensor(cosm1, s2, -2.0, s2, ALU.mult, ALU.mult)
            V.tensor_tensor(t2, col("lre"), col("lre"), ALU.mult)
            V.tensor_tensor(t1, col("lim"), col("lim"), ALU.mult)
            fence()
            V.tensor_scalar(pw[0][0], cosm1, 1.0, None, ALU.add)
            V.tensor_copy(pw[0][1], sin1)
            V.tensor_tensor(t2, t2, t1, ALU.add)
            V.tensor_tensor(aim, mag, sin1, ALU.mult)
            fence()
            V.tensor_tensor(are, em1, pw[0][0], ALU.mult)
            V.reciprocal(t2, t2)
            fence()
            V.tensor_tensor(are, are, cosm1, ALU.add)
            fence()
            V.tensor_tensor(kre, are, col("lre"), ALU.mult)
            V.tensor_tensor(t0, aim, col("lim"), ALU.mult)
            V.tensor_tensor(kim, aim, col("lre"), ALU.mult)
            V.tensor_tensor(t1, are, col("lim"), ALU.mult)
            fence()
            V.tensor_tensor(kre, kre, t0, ALU.add)
            V.tensor_tensor(kim, kim, t1, ALU.subtract)
            fence()
            V.tensor_tensor(kre, kre, t2, ALU.mult)
            V.tensor_tensor(kim, kim, t2, ALU.mult)
            V.memset(phase_c[:, :, 0:1], 1.0)
            V.memset(phase_s[:, :, 0:1], 0.0)
            fence()
            n = 1
            while n < SEQ:
                pc, psn = pw[0] if n in (1, 4, 16, 64) else pw[1]
                nc_, ns_ = pw[1] if n in (1, 4, 16, 64) else pw[0]
                A = s5a.rearrange("p (m t) -> p m t", m=MT)[:, :, 0:n]
                B = s5b.rearrange("p (m t) -> p m t", m=MT)[:, :, 0:n]
                pcb, psb = bc(pc[:, :, None], [P, MT, n]), bc(psn[:, :, None], [P, MT, n])
                V.tensor_tensor(A, phase_c[:, :, 0:n], pcb, ALU.mult)
                V.tensor_tensor(B, phase_s[:, :, 0:n], psb, ALU.mult)
                V.tensor_tensor(t0, pc, pc, ALU.mult)
                V.tensor_tensor(t1, psn, psn, ALU.mult)
                V.scalar_tensor_tensor(ns_, pc, 2.0, psn, ALU.mult, ALU.mult)
                fence()
                V.tensor_tensor(phase_c[:, :, n:2 * n], A, B, ALU.subtract)
                V.tensor_tensor(nc_, t0, t1, ALU.subtract)
                fence()
                V.tensor_tensor(A, phase_c[:, :, 0:n], psb, ALU.mult)
                V.tensor_tensor(B, phase_s[:, :, 0:n], pcb, ALU.mult)
                fence()
                V.tensor_tensor(phase_s[:, :, n:2 * n], A, B, ALU.add)
                fence()
                n *= 2
            cre, cim = (col(x).rearrange("p (m c) -> p m c", m=MT) for x in ("cre", "cim"))
            krb, kib = bc(kre[:, :, None], [P, MT, 32]), bc(kim[:, :, None], [P, MT, 32])
            A, B, A2, B2 = (s5a[:, i * 256:(i + 1) * 256].rearrange("p (m c) -> p m c", m=MT) for i in range(4))
            V.memset(reg[:, 4096:6144], 0.0)
            V.tensor_tensor(A, cre, krb, ALU.mult)
            V.tensor_tensor(B, cim, kib, ALU.mult)
            V.tensor_tensor(A2, cre, kib, ALU.mult)
            V.tensor_tensor(B2, cim, krb, ALU.mult)
            fence()
            for j in range(4):
                c = slice(32 * j, 32 * j + 32)
                V.tensor_tensor(cz_re[:, j:MT:4, c], A[:, j:MT:4, :], B[:, j:MT:4, :], ALU.subtract)
                V.scalar_tensor_tensor(cz_im[:, j:MT:4, c], A2[:, j:MT:4, :], -1.0, B2[:, j:MT:4, :],
                                       ALU.mult, ALU.subtract)
            V.drain().then_inc(cz_ready.sem, 1)
            for m in range(MT):
                dve.wait_ge(*bu_done(layer, m + 1))
                o = bank(m % 3).rearrange("p (r t) -> p r t", r=2)
                A = s5a[:, 0:512].rearrange("p (r t) -> p r t", r=2)
                B = s5b[:, 0:512].rearrange("p (r t) -> p r t", r=2)
                R = s5a[:, 512:1024].rearrange("p (r t) -> p r t", r=2)
                S = s5b[:, 512:1024].rearrange("p (r t) -> p r t", r=2)
                c_ = bc(phase_c[:, m:m + 1, :], [P, 2, SEQ])
                s_ = bc(phase_s[:, m:m + 1, :], [P, 2, SEQ])
                V.tensor_tensor(A, o, c_, ALU.mult)
                V.tensor_tensor(B, o, s_, ALU.mult)
                V.drain().then_inc(bu_used.sem, 1)
                V.tensor_tensor(R[:, 0, :], A[:, 0, :], B[:, 1, :], ALU.add)
                V.tensor_tensor(R[:, 1, :], A[:, 1, :], B[:, 0, :], ALU.subtract)
                fence()
                for r in range(2):
                    V.tensor_tensor_scan(S[:, r, :], bc(mag[:, m:m + 1], [P, SEQ]), R[:, r, :], 0.0, ALU.mult, ALU.add)
                fence()
                V.tensor_tensor(A, S, c_, ALU.mult)
                V.tensor_tensor(B, S, s_, ALU.mult)
                fence()
                if m >= 2:
                    dve.wait_ge(*y_acc(layer, m - 1))
                V.tensor_tensor(s5st[:, m % 2, 0, :], A[:, 0, :], B[:, 1, :], ALU.subtract)
                V.tensor_tensor(s5st[:, m % 2, 1, :], A[:, 1, :], B[:, 0, :], ALU.add)
                V.drain().then_inc(state_ready.sem, 1)
            dve.wait_ge(*y_acc(layer, MT))
            for j in range(2):
                V.scalar_tensor_tensor(s5y[:, j, :], uT[:, j, :], col("dsk")[:, j:j + 1],
                                       bank(3)[:, 256 * j:256 * j + 256], ALU.mult, ALU.add)
            fence()
            V.tensor_tensor(s5w, s5y, s5y, ALU.mult)
            fence()
            V.tensor_scalar(s5w, s5w, 0.044715, 1.0, ALU.mult, ALU.add)
            fence()
            V.tensor_tensor(s5w, s5w, s5y, ALU.mult).then_inc(y_arg.sem, 1)
            V.tensor_scalar(s5y, s5y, 0.5, None, ALU.mult)
            dve.wait_ge(*fill_act(layer, 5))
            V.tensor_tensor(ga, ab[:, :, 0:4], bc(row("dt")[:, None, :], [P, TB, 4]), ALU.add)
            fence()
            V.scalar_tensor_tensor(gb_, ga, -1.0, ga, ALU.mult, ALU.max)
            V.tensor_scalar(ga, ga, 0.0, None, ALU.max)
            V.drain().then_inc(a_pre.sem, 1)
            dve.wait_ge(*y_tanh(layer, 1))
            V.scalar_tensor_tensor(s5w, s5w, 1.0, s5y, ALU.add, ALU.mult).then_inc(yT_ready.sem, 1)
            dve.wait_ge(*a_ln(layer, 1))
            V.tensor_tensor(ga, ga, gb_, ALU.add)
            V.tensor_scalar(beta, beta, 0.5, 0.5, ALU.mult, ALU.add)
            fence()
            V.scalar_tensor_tensor(gg, ga, -1.0, bc(ea[:, None, :], [P, TB, 4]), ALU.mult, ALU.mult)
            fence()
            for j in range(CT):
                V.tensor_scalar(convd[:, j, :], raw[:, j, 0:SEQ], convh[:, 4 * j:4 * j + 1], None, ALU.mult)
                for w in range(1, CONV):
                    fence()
                    ins = V.scalar_tensor_tensor(convd[:, j, :], raw[:, j, w:w + SEQ], convh[:, 4 * j + w:4 * j + w + 1],
                                                 convd[:, j, :], ALU.mult, ALU.add)
                ins.then_inc(conv_done.sem, 1)
            fence()
            for c in range(TB):
                V.tensor_copy(XM[c], bc(gg[:, c, :][:, :, None], [P, HEADS, P]))
            V.drain().then_inc(g_ready.sem, 1)
            for j in range(CT):
                dve.wait_ge(*conv_tanh(layer, j + 1))
                V.scalar_tensor_tensor(convd[:, j, :], nat_tanh(j), 1.0, convd[:, j, :], ALU.add,
                                       ALU.mult).then_inc(silu_ready.sem, 1)
            dve.wait_ge(*gcum_done(layer, 1))
            V.tensor_copy(gc, bank(4)[:, 0:8].rearrange("p (b c) -> p b c", b=TB))
            fence()
            for c in range(TB):
                for hd in range(HEADS):
                    V.scalar_tensor_tensor(dec[c][:, hd, :], bank(2 + c)[:, hd * P:(hd + 1) * P], gc[:, c, hd:hd + 1],
                                           negT, ALU.subtract, ALU.add)
                V.drain().then_inc(dec_pre.sem, 1)
            for t in range(TB):
                dve.wait_ge(*glu_done(layer, t + 1))
                V.tensor_tensor(s5a[:, 0:512] if t == 0 else s5b[:, 0:512], bank(t), row("glb"), ALU.add).then_inc(glu_pre.sem, 1)
            for t in range(TB):
                s = s5a if t == 0 else s5b
                dve.wait_ge(*glu_tanh(layer, t + 1))
                V.tensor_scalar(s[:, 256:512], s[:, 256:512], 0.5, 0.5, ALU.mult, ALU.add)
                fence()
                V.tensor_tensor(hn[:, t, 256:512], s[:, 0:256], s[:, 256:512], ALU.mult)
            dve.wait_ge(*nat_ready(layer, TB))
            V.tensor_tensor(sreg[:, 0:1024].rearrange("p (b c) -> p b c", b=TB), nat[:, :, 0:512], nat[:, :, 0:512], ALU.mult)
            fence()
            V.tensor_reduce(qkn, sreg[:, 0:1024].rearrange("p (b h c) -> p b h c", b=TB, h=8), AX, ALU.add)
            fence()
            V.tensor_scalar(qkn, qkn, 1e-6, None, ALU.add)
            fence()
            V.reciprocal(qkn, qkn).then_inc(qk_inv.sem, 1)
            dve.wait_ge(*qk_root(layer, 1))
            V.tensor_scalar(qkn[:, :, 0:4], qkn[:, :, 0:4], DK ** -0.5, None, ALU.mult)
            fence()
            for c in range(TB):
                n8 = nat[:, c, 0:512].rearrange("p (h d) -> p h d", h=8)
                V.tensor_tensor(n8, n8, bc(qkn[:, c, :][:, :, None], [P, 8, DK]), ALU.mult)
                fence()
                bb = bc(beta[:, c, :][:, :, None], [P, HEADS, DK])
                V.tensor_tensor(kb[:, c, :].rearrange("p (h d) -> p h d", h=HEADS),
                                nat[:, c, 256:512].rearrange("p (h d) -> p h d", h=HEADS), bb, ALU.mult)
                n4 = nat[:, c, 512:768].rearrange("p (h d) -> p h d", h=HEADS)
                V.tensor_tensor(n4, n4, bb, ALU.mult)
                V.drain().then_inc(qkb_ready.sem, 1)
            idb = bc(ident[:, None, :], [P, HEADS, P])
            for c in range(TB):
                dve.wait_ge(*kk_done(layer, c + 1))
                dve.wait_ge(*dec_ready(layer, c + 1))
                for r in range(2):
                    o = bank(4 * c + r).rearrange("p (k g i) -> p k g i", k=2, g=2)
                    V.tensor_tensor(LT[c][:, r:HEADS:2, :], o[:, 0], dec[c][:, r:HEADS:2, :], ALU.mult)
                    V.tensor_tensor(QK[c][:, r:HEADS:2, :], o[:, 1], dec[c][:, r:HEADS:2, :], ALU.mult)
                fence()
                V.tensor_tensor(TIT[c], LT[c], bc(lev[:, 0:1, :], [P, HEADS, P]), ALU.mult)
                V.tensor_tensor(ML[c], LT[c], bc(lev[:, 1:2, :], [P, HEADS, P]), ALU.mult)
                fence()
                V.tensor_tensor(TIT[c], idb, TIT[c], ALU.subtract).then_inc(t1T_ready.sem, 1)
            for c in range(TB):
                dve.wait_ge(*t1_done(layer, c + 1))
                V.tensor_copy(TI[c], bank(4 * c + 2).rearrange("p (h i) -> p h i", h=HEADS)).then_inc(t_ready.sem, 1)
            for lv in range(1, LEVELS):
                for c in range(TB):
                    b4 = [bank(4 * c + i).rearrange("p (h i) -> p h i", h=HEADS) for i in range(3)]
                    dve.wait_ge(*upd_done(layer, TB * (lv - 1) + c + 1))
                    V.tensor_tensor(TIT[c], TIT[c], b4[1], ALU.subtract)
                    if lv < LEVELS - 1:
                        V.tensor_tensor(TI[c], TI[c], b4[2], ALU.subtract)
                        V.tensor_tensor(ML[c], LT[c], bc(lev[:, lv + 1:lv + 2, :], [P, HEADS, P]), ALU.mult)
                    V.drain().then_inc(t_ready.sem, 1)
            dve.wait_ge(*z_tanh(layer, 1))
            V.scalar_tensor_tensor(glu_t, glu_t, 1.0, zbuf, ALU.add, ALU.mult).then_inc(rhs_ready.sem, 1)
            V.tensor_tensor(kd.rearrange("p (h d) -> p h d", h=HEADS),
                            nat[:, 0, 256:512].rearrange("p (h d) -> p h d", h=HEADS),
                            bc(dec[0][:, :, P - 1:P], [P, HEADS, DK]), ALU.mult)
            V.memset(XM[0][:, :, :], 0.0)
            V.drain().then_inc(kd_ready.sem, 1)
            dve.wait_ge(*state_done(layer, 1))
            for g in range(2):
                for i in range(2):
                    r = slice(64 * i, 64 * i + 64)
                    V.tensor_copy(XM[0][r, g, r], bank(3)[r, g * P + 64 * i:g * P + 64 * i + 64])
            V.drain().then_inc(sbd_ready.sem, 1)
            dve.wait_ge(*inter_done(layer, 1))
            egb = bc(eg[:, 1, :][:, :, None], [P, HEADS, DK])
            inter = [s5a[:, i * 256:(i + 1) * 256] for i in range(2)]
            for i in range(2):
                V.tensor_tensor(inter[i].rearrange("p (h d) -> p h d", h=HEADS),
                                bank(7)[:, 256 * i:256 * i + 256].rearrange("p (h d) -> p h d", h=HEADS), egb, ALU.mult)
            fence()
            V.tensor_tensor(nat[:, 1, 512:768], nat[:, 1, 512:768], inter[0], ALU.subtract).then_inc(rhs_ready.sem, 1)
            og = s5b[:, 0:512].rearrange("p (b c) -> p b c", b=TB)
            og2 = s5b[:, 512:1024].rearrange("p (b c) -> p b c", b=TB)
            dve.wait_ge(*gout_done(layer, 1))
            V.tensor_copy(og[:, 0, :], bank(2)[:, 0:256])
            dve.wait_ge(*gout_done(layer, 2))
            V.tensor_tensor(og[:, 1, :], inter[1], bank(6)[:, 0:256], ALU.add)
            fence()
            V.tensor_tensor(og2, og, og, ALU.mult)
            fence()
            V.tensor_reduce(gss, og2.rearrange("p b (h d) -> p b h d", h=HEADS), AX, ALU.add)
            fence()
            V.tensor_scalar(gss, gss, 1.0 / DK, EPS, ALU.mult, ALU.add)
            fence()
            V.reciprocal(gss, gss).then_inc(go_inv.sem, 1)
            dve.wait_ge(*go_root(layer, 1))
            for t in range(TB):
                o4 = og[:, t, :].rearrange("p (h d) -> p h d", h=HEADS)
                V.tensor_tensor(o4, o4, bc(gss[:, t, :][:, :, None], [P, HEADS, DK]), ALU.mult)
                fence()
                V.tensor_tensor(o4, o4, bc(row("gng")[:, None, :], [P, HEADS, DK]), ALU.mult)
            fence()
            V.tensor_tensor(hn[:, :, 0:256], og, glu_t, ALU.mult)
            V.drain().then_inc(gdn_out.sem, 1)
            V.tensor_tensor_reduce(s5a[:, 512:576], row("lq1"), row("lk1"), 1.0, 0.0, ALU.mult, ALU.add, lsum[:, 0:1])
            V.tensor_tensor_reduce(s5a[:, 576:640], row("lq2"), row("lk2"), 1.0, 0.0, ALU.mult, ALU.add, lsum[:, 1:2])
            V.drain().then_inc(lam_sum.sem, 1)
            for t in range(TB):
                nk = (t + 1) * P
                dve.wait_ge(*att_done(layer, t + 1))
                prob = prob0 if t == 0 else prob1
                pr = prob.rearrange("p h m k -> p (h m) k")
                for m in range(2):
                    o = (bank(m) if t == 0 else ps[:, 2 + 2 * m:4 + 2 * m, :].rearrange("p b n -> p (b n)")
                         ).rearrange("p (h k) -> p h k", k=nk)
                    if t == 1:
                        V.tensor_copy(prob[:, :, m, 0:P], o[:, :, 0:P])
                    V.tensor_tensor(prob[:, :, m, t * P:nk], o[:, :, t * P:nk], bc(negq[:, None, :], [P, HEADS, P]),
                                    ALU.add)
                fence()
                V.tensor_reduce(mx[:, 8 * t:8 * t + 8], pr, AX, ALU.max)
                fence()
                V.tensor_scalar(mx[:, 8 * t:8 * t + 8], mx[:, 8 * t:8 * t + 8], -(DK ** -0.5), None,
                                ALU.mult).then_inc(att_max.sem, 1)
            dve.wait_ge(*lam_exp(layer, 1))
            V.tensor_tensor(lam, lsum[:, 0:1], lsum[:, 1:2], ALU.subtract)
            fence()
            V.tensor_tensor(lam, lam, row("laminit"), ALU.add)
            fence()
            for t in range(TB):
                dve.wait_ge(*att_exp(layer, t + 1))
                z8 = rz[:, 8 * t:8 * t + 8]
                V.reciprocal(z8, zsum[:, 8 * t:8 * t + 8])
                fence()
                zl = lrz[:, 4 * t:4 * t + 4]
                V.tensor_scalar(zl, z8.rearrange("p (h m) -> p h m", m=2)[:, :, 1], lam, -1.0, ALU.mult, ALU.mult)
                fence()
                prob = prob0 if t == 0 else prob1
                for hd in range(HEADS):
                    V.tensor_scalar(prob[:, hd, 1, :], prob[:, hd, 1, :], zl[:, hd:hd + 1], None, ALU.mult)
                fence()
                for hd in range(HEADS):
                    V.scalar_tensor_tensor(prob[:, hd, 0, :], prob[:, hd, 0, :], z8[:, 2 * hd:2 * hd + 1],
                                           prob[:, hd, 1, :], ALU.mult, ALU.add)
                V.drain().then_inc(pd_ready.sem, 1)
            ao = hn[:, :, 512:1024]
            for t in range(TB):
                dve.wait_ge(*ao_done(layer, t + 1))
                V.tensor_copy(ao[:, t, :], bank(7 if t == 0 else 5))
            fence()
            sq = sreg[:, 0:1024].rearrange("p (b c) -> p b c", b=TB)
            V.tensor_tensor(sq, ao, ao, ALU.mult)
            fence()
            V.tensor_reduce(dss.rearrange("p (b h) -> p b h", b=TB), sq.rearrange("p b (h e) -> p b h e", h=HEADS), AX, ALU.add)
            fence()
            V.tensor_scalar(dss, dss, 1.0 / DV2, EPS, ALU.mult, ALU.add)
            fence()
            V.reciprocal(dss, dss).then_inc(ao_inv.sem, 1)
            dve.wait_ge(*ao_root(layer, 1))
            for t in range(TB):
                for hd in range(HEADS):
                    a = ao[:, t, hd * P:(hd + 1) * P]
                    V.scalar_tensor_tensor(a, a, dss[:, 4 * t + hd:4 * t + hd + 1], row("dng"), ALU.mult, ALU.mult)
            fence()
            V.tensor_scalar(ao, ao, row("lamrest"), None, ALU.mult)
            V.drain().then_inc(mix_ready.sem, 1)
            for i in range(4):
                dve.wait_ge(*proj_done(layer, i + 1))
                hh = h[:, :, 256 * i:256 * i + 256]
                V.tensor_tensor(hh, hh, bank(4 + i).rearrange("p (b c) -> p b c", b=TB), ALU.add).then_inc(resid.sem, 1)
            norm_tokens(layer, 2)
            dve.wait_ge(*trT_ready(layer, 8))
            for t in range(TB):
                V.scalar_tensor_tensor(hn[:, t, :], h[:, t, :], rstd[:, t:t + 1], row("g2"), ALU.mult, ALU.mult)
            V.drain().then_inc(hn_ready.sem, 1)

            def top(layer, head, t, n_wait=True):
                if n_wait:
                    dve.wait_ge(*v_used(layer, (head * TB + t - 1) * TOPK))
                V.tensor_copy(scur, scores[:, t, bass.ds(head, 1), :].rearrange("p o (a n) -> p (o a) n", a=2))
                fence()
                for a in range(2):
                    V.max(sv[:, a, 0:8], scur[:, a, :])
                fence()
                for a in range(2):
                    V.max_index(si[:, a, 0:8], sv[:, a, 0:8], scur[:, a, :])
                    V.match_replace(scur2[:, a, :], sv[:, a, 0:8], scur[:, a, :], LOWEST)
                fence()
                for a in range(2):
                    V.max(sv[:, a, 8:16], scur2[:, a, :])
                fence()
                for a in range(2):
                    V.max_index(si[:, a, 8:16], sv[:, a, 8:16], scur2[:, a, :])
                c2d = cand.rearrange("p (a b) -> p a b", a=TOPK)
                V.tensor_tensor(c2d, bc(sv[:, 0, :][:, :, None], [P, TOPK, TOPK]),
                                bc(sv[:, 1, :][:, None, :], [P, TOPK, TOPK]), ALU.add)
                fence()
                V.tensor_copy(sif, si)
                V.max(tv[:, 0:8], cand)
                fence()
                V.max_index(tp[:, 0:8], tv[:, 0:8], cand)
                V.match_replace(cand2, tv[:, 0:8], cand, LOWEST)
                fence()
                V.max(tv[:, 8:16], cand2)
                fence()
                V.max_index(tp[:, 8:16], tv[:, 8:16], cand2)
                V.tensor_scalar(gate[:, t, :], tv, tv[:, 0:1], None, ALU.subtract).then_inc(top_ready.sem, 1)
                fence()
                V.tensor_scalar(ab_u[:, 0, :], tp, 4, None, ALU.logical_shift_right)
                V.tensor_scalar(ab_u[:, 1, :], tp, 15, None, ALU.bitwise_and)
                fence()
                V.tensor_copy(ab_f, ab_u)
                fence()
                V.tensor_tensor(onehot.rearrange("p a k n -> p (a k) n"),
                                bc(ab_f.rearrange("p a k -> p (a k)")[:, :, None], [P, 2 * TOPK, TOPK]),
                                bc(iota[:, None, :], [P, 2 * TOPK, TOPK]), ALU.is_equal)
                fence()
                for a in range(2):
                    V.tensor_tensor(onehot[:, a, :, :], onehot[:, a, :, :],
                                    bc(sif[:, a, :][:, None, :], [P, TOPK, TOPK]), ALU.mult)
                fence()
                V.tensor_reduce(eij.rearrange("p a k -> p (a k)"), onehot.rearrange("p a k n -> p (a k) n"), AX, ALU.add)
                fence()
                V.scalar_tensor_tensor(eij[:, 0, :], eij[:, 0, :], float(NKEY), eij[:, 1, :], ALU.mult, ALU.add)
                fence()
                V.tensor_scalar(ids[:, t, :], eij[:, 0, :], expoff, None, ALU.add).then_inc(ids_ready.sem, 1)

            def use(layer, head, t):
                n = head * TB + t
                xt = ps[:, 2 * t:2 * t + 2, :].rearrange("p b n -> p (b n)")
                for k in range(TOPK):
                    dve.wait_ge(*u_in[k](layer, n * 16 + 16))
                    V.tensor_tensor_reduce(uring[:, k, :], uring[:, k, :], xt, 1.0, 0.0, ALU.mult, ALU.add,
                                           dots[:, t, k:k + 1]).then_inc(dot_done.sem, 1)
                fence()
                dt_ = dots[:, t, :]
                V.tensor_tensor(ge[:, 0, :], dt_, dt_, ALU.mult)
                fence()
                V.tensor_scalar(ge[:, 0, :], ge[:, 0, :], 0.044715, 1.0, ALU.mult, ALU.add)
                fence()
                V.tensor_tensor(gt[:, t, :], ge[:, 0, :], dt_, ALU.mult).then_inc(gelu_arg.sem, 1)
                dve.wait_ge(*gexp_ready(layer, n + 1))
                V.reciprocal(nmax[:, t:t + 1], gz[:, t:t + 1])
                fence()
                V.tensor_scalar(dt_, dt_, nmax[:, t:t + 1], 0.5, ALU.mult, ALU.mult)
                fence()
                V.tensor_tensor(dt_, dt_, gate[:, t, :], ALU.mult)
                fence()
                dve.wait_ge(*gelu_tanh(layer, n + 1))
                V.scalar_tensor_tensor(pk[:, t, :], gt[:, t, :], 1.0, dt_, ALU.add, ALU.mult).then_inc(p_ready.sem, 1)

            dve.wait_ge(*sc_ready(layer, 4))
            dve.wait_ge(*xy_ready(layer, 2))
            dve.wait_ge(*y_init(layer, 1))
            V.tensor_copy(expoff, row("expoff"))
            V.drain().then_inc(params_free.sem, 1)
            top(layer, 0, 0, False)
            with dve.Fori(0, PH - 1) as head:
                use(layer, head, 0)
                top(layer, head, 1)
                use(layer, head, 1)
                top(layer, head + 1, 0)
            use(layer, PH - 1, 0)
            top(layer, PH - 1, 1)
            use(layer, PH - 1, 1)
            dve.wait_ge(*v_used(layer, NG * TOPK))
            for t in range(TB):
                ins = V.tensor_copy(h[:, t, :], ps[:, 4 + 2 * t:6 + 2 * t, :].rearrange("p b n -> p (b n)"))
            V.drain().then_inc(h_ready.sem, 1)
        dve.wait_ge(final_ss.sem, 1)
        V.tensor_scalar(rstd, ss, 1.0 / D, EPS, ALU.mult, ALU.add)
        fence()
        V.reciprocal(rstd, rstd).then_inc(final_inv.sem, 1)
        dve.wait_ge(final_root.sem, 1)
        dve.wait_ge(fin_in.sem, 16)
        for t in range(TB):
            V.scalar_tensor_tensor(hn[:, t, :], h[:, t, :], rstd[:, t:t + 1], row("g2"), ALU.mult, ALU.mult)
        V.drain().then_inc(final_ready.sem, 1)

    @block.scalar
    def _(act):
        S = nc.scalar
        fence = S.drain

        def squares(sig):
            for t in range(TB):
                S.activation(hn[:, t, :], h[:, t, :], ACT.Square, accum_out=ss[:, t:t + 1])
            S.drain().then_inc(sig.sem, 1)

        def copy_turned(layer, turn_no, banks, gain):
            for b in range(4):
                act.wait_ge(*tr_done(layer, 4 * turn_no + b + 1))
                for k in range(2):
                    src = bank(banks[b])[:, 256 * k:256 * k + 256]
                    dst = hnT[:, 2 * b + k, :]
                    if gain:
                        S.activation(dst, src, ACT.Copy, scale=col("g1")[:, 2 * b + k:2 * b + k + 1])
                    else:
                        S.activation(dst, src, ACT.Copy)
                S.drain().then_inc(trT_ready.sem, 1)

        act.wait_ge(cst_in.sem, 16)
        act.wait_ge(x_in.sem, 16)
        with act.Fori(0, DEPTH) as layer:
            act.wait_ge(*h_ready(layer, 0))
            squares(ss_ready)
            act.wait_ge(*inv_ready(layer, 1))
            S.activation(rstd, rstd, ACT.Sqrt).then_inc(rstd_ready.sem, 1)
            act.wait_ge(*params_in(layer, 48))
            S.activation(stp, col("lst"), ACT.Exp).then_inc(step_ready.sem, 1)
            act.wait_ge(*half_angle(layer, 1))
            S.activation(s2, s2, ACT.Sin)
            S.activation(c2, c2, ACT.Sin)
            S.drain().then_inc(sines_ready.sem, 1)
            copy_turned(layer, 0, (4, 5, 6, 7), True)
            act.wait_ge(*pads_ready(layer, 1))
            dests = {f"qkv{i}": raw[:, 2 * i:2 * i + 2, 3:3 + SEQ] for i in range(3)}
            dests |= {"u": uT, "z": zbuf, "v0": vbuf[:, :, 0:256], "v1": vbuf[:, :, 256:512],
                     "q0": qT[:, 0:2, :], "q1": qT[:, 2:4, :], "k0": kT[:, 0:2, :], "k1": kT[:, 2:4, :]}
            for f, name in enumerate(FILLS):
                act.wait_ge(*fill_done(layer, f + 1))
                o = bank(4 + f % 4)
                if name == "ab":
                    S.activation(ab, o[:, 0:16].rearrange("p (b c) -> p b c", b=TB), ACT.Copy).then_inc(fill_act.sem, 1)
                else:
                    S.activation(dests[name], o.rearrange("p (b c) -> p b c", b=2), ACT.Copy).then_inc(fill_act.sem, 1)
            act.wait_ge(*y_arg(layer, 1))
            S.activation(s5w, s5w, ACT.Tanh, scale=float(np.sqrt(2.0 / np.pi))).then_inc(y_tanh.sem, 1)
            act.wait_ge(*a_pre(layer, 1))
            S.activation(beta, ab[:, :, 4:8], ACT.Tanh, scale=0.5)
            S.activation(gb_, gb_, ACT.Exp, scale=-1.0)
            S.activation(ea, row("alog"), ACT.Exp)
            fence()
            S.activation(gb_, gb_, ACT.Ln, bias=1.0)
            S.drain().then_inc(a_ln.sem, 1)
            for j in range(CT):
                act.wait_ge(*conv_done(layer, j + 1))
                S.activation(nat_tanh(j), convd[:, j, :], ACT.Tanh).then_inc(conv_tanh.sem, 1)
            act.wait_ge(*y_arg(layer, 1))
            S.activation(glu_t, zbuf, ACT.Tanh, scale=0.5)
            S.activation(zbuf, zbuf, ACT.Copy, scale=0.5)
            S.drain().then_inc(z_tanh.sem, 1)
            for c in range(TB):
                act.wait_ge(*dec_pre(layer, c + 1))
                S.activation(dec[c], dec[c], ACT.Exp)
                S.drain().then_inc(dec_ready.sem, 1)
            S.activation(eg, gc, ACT.Exp)
            for t in range(TB):
                s = s5a if t == 0 else s5b
                act.wait_ge(*glu_pre(layer, t + 1))
                S.activation(s[:, 256:512], s[:, 256:512], ACT.Tanh, scale=0.5).then_inc(glu_tanh.sem, 1)
            for c in range(TB):
                act.wait_ge(*nat_done(layer, c + 1))
                if c == 0:
                    act.wait_ge(*silu_ready(layer, CT))
                S.activation(nat[:, c, 0:512], bank(4 + 2 * c), ACT.Copy)
                S.activation(nat[:, c, 512:768], bank(5 + 2 * c)[:, 0:256], ACT.Copy)
                S.drain().then_inc(nat_ready.sem, 1)
            act.wait_ge(*qk_inv(layer, 1))
            S.activation(qkn, qkn, ACT.Sqrt).then_inc(qk_root.sem, 1)
            for c in range(TB):
                act.wait_ge(*keyT_done(layer, c + 1))
                if c == 0:
                    act.wait_ge(*nat_done(layer, 2))
                S.activation(keyT[c][:, 0:2, :, :], bank(4 + 2 * c).rearrange("p (k g t) -> p k g t", k=2, g=2), ACT.Copy)
                S.activation(keyT[c][:, 2, :, :], bank(5 + 2 * c)[:, 0:256].rearrange("p (g t) -> p g t", g=2), ACT.Copy)
                S.drain().then_inc(keyT_ready.sem, 1)
            for lv in range(1, LEVELS):
                for c in range(TB):
                    act.wait_ge(*x_done(layer, TB * (lv - 1) + c + 1))
                    if lv == 1:
                        act.wait_ge(*gcum_done(layer, 1))
                    else:
                        act.wait_ge(*upd_done(layer, TB * (lv - 2) + c + 1))
                    S.activation(XM[c], bank(4 * c).rearrange("p (h i) -> p h i", h=HEADS), ACT.Copy).then_inc(x_ready.sem, 1)
            for c in range(TB):
                act.wait_ge(*vnew_done(layer, c + 1))
                S.activation(unew[:, c, :], bank(4 * c)[:, 0:256], ACT.Copy).then_inc(vnew_ready.sem, 1)
            act.wait_ge(*go_inv(layer, 1))
            S.activation(gss, gss, ACT.Sqrt).then_inc(go_root.sem, 1)
            act.wait_ge(*lam_sum(layer, 1))
            S.activation(lsum, lsum, ACT.Exp).then_inc(lam_exp.sem, 1)
            for t in range(TB):
                prob = (prob0 if t == 0 else prob1).rearrange("p h m k -> p (h m) k")
                act.wait_ge(*att_max(layer, t + 1))
                for i in range(8):
                    S.activation(prob[:, i, :], prob[:, i, :], ACT.Exp, bias=mx[:, 8 * t + i:8 * t + i + 1],
                                 scale=DK ** -0.5, accum_out=zsum[:, 8 * t + i:8 * t + i + 1])
                S.drain().then_inc(att_exp.sem, 1)
            for t in range(TB):
                act.wait_ge(*pT_done(layer, t + 1))
                if t == 0:
                    S.activation(pT0, bank(6).rearrange("p (b g q) -> p b g q", b=2, g=2), ACT.Copy).then_inc(pT_ready.sem, 1)
                else:
                    for i in range(2):
                        S.activation(pT1.rearrange("p h c q -> p (h c q)")[:, 512 * i:512 * i + 512], bank(2 + i), ACT.Copy)
                    S.drain().then_inc(pT_ready.sem, 1)
            act.wait_ge(*ao_inv(layer, 1))
            S.activation(dss, dss, ACT.Sqrt).then_inc(ao_root.sem, 1)
            copy_turned(layer, 1, (0, 1, 2, 3), False)
            act.wait_ge(*resid(layer, 4))
            squares(ss_ready)
            act.wait_ge(*inv_ready(layer, 2))
            S.activation(rstd, rstd, ACT.Sqrt).then_inc(rstd_ready.sem, 1)
            copy_turned(layer, 2, (0, 1, 2, 3), False)
            for i in range(4):
                act.wait_ge(*pq_done(layer, i + 1))
                S.activation(qpT[:, 2 * i:2 * i + 2, :], bank(4 + i).rearrange("p (b t) -> p b t", b=2), ACT.Copy).then_inc(pq_ready.sem, 1)
            for i in range(4):
                t, hg = i // 2, i % 2
                act.wait_ge(*sc_done(layer, i + 1))
                S.activation(scores[:, t, 4 * hg:4 * hg + 4, :].rearrange("p h (a n) -> p a h n", a=2),
                             ps[:, 2 * (i % 2):2 * (i % 2) + 2, :].rearrange("p a (h n) -> p a h n", h=4),
                             ACT.Copy).then_inc(sc_ready.sem, 1)
            fence()
            for t in range(TB):
                for j in range(2):
                    S.activation(bank(2 * t + j), hn[:, t, 512 * j:512 * j + 512], ACT.Copy)
                S.drain().then_inc(xy_ready.sem, 1)

            def softmax(layer, head, t):
                n = head * TB + t
                act.wait_ge(*top_ready(layer, n + 1))
                S.activation(gate[:, t, :], gate[:, t, :], ACT.Exp, accum_out=gz[:, t:t + 1])
                S.drain().then_inc(gexp_ready.sem, 1)

            def gates(layer, head, t):
                n = head * TB + t
                act.wait_ge(*gelu_arg(layer, n + 1))
                S.activation(gt[:, t, :], gt[:, t, :], ACT.Tanh, scale=float(np.sqrt(2.0 / np.pi))).then_inc(gelu_tanh.sem, 1)
                act.wait_ge(*p_ready(layer, n + 1))
                for k in range(TOPK):
                    act.wait_ge(*v_used(layer, n * TOPK + (k - 3)))
                    S.activation(diag[:, k % 4, :], ident, ACT.Copy, scale=pk[:, t, k:k + 1]).then_inc(diag_ready.sem, 1)

            with act.Fori(0, PH) as head:
                for t in range(TB):
                    softmax(layer, head, t)
                    gates(layer, head, t)
        act.wait_ge(*h_ready(DEPTH, 0))
        squares(final_ss)
        act.wait_ge(final_inv.sem, 1)
        S.activation(rstd, rstd, ACT.Sqrt).then_inc(final_root.sem, 1)

    @block.gpsimd
    def _(pool):
        def gather(dst, table, index, done):
            nc.gpsimd.indirect_dma_start(dst, None, table, bass.IndirectOffsetOnAxis(ap=index, axis=0)
                                         ).then_inc(done.sem, 16)

        with pool.Fori(0, DEPTH) as layer:
            with pool.Fori(0, PH) as head:
                for t in range(TB):
                    n = head * TB + t
                    pool.wait_ge(*ids_ready(layer, n + 1))
                    pool.sem_inc(pool_gate.sem, 1)
                    for k in range(TOPK):
                        pool.wait_ge(*dot_done(layer, (n - 1) * TOPK + (k + 1)))
                        pool.sem_inc(pool_gate.sem, 1)
                        gather(uring[:, k, :], u_tab, ids[:, t, k:k + 1], u_in[k])
                    for k in range(TOPK):
                        pool.wait_ge(*v_used(layer, (n - 1) * TOPK + (k + 1)))
                        pool.sem_inc(pool_gate.sem, 1)
                        gather(vring[:, k, :], v_tab, ids[:, t, k:k + 1], v_in[k])


def kernel(**inputs):
    import concourse.bacc as bacc
    from concourse.bass_utils import run_bass_kernel_spmd

    a = {k: np.asarray(v) for k, v in inputs.items()}
    L = DEPTH

    def tiles(w):
        return w.reshape(L, KT, P, -1).transpose(0, 2, 1, 3)

    w_in, w_out, w_q = tiles(a["w_in"]), tiles(a["w_out"]), tiles(a["peer_wq"])
    blocks = [w_in[..., c:c + BLK] for c in IN_COLS.values()]
    blocks += [w[..., i * BLK:(i + 1) * BLK] for w in (w_out, w_q) for i in range(4)]
    w_blocks = np.stack(blocks, 1).reshape(L * NB, P, KT * BLK)

    def states(v):
        return v.reshape(L, MT, P).transpose(0, 2, 1)

    cols = np.zeros((L, P, NCOLS), np.float32)

    def put(arr, where, name, value):
        lo, hi = where[name]
        arr[:, :, lo:hi] = value.reshape(L, -1, hi - lo)

    put(cols, COLS, "g1", a["norm1_g"].reshape(L, KT, P).transpose(0, 2, 1))
    put(cols, COLS, "conv", a["gdn_conv_w"].reshape(L, CONV, CT, P).transpose(0, 3, 2, 1))
    put(cols, COLS, "lre", states(a["s5_lambda_re"]))
    put(cols, COLS, "lim", states(a["s5_lambda_im"]))
    put(cols, COLS, "lst", states(np.repeat(a["s5_log_step"][:, :, None], NSTATE, 2)))
    put(cols, COLS, "dsk", a["s5_d"].reshape(L, 2, P).transpose(0, 2, 1))
    put(cols, COLS, "wab", w_in[..., 1024:1032])
    for name, key in (("bre", "s5_b_re"), ("bim", "s5_b_im")):
        b = np.zeros((L, 2, P, P), np.float32)
        for g in range(GROUPS):
            r = GCH * (g % 8)
            c = NSTATE * (g % 2)
            b[:, g // 8, r:r + GCH, c:c + NSTATE] = a[key][:, g].transpose(0, 2, 1)
        put(cols, COLS, name, b.transpose(0, 2, 1, 3))
    for name, key in (("cre", "s5_c_re"), ("cim", "s5_c_im")):
        c = np.zeros((L, P, MT, 32), np.float32)
        for g in range(GROUPS):
            i = g % 2
            c[:, NSTATE * i:NSTATE * (i + 1), g // 2, GCH * i:GCH * (i + 1)] = a[key][:, g].transpose(0, 2, 1)
        put(cols, COLS, name, c)
    put(cols, COLS, "glu", a["s5_glu_w"].reshape(L, 2, P, 512).transpose(0, 2, 1, 3))

    rows = np.zeros((L, 1, NROWS), np.float32)
    for name, key in (("alog", "gdn_a_log"), ("dt", "gdn_dt_bias"), ("gng", "gdn_norm_g"), ("lq1", "diff_lq1"),
                      ("lk1", "diff_lk1"), ("lq2", "diff_lq2"), ("lk2", "diff_lk2"), ("dng", "diff_norm_g"),
                      ("glb", "s5_glu_b"), ("g2", "norm2_g")):
        put(rows, ROWS, name, a[key])
    lam_init = np.array([0.8 - 0.6 * np.exp(-0.3 * i) for i in range(L)])
    put(rows, ROWS, "laminit", lam_init)
    put(rows, ROWS, "lamrest", 1.0 - lam_init)
    put(rows, ROWS, "expoff", np.arange(L) * float(NEXP))
    rows = np.repeat(rows, P, 1)

    keys = a["peer_keys"].transpose(0, 2, 4, 1, 3).reshape(L, P, PH * NKEY)

    i, j = np.arange(P)[None, :], np.arange(P)[:, None]
    cst = np.zeros((P, NCST), np.float32)
    levels = [((i >> (l + 1)) == (j >> (l + 1))) & ((i >> l) % 2 == 1) & ((j >> l) % 2 == 0) for l in range(LEVELS)]
    for name, value in (("ident", i == j), ("tri", j <= i), ("negT", np.where(j <= i, 0.0, NEG)),
                        ("negq", np.where(i <= j, 0.0, NEG)), ("lev", np.concatenate(levels, 1)),
                        ("iota", np.tile(np.arange(TOPK), (P, 1)))):
        cst[:, CST[name][0]:CST[name][1]] = value

    arrays = {
        "x": a["x"], "w_blocks": w_blocks, "cols": cols, "rows": rows, "keys": keys,
        "u_tab": a["peer_u"].reshape(L * NEXP, D), "v_tab": a["peer_v"].reshape(L * NEXP, D),
        "cst": cst, "final_g": np.repeat(a["final_g"][None, :], P, 0),
    }
    nc = bacc.Bacc("TRN2", target_bir_lowering=False, num_devices=1)
    named = {f"in_{k}": np.ascontiguousarray(v) for k, v in arrays.items()}
    args = [nc.dram_tensor(k, v.shape, F32, kind="ExternalInput").ap() for k, v in named.items()]
    args.append(nc.dram_tensor("out_0", (1, SEQ, D), F32, kind="ExternalOutput").ap())
    build(nc, *args)
    r = run_bass_kernel_spmd(nc, [named], core_ids=[0])
    return r.results[0]["out_0"]
```

```python
from contextlib import ExitStack

import numpy as np

import concourse.bass as bass
from concourse import mybir

P = 128
D = 1024
KT = D // P
SEQ = 256
TB = SEQ // P
DEPTH = 2
HEADS = 4
DK = 64
CONV = 4
QKV = 3 * HEADS * DK
CT = QKV // P
GROUPS, GCH, NSTATE = 16, 16, 64
ROUNDS = 3
MT = GROUPS * NSTATE // P
DV2 = 128
PH = 8
NKEY = 128
TOPK = 16
NEXP = NKEY * NKEY
EPS = 1e-6
BLK = 256
NEG = -1.0e30
LOWEST = -3.0e38

F32 = mybir.dt.float32
U32 = mybir.dt.uint32
ALU = mybir.AluOpType
ACT = mybir.ActivationFunctionType
AX = mybir.AxisListType.X

IN_COLS = {"u": 1032, "qkv0": 0, "qkv1": 256, "qkv2": 512, "z": 768,
           "v0": 2312, "v1": 2568, "q0": 1288, "q1": 1544, "k0": 1800, "k1": 2056}
BLOCKS = list(IN_COLS) + [f"out{i}" for i in range(4)] + [f"wq{i}" for i in range(4)]
NB = len(BLOCKS)
RING = 8
FIRST_SLOT = RING - NB % RING


def slot(n):
    return (n + FIRST_SLOT) % RING


FILLS = ["u", "qkv0", "qkv1", "qkv2", "ab", "z", "v0", "v1", "q0", "q1", "k0", "k1"]


def fields(*pairs):
    at, out = 0, {}
    for name, n in pairs:
        out[name] = (at, at + n)
        at += n
    return out, at


COLS, NCOLS = fields(("g1", KT), ("conv", CT * CONV), ("lre", MT), ("lim", MT), ("lst", MT), ("dsk", 2),
                     ("wab", KT * 8), ("bre", 2 * P), ("bim", 2 * P), ("cre", MT * 32), ("cim", MT * 32),
                     ("glu", 2 * 512))
ROWS, NROWS = fields(("alog", HEADS), ("dt", HEADS), ("gng", DK), ("lq1", 64), ("lk1", 64), ("lq2", 64),
                     ("lk2", 64), ("dng", DV2), ("glb", 512), ("g2", D), ("laminit", 1), ("lamrest", 1),
                     ("expoff", 1), ("pad", 1))
LEVELS = 7
CST, NCST = fields(("ident", P), ("tri", P), ("negT", P), ("negq", P), ("lev", LEVELS * P), ("iota", TOPK))


class Signal:

    def __init__(self, sem, per_layer, start=0):
        self.sem, self.per_layer, self.start = sem, per_layer, start

    def __call__(self, layer, k):
        return self.sem, layer * self.per_layer + (k + self.start)


def build(nc, x, w_blocks, cols_d, rows_d, keys_d, u_tab, v_tab, cst_d, fin_d, out):
    with ExitStack() as ctx:
        _build(nc, ctx, x, w_blocks, cols_d, rows_d, keys_d, u_tab, v_tab, cst_d, fin_d, out)


def _build(nc, ctx, x, w_blocks, cols_d, rows_d, keys_d, u_tab, v_tab, cst_d, fin_d, out):
    def sb(name, shape, dt=F32):
        return ctx.enter_context(nc.sbuf_tensor(name, shape, dt))

    def signal(name, per_layer, start=0):
        return Signal(ctx.enter_context(nc.semaphore(name)), per_layer, start)

    h = sb("h", [P, TB, D])
    hn = sb("hn", [P, TB, D])
    hnT = sb("hnT", [P, KT, SEQ])
    cst = sb("cst", [P, NCST])
    rows = sb("rows", [P, NROWS])
    cols = sb("cols", [P, NCOLS])
    keysT = sb("keysT", [P, PH, NKEY])
    scores = sb("scores", [P, TB, PH, 2 * NKEY])
    small = sb("small", [P, 1024])
    big = sb("big", [P, 2 * 16 * 1024])

    def col(name):
        return cols[:, COLS[name][0]:COLS[name][1]]

    def row(name):
        return rows[:, ROWS[name][0]:ROWS[name][1]]

    def const(name):
        return cst[:, CST[name][0]:CST[name][1]]

    ident, tri, negT, negq = const("ident"), const("tri"), const("negT"), const("negq")
    lev = const("lev").rearrange("p (l i) -> p l i", l=LEVELS)
    iota = const("iota")

    wring = big[:, 0:16384].rearrange("p (s k c) -> p s k c", s=RING, k=KT)
    uring = big[:, 0:16384].rearrange("p (s d) -> p s d", s=TOPK)
    vring = big[:, 16384:32768].rearrange("p (s d) -> p s d", s=TOPK)
    taken = [16384]

    def scratch(n):
        a = taken[0]
        taken[0] += n
        assert taken[0] <= 32768, taken[0]
        return big[:, a:a + n]

    reg = scratch(6144)
    phase_c = reg[:, 0:2048].rearrange("p (m t) -> p m t", m=MT)
    phase_s = reg[:, 2048:4096].rearrange("p (m t) -> p m t", m=MT)
    cz_re = reg[:, 4096:5120].rearrange("p (m c) -> p m c", m=MT)
    cz_im = reg[:, 5120:6144].rearrange("p (m c) -> p m c", m=MT)
    raw = scratch(1554).rearrange("p (c t) -> p c t", c=CT)
    convd = scratch(1536).rearrange("p (c t) -> p c t", c=CT)
    nat = scratch(1536).rearrange("p (b c) -> p b c", b=TB)
    zbuf = scratch(512).rearrange("p (b c) -> p b c", b=TB)
    vbuf = scratch(1024).rearrange("p (b c) -> p b c", b=TB)
    qT = scratch(1024).rearrange("p (c t) -> p c t", c=4)
    kT = scratch(1024).rearrange("p (c t) -> p c t", c=4)
    uT = scratch(512).rearrange("p (c t) -> p c t", c=2)
    kb = scratch(512).rearrange("p (b c) -> p b c", b=TB)
    flat_raw = big[:, 16384 + 6144:16384 + 6144 + 1554]
    places = [reg[:, 512 * i:512 * i + 512] for i in range(12)] + [flat_raw[:, 0:512], flat_raw[:, 512:1024]]
    mats = [[m.rearrange("p (h i) -> p h i", h=HEADS) for m in places[7 * c:7 * c + 7]] for c in range(TB)]
    dec, LT, ML, TI, TIT, XM, QK = (
        [mats[c][i] for c in range(TB)] for i in range(7))
    keyT = [convd[:, 3 * c:3 * c + 3, :].rearrange("p k (g t) -> p k g t", g=2) for c in range(TB)]
    sreg = scores[:, :, :, :].rearrange("p b h n -> p (b h n)")
    s5a = sreg[:, 0:1024]
    s5b = sreg[:, 1024:2048]
    s5st = sreg[:, 2048:3072].rearrange("p (b r t) -> p b r t", b=2, r=2)
    s5y = sreg[:, 3072:3584].rearrange("p (c t) -> p c t", c=2)
    s5w = sreg[:, 3584:4096].rearrange("p (c t) -> p c t", c=2)
    prob1 = sreg[:, 0:2048].rearrange("p (h m k) -> p h m k", h=HEADS, m=2)
    prob0 = sreg[:, 2048:3072].rearrange("p (h m k) -> p h m k", h=HEADS, m=2)
    pT1 = sreg[:, 3072:4096].rearrange("p (h c q) -> p h c q", h=HEADS, c=2)
    pT0 = nat[:, :, 0:256].rearrange("p b (g q) -> p b g q", g=2)
    qpT = big[:, 16384:16384 + 2048].rearrange("p (h t) -> p h t", h=PH)
    glu_t = uT
    kd = kb[:, 0, :]
    unew = zbuf
    sel = sb("sel", [P, 2048])
    scur = sel[:, 0:256].rearrange("p (a n) -> p a n", a=2)
    scur2 = sel[:, 256:512].rearrange("p (a n) -> p a n", a=2)
    cand = sel[:, 512:768]
    cand2 = sel[:, 768:1024]
    onehot = sel[:, 1024:1536].rearrange("p (a k n) -> p a k n", a=2, k=TOPK)
    diag = sel[:, 1536:2048].rearrange("p (r c) -> p r c", r=4)

    sm = [0]

    def tiny(n, dt=F32):
        a = sm[0]
        sm[0] += n
        assert sm[0] <= 1024
        return small[:, a:a + n] if dt == F32 else small[:, a:a + n].bitcast(dt)

    ss, rstd, expoff = tiny(2), tiny(2), tiny(1)
    (stp, xr, th, zz, em1, kk_, s2, c2, t0, t1, t2, sin1, cosm1, are, aim, kre, kim, mag) = (tiny(8) for _ in range(18))
    pw = [(tiny(8), tiny(8)), (tiny(8), tiny(8))]
    convh = tiny(24)
    ab = tiny(16).rearrange("p (b c) -> p b c", b=TB)
    beta = tiny(8).rearrange("p (b c) -> p b c", b=TB)
    gg = tiny(8).rearrange("p (b c) -> p b c", b=TB)
    ga, gb_, ea = tiny(8).rearrange("p (b c) -> p b c", b=TB), tiny(8).rearrange("p (b c) -> p b c", b=TB), tiny(4)
    gc = tiny(8).rearrange("p (b c) -> p b c", b=TB)
    eg = tiny(8).rearrange("p (b c) -> p b c", b=TB)
    qkn = tiny(16).rearrange("p (b c) -> p b c", b=TB)
    gss = tiny(8).rearrange("p (b c) -> p b c", b=TB)
    lam, lsum = tiny(1), tiny(2)
    mx, zsum, rz, lrz = tiny(16), tiny(16), tiny(16), tiny(8)
    dss = tiny(8)
    sv = [tiny(32).rearrange("p (a k) -> p a k", a=2) for _ in range(1)][0]
    si = tiny(32, U32).rearrange("p (a k) -> p a k", a=2)
    sif = tiny(32).rearrange("p (a k) -> p a k", a=2)
    tv, tp = tiny(16), tiny(16, U32)
    ab_u = tiny(32, U32).rearrange("p (a k) -> p a k", a=2)
    ab_f = tiny(32).rearrange("p (a k) -> p a k", a=2)
    eij = tiny(32).rearrange("p (a k) -> p a k", a=2)
    ids = tiny(32, U32).rearrange("p (b k) -> p b k", b=TB)
    nmax, gz = tiny(2), tiny(2)
    gate = tiny(32).rearrange("p (b k) -> p b k", b=TB)
    dots = tiny(32).rearrange("p (b k) -> p b k", b=TB)
    ge = tiny(32).rearrange("p (a k) -> p a k", a=2)
    gt = tiny(32).rearrange("p (b k) -> p b k", b=TB)
    pk = tiny(32).rearrange("p (b k) -> p b k", b=TB)

    MX = (0, 8, 12, 16)

    ps = ctx.enter_context(nc.psum_tensor("ps", [P, 8, 512], F32))

    def bank(i):
        return ps[:, i, :]

    cst_in = signal("cst_in", 0)
    x_in = signal("x_in", 0)
    params_in = signal("params_in", 3 * 16)
    slot_blocks = [len([n for n in range(NB) if slot(n) == s]) for s in range(RING)]
    w_in = [signal(f"w_in{s}", 16 * slot_blocks[s]) for s in range(RING)]
    w_used = signal("w_used", NB)
    u_in = [signal(f"u_in{k}", 16 * PH * TB) for k in range(TOPK)]
    v_in = [signal(f"v_in{k}", 16 * PH * TB) for k in range(TOPK)]
    fin_in = signal("fin_in", 0)
    out_done = signal("out_done", 0)

    h_ready = signal("h_ready", 1, start=1)
    ss_ready = signal("ss_ready", 2)
    inv_ready = signal("inv_ready", 2)
    rstd_ready = signal("rstd_ready", 2)
    hn_ready = signal("hn_ready", 2)
    tr_done = signal("tr_done", 12)
    trT_ready = signal("trT_ready", 12)
    fill_done = signal("fill_done", len(FILLS))
    fill_act = signal("fill_act", len(FILLS))
    pads_ready = signal("pads_ready", 1)
    step_ready = signal("step_ready", 1)
    half_angle = signal("half_angle", 1)
    sines_ready = signal("sines_ready", 1)
    cz_ready = signal("cz_ready", 1)
    bu_done = signal("bu_done", MT)
    bu_used = signal("bu_used", MT)
    state_ready = signal("state_ready", MT)
    y_acc = signal("y_acc", MT)
    y_arg = signal("y_arg", 1)
    y_tanh = signal("y_tanh", 1)
    yT_ready = signal("yT_ready", 1)
    glu_done = signal("glu_done", 2)
    glu_pre = signal("glu_pre", 2)
    glu_tanh = signal("glu_tanh", 2)
    a_pre = signal("a_pre", 1)
    a_exp = signal("a_exp", 1)
    a_ln = signal("a_ln", 1)
    g_ready = signal("g_ready", 1)
    gcum_done = signal("gcum_done", 1)
    dec_pre = signal("dec_pre", TB)
    dec_ready = signal("dec_ready", TB)
    conv_done = signal("conv_done", CT)
    conv_tanh = signal("conv_tanh", CT)
    silu_ready = signal("silu_ready", CT)
    nat_done = signal("nat_done", TB)
    nat_ready = signal("nat_ready", TB)
    qk_inv = signal("qk_inv", 1)
    qk_root = signal("qk_root", 1)
    qkb_ready = signal("qkb_ready", TB)
    keyT_done = signal("keyT_done", TB)
    keyT_ready = signal("keyT_ready", TB)
    kk_done = signal("kk_done", TB)
    t1T_ready = signal("t1T_ready", TB)
    t1_done = signal("t1_done", TB)
    t_ready = signal("t_ready", TB * LEVELS)
    x_done = signal("x_done", TB * (LEVELS - 1))
    x_ready = signal("x_ready", TB * (LEVELS - 1))
    upd_done = signal("upd_done", TB * (LEVELS - 1))
    rhs_ready = signal("rhs_ready", TB)
    vnew_done = signal("vnew_done", TB)
    vnew_ready = signal("vnew_ready", TB)
    kd_ready = signal("kd_ready", 1)
    state_done = signal("state_done", 1)
    sbd_ready = signal("sbd_ready", 1)
    inter_done = signal("inter_done", 1)
    gout_done = signal("gout_done", TB)
    go_inv = signal("go_inv", 1)
    go_root = signal("go_root", 1)
    z_tanh = signal("z_tanh", 1)
    lam_sum = signal("lam_sum", 1)
    lam_exp = signal("lam_exp", 1)
    att_done = signal("att_done", ROUNDS)
    att_max = signal("att_max", ROUNDS)
    att_exp = signal("att_exp", ROUNDS)
    pd_ready = signal("pd_ready", ROUNDS)
    pT_done = signal("pT_done", ROUNDS)
    pT_ready = signal("pT_ready", ROUNDS)
    ao_done = signal("ao_done", TB)
    ao_inv = signal("ao_inv", 1)
    ao_root = signal("ao_root", 1)
    mix_ready = signal("mix_ready", 1)
    proj_done = signal("proj_done", 4)
    resid = signal("resid", 4)
    pq_done = signal("pq_done", 4)
    pq_ready = signal("pq_ready", 4)
    sc_done = signal("sc_done", 4)
    sc_ready = signal("sc_ready", 4)
    xy_ready = signal("xy_ready", 2)
    y_init = signal("y_init", 1)
    NG = PH * TB
    params_free = signal("params_free", 1, start=1)
    ids_ready = signal("ids_ready", NG)
    top_ready = signal("top_ready", NG)
    gexp_ready = signal("gexp_ready", NG)
    dot_done = signal("dot_done", NG * TOPK, start=TOPK)
    gelu_arg = signal("gelu_arg", NG)
    gelu_tanh = signal("gelu_tanh", NG)
    p_ready = signal("p_ready", NG)
    diag_ready = signal("diag_ready", NG * TOPK)
    v_used = signal("v_used", NG * TOPK, start=TOPK)
    pool_gate = signal("pool_gate", 0)
    final_ss = signal("final_ss", 0)
    final_inv = signal("final_inv", 0)
    final_root = signal("final_root", 0)
    final_ready = signal("final_ready", 0)

    block = ctx.enter_context(nc.Block())

    def nat_tanh(j):
        return nat[:, :, :].rearrange("p b c -> p (b c)")[:, j * SEQ:(j + 1) * SEQ]

    @block.sync
    def _(sp):
        sp.dma_start(cst[:, :], cst_d).then_inc(cst_in.sem, 16)
        sp.dma_start(h[:, :, :], x.rearrange("o (b p) d -> p (o b) d", p=P)).then_inc(x_in.sem, 16)
        with sp.Fori(0, DEPTH) as layer:
            sp.wait_ge(*params_free(layer, 0))
            sp.dma_start(cols[:, :], cols_d[bass.ds(layer, 1), :, :].rearrange("o p c -> p (o c)")).then_inc(params_in.sem, 16)
            sp.dma_start(rows[:, :], rows_d[bass.ds(layer, 1), :, :].rearrange("o p c -> p (o c)")).then_inc(params_in.sem, 16)
            sp.dma_start(keysT[:, :, :].rearrange("p h n -> p (h n)"),
                         keys_d[bass.ds(layer, 1), :, :].rearrange("o p c -> p (o c)")).then_inc(params_in.sem, 16)
            for n in range(NB):
                if n == 0:
                    sp.wait_ge(*dot_done(layer, 0))
                elif n >= RING:
                    sp.wait_ge(*w_used(layer, n - RING + 1))
                sp.dma_start(wring[:, slot(n), :, :].rearrange("p k c -> p (k c)"),
                             w_blocks[bass.ds(layer * NB + n, 1), :, :].rearrange("o p c -> p (o c)")
                             ).then_inc(w_in[slot(n)].sem, 16)
        sp.wait_ge(*params_free(DEPTH, 0))
        sp.dma_start(row("g2"), fin_d).then_inc(fin_in.sem, 16)
        sp.wait_ge(final_ready.sem, 1)
        sp.dma_start(out.rearrange("o (b p) d -> p (o b) d", p=P), hn[:, :, :]).then_inc(out_done.sem, 16)
        sp.wait_ge(out_done.sem, 16)

    @block.tensor
    def _(pe):
        def mm(o, a, b, start=True, stop=True):
            return nc.tensor.matmul(o, a, b, start=start, stop=stop, skip_group_check=True)

        def turn(o, a):
            return nc.tensor.transpose(o, a, ident)

        def turn_tokens(src, banks, ready):
            for b in range(4):
                if ready is not None:
                    ready(b)
                for k in range(2):
                    for t in range(TB):
                        ins = turn(bank(banks[b])[:, (2 * k + t) * P:(2 * k + t + 1) * P],
                                   src[:, t, (2 * b + k) * P:(2 * b + k + 1) * P])
                ins.then_inc(tr_done.sem, 1)

        def block_in(layer, n):
            pe.wait_ge(*w_in[slot(n)](layer, 16 * (n // RING + 1)))

        def fill_wait(layer, f):
            prev = f - 4
            if prev >= 0:
                pe.wait_ge(*fill_act(layer, prev + 1))

        def fill(layer, f):
            name = FILLS[f]
            o = bank(4 + f % 4)
            fill_wait(layer, f)
            if name == "ab":
                for t in range(TB):
                    for k in range(KT):
                        ins = mm(o[:, 8 * t:8 * t + 8], hnT[:, k, t * P:(t + 1) * P],
                                 col("wab").rearrange("p (k c) -> p k c", k=KT)[:, k, :], k == 0, k == KT - 1)
                ins.then_inc(fill_done.sem, 1)
                return
            n = BLOCKS.index(name)
            w = wring[:, slot(n), :, :]
            block_in(layer, n)
            for j in range(2):
                for k in range(KT):
                    if name[0] in "zv":
                        ins = mm(o[:, j * 256:(j + 1) * 256], hnT[:, k, j * P:(j + 1) * P], w[:, k, :],
                                 k == 0, k == KT - 1)
                    else:
                        ins = mm(o[:, j * 256:(j + 1) * 256], w[:, k, j * P:(j + 1) * P], hnT[:, k, :],
                                 k == 0, k == KT - 1)
            ins.then_inc(fill_done.sem, 1)
            pe.wait_ge(*fill_done(layer, f + 1))
            pe.sem_inc(w_used.sem, 1)

        def bu(layer, m):
            if m >= 3:
                pe.wait_ge(*bu_used(layer, m - 2))
            r = slice(32 * (m % 4), 32 * (m % 4) + 32)
            for i, name in enumerate(("bre", "bim")):
                ins = mm(bank(m % 3)[:, 256 * i:256 * i + 256],
                         col(name).rearrange("p (c n) -> p c n", c=2)[r, m // 4, :], uT[r, m // 4, :])
            ins.then_inc(bu_done.sem, 1)

        def y_part(layer, m):
            pe.wait_ge(*state_ready(layer, m + 1))
            if m == 0:
                pe.wait_ge(*cz_ready(layer, 1))
            for i, cz in enumerate((cz_re, cz_im)):
                ins = mm(bank(3)[:, 256 * (m // 4):256 * (m // 4) + 256], cz[:, m, :], s5st[:, m % 2, i, :],
                         m % 4 == 0 and i == 0, m % 4 == 3 and i == 1)
            ins.then_inc(y_acc.sem, 1)

        pe.wait_ge(cst_in.sem, 16)
        pe.sem_inc(v_used.sem, TOPK)
        with pe.Fori(0, DEPTH) as layer:
            pe.wait_ge(*hn_ready(layer, 1))
            turn_tokens(hn, (4, 5, 6, 7), None)
            pe.wait_ge(*params_in(layer, 48))
            pe.wait_ge(*trT_ready(layer, 4))
            fill(layer, 0)
            pe.wait_ge(*fill_act(layer, 1))
            for m in range(3):
                bu(layer, m)
            for f in range(1, len(FILLS)):
                fill(layer, f)
                m = f - 4
                if 0 <= m < MT:
                    y_part(layer, m)
                    if m + 3 < MT:
                        bu(layer, m + 3)
            pe.wait_ge(*g_ready(layer, 1))
            for c in range(TB):
                ins = mm(bank(0)[:, 4 * c:4 * c + 4], tri, gg[:, c, :])
            for c in range(TB):
                for hd in range(HEADS):
                    ins = mm(bank(1 + c)[:, hd * P:(hd + 1) * P], XM[c][:, hd, :], tri)
            ins.then_inc(gcum_done.sem, 1)
            pe.wait_ge(*fill_act(layer, len(FILLS)))
            pe.wait_ge(*silu_ready(layer, CT))
            for c in range(TB):
                for j in range(CT):
                    o = bank(4 + 2 * c + j // 4)
                    ins = turn(o[:, (j % 4) * P:(j % 4 + 1) * P], convd[:, j, c * P:(c + 1) * P])
                ins.then_inc(nat_done.sem, 1)
            pe.wait_ge(*yT_ready(layer, 1))

            def glu(t):
                for k in range(2):
                    ins = mm(bank(3 + 4 * t), s5w[:, k, t * P:(t + 1) * P],
                             col("glu").rearrange("p (k n) -> p k n", k=2)[:, k, :], k == 0, k == 1)
                ins.then_inc(glu_done.sem, 1)

            glu(0)
            for c in range(TB):
                pe.wait_ge(*qkb_ready(layer, c + 1))
                pe.wait_ge(*nat_ready(layer, c + 1))
                for kind in range(3):
                    for g in range(2):
                        src = (nat[:, c, kind * 256 + g * P:kind * 256 + (g + 1) * P] if kind < 2
                               else kb[:, c, g * P:(g + 1) * P])
                        i = 2 * kind + g
                        ins = turn(bank(4 + 2 * c + i // 4)[:, (i % 4) * P:(i % 4 + 1) * P], src)
                ins.then_inc(keyT_done.sem, 1)
            pe.wait_ge(*dec_pre(layer, 2))
            for c in range(TB):
                pe.wait_ge(*keyT_ready(layer, c + 1))
                if c == 1:
                    glu(1)
                for hd in range(HEADS):
                    r = slice(64 * (hd % 2), 64 * (hd % 2) + 64)
                    g = hd // 2
                    k_ = keyT[c][r, 1, g, :]
                    o = bank(4 * c + hd % 2)
                    mm(o[:, g * P:(g + 1) * P], k_, keyT[c][r, 2, g, :])
                    ins = mm(o[:, 256 + g * P:256 + (g + 1) * P], k_, keyT[c][r, 0, g, :])
                ins.then_inc(kk_done.sem, 1)
            for c in range(TB):
                pe.wait_ge(*t1T_ready(layer, c + 1))
                for hd in range(HEADS):
                    ins = turn(bank(4 * c + 2)[:, hd * P:(hd + 1) * P], TIT[c][:, hd, :])
                ins.then_inc(t1_done.sem, 1)

            def att_scores(r):
                if r == 0:
                    pe.wait_ge(*glu_pre(layer, 2))
                else:
                    pe.wait_ge(*att_max(layer, r))
                t = min(r, 1)
                nk = (t + 1) * P
                heads = range(HEADS) if r == 0 else range(2 * r - 2, 2 * r)
                for i, hd in enumerate(heads):
                    for m in range(2):
                        rows_ = slice(64 * m, 64 * m + 64)
                        ins = mm(bank(3 + 4 * m)[:, i * nk:(i + 1) * nk], qT[rows_, hd, t * P:(t + 1) * P],
                                 kT[rows_, hd, 0:nk])
                ins.then_inc(att_done.sem, 1)

            def att_turn(r):
                pe.wait_ge(*pd_ready(layer, r + 1))
                if r == 0:
                    pe.wait_ge(*att_max(layer, ROUNDS))
                elif r == 2:
                    pe.wait_ge(*pT_ready(layer, 1))
                for i in range(4):
                    src = (prob0[:, i, 0, :] if r == 0 else
                           prob1[:, 2 * (r - 1) + i // 2, 0, (i % 2) * P:(i % 2 + 1) * P])
                    ins = turn(bank(7 if r == 1 else 3)[:, i * P:(i + 1) * P], src)
                ins.then_inc(pT_done.sem, 1)

            def att_values(t):
                pe.wait_ge(*pT_ready(layer, 2 if t == 0 else 3))
                for hd in range(HEADS):
                    for kb_ in range(t + 1):
                        lhs = pT0[:, hd // 2, hd % 2, :] if t == 0 else pT1[:, hd, kb_, :]
                        ins = mm(bank(7 if t == 0 else 3)[:, hd * P:(hd + 1) * P], lhs,
                                 vbuf[:, kb_, hd * P:(hd + 1) * P], kb_ == 0, kb_ == t)
                ins.then_inc(ao_done.sem, 1)

            between = {1: [lambda: att_scores(0)], 2: [lambda: att_scores(1)], 3: [lambda: att_scores(2)],
                       4: [lambda: att_turn(0)], 5: [lambda: att_turn(1), lambda: att_turn(2)],
                       6: [lambda: att_values(0)]}
            for lv in range(1, LEVELS):
                for c in range(TB):
                    pe.wait_ge(*t_ready(layer, TB * (lv - 1) + c + 1))
                    for hd in range(HEADS):
                        ins = mm(bank(4 * c)[:, hd * P:(hd + 1) * P], ML[c][:, hd, :], TI[c][:, hd, :])
                    ins.then_inc(x_done.sem, 1)
                for c in range(TB):
                    pe.wait_ge(*x_ready(layer, TB * (lv - 1) + c + 1))
                    for hd in range(HEADS):
                        ins = mm(bank(4 * c + 1)[:, hd * P:(hd + 1) * P], XM[c][:, hd, :], TIT[c][:, hd, :])
                        if lv < LEVELS - 1:
                            ins = mm(bank(4 * c + 2)[:, hd * P:(hd + 1) * P], TIT[c][:, hd, :], XM[c][:, hd, :])
                    ins.then_inc(upd_done.sem, 1)
                for step in between[lv]:
                    step()

            def solve(c, rhs):
                for hd in range(HEADS):
                    ins = mm(bank(4 * c)[:, hd * DK:(hd + 1) * DK], TIT[c][:, hd, :], rhs[:, hd * DK:(hd + 1) * DK])
                ins.then_inc(vnew_done.sem, 1)

            def inside(c):
                for hd in range(HEADS):
                    ins = mm(bank(4 * c + 2)[:, hd * DK:(hd + 1) * DK], QK[c][:, hd, :],
                             unew[:, c, hd * DK:(hd + 1) * DK])
                ins.then_inc(gout_done.sem, 1)

            pe.wait_ge(*rhs_ready(layer, 1))
            pe.wait_ge(*t_ready(layer, TB * LEVELS))
            solve(0, nat[:, 0, 512:768])
            att_values(1)
            pe.wait_ge(*vnew_ready(layer, 1))
            pe.wait_ge(*kd_ready(layer, 1))
            for g in range(2):
                ins = mm(bank(1)[:, g * P:(g + 1) * P], kd[:, g * P:(g + 1) * P], unew[:, 0, g * P:(g + 1) * P])
            ins.then_inc(state_done.sem, 1)
            inside(0)
            pe.wait_ge(*sbd_ready(layer, 1))
            for i, kind in enumerate((2, 0)):
                for g in range(2):
                    ins = mm(bank(5)[:, 256 * i + g * P:256 * i + (g + 1) * P], keyT[1][:, kind, g, :],
                             XM[0][:, g, :])
            ins.then_inc(inter_done.sem, 1)
            pe.wait_ge(*rhs_ready(layer, 2))
            solve(1, nat[:, 1, 512:768])
            pe.wait_ge(*vnew_ready(layer, 2))
            inside(1)

            pe.wait_ge(*mix_ready(layer, 1))
            turn_tokens(hn, (0, 1, 2, 3), None)
            pe.wait_ge(*trT_ready(layer, 8))
            for i in range(4):
                n = BLOCKS.index(f"out{i}")
                block_in(layer, n)
                for t in range(TB):
                    for k in range(KT):
                        ins = mm(bank(4 + i)[:, 256 * t:256 * t + 256], hnT[:, k, t * P:(t + 1) * P],
                                 wring[:, slot(n), k, :], k == 0, k == KT - 1)
                ins.then_inc(proj_done.sem, 1)
                pe.wait_ge(*proj_done(layer, i + 1))
                pe.sem_inc(w_used.sem, 1)
            pe.wait_ge(*hn_ready(layer, 2))
            turn_tokens(hn, (0, 1, 2, 3), None)
            pe.wait_ge(*trT_ready(layer, 12))
            for i in range(4):
                n = BLOCKS.index(f"wq{i}")
                block_in(layer, n)
                for j in range(2):
                    for k in range(KT):
                        ins = mm(bank(4 + i % 2)[:, 256 * j:256 * j + 256], wring[:, slot(n), k, j * P:(j + 1) * P],
                                 hnT[:, k, :], k == 0, k == KT - 1)
                ins.then_inc(pq_done.sem, 1)
                pe.wait_ge(*pq_done(layer, i + 1))
                pe.sem_inc(w_used.sem, 1)
                pe.wait_ge(*pq_ready(layer, i + 1))
                if i >= 1:
                    pe.wait_ge(*sc_ready(layer, i))
                for j in range(2):
                    for t in range(TB):
                        for a in range(2):
                            r = slice(64 * a, 64 * a + 64)
                            ins = mm(bank(6 + a)[:, (2 * t + j) * P:(2 * t + j + 1) * P],
                                     qpT[r, 2 * i + j, t * P:(t + 1) * P], keysT[r, 2 * i + j, :])
                ins.then_inc(sc_done.sem, 1)
            pe.wait_ge(*sc_ready(layer, 4))
            for t in range(TB):
                for j in range(2):
                    ins = mm(bank(4 + 2 * t + j), ident, h[:, t, 512 * j:512 * j + 512])
            ins.then_inc(y_init.sem, 1)
            with pe.Fori(0, PH) as head:
                for t in range(TB):
                    for k in range(TOPK):
                        n = head * (TB * TOPK) + (t * TOPK + k)
                        pe.wait_ge(*v_in[k](layer, (head * TB + t) * 16 + 16))
                        pe.wait_ge(*diag_ready(layer, n + 1))
                        for j in range(2):
                            ins = mm(bank(4 + 2 * t + j), diag[:, k % 4, :], vring[:, k, 512 * j:512 * j + 512],
                                     False, True)
                        ins.then_inc(v_used.sem, 1)

    @block.vector
    def _(dve):
        V = nc.vector
        fence = V.drain

        def norm_tokens(layer, which):
            dve.wait_ge(*ss_ready(layer, which))
            V.tensor_scalar(rstd, ss, 1.0 / D, EPS, ALU.mult, ALU.add)
            fence()
            V.reciprocal(rstd, rstd).then_inc(inv_ready.sem, 1)
            dve.wait_ge(*rstd_ready(layer, which))

        def bc(a, shape):
            return a.broadcast_to(shape)

        def conv(layer, j):
            dve.wait_ge(*fill_act(layer, 2 + j // 2))
            V.tensor_scalar(convd[:, j, :], raw[:, j, 0:SEQ], convh[:, 4 * j:4 * j + 1], None, ALU.mult)
            for w in range(1, CONV):
                fence()
                ins = V.scalar_tensor_tensor(convd[:, j, :], raw[:, j, w:w + SEQ], convh[:, 4 * j + w:4 * j + w + 1],
                                             convd[:, j, :], ALU.mult, ALU.add)
            ins.then_inc(conv_done.sem, 1)

        def silu(layer, j):
            dve.wait_ge(*conv_tanh(layer, j + 1))
            V.scalar_tensor_tensor(convd[:, j, :], nat_tanh(j), 1.0, convd[:, j, :], ALU.add,
                                   ALU.mult).then_inc(silu_ready.sem, 1)

        dve.wait_ge(cst_in.sem, 16)
        dve.wait_ge(x_in.sem, 16)
        dve.sem_inc(h_ready.sem, 1)
        dve.sem_inc(dot_done.sem, TOPK)
        dve.sem_inc(params_free.sem, 1)
        with dve.Fori(0, DEPTH) as layer:
            norm_tokens(layer, 1)
            for t in range(TB):
                ins = V.tensor_scalar(hn[:, t, :], h[:, t, :], rstd[:, t:t + 1], None, ALU.mult)
            ins.then_inc(hn_ready.sem, 1)

            V.memset(raw[:, :, 0:3], 0.0).then_inc(pads_ready.sem, 1)
            dve.wait_ge(*params_in(layer, 48))
            V.tensor_scalar(convh, col("conv"), 0.5, None, ALU.mult)
            dve.wait_ge(*step_ready(layer, 1))
            V.tensor_tensor(xr, col("lre"), stp, ALU.mult)
            V.tensor_tensor(th, col("lim"), stp, ALU.mult)
            fence()
            V.tensor_scalar(xr, xr, -80.0, 80.0, ALU.max, ALU.min)
            magic = 12582912.0
            V.tensor_scalar(kk_, th, float(1.0 / (2.0 * np.pi)), magic, ALU.mult, ALU.add)
            fence()
            V.tensor_scalar(zz, xr, 1.0 / 128.0, None, ALU.mult)
            V.tensor_scalar(kk_, kk_, magic, None, ALU.subtract)
            fence()
            turn_parts = (6.28125, 0.0019340515136718750, 2.0 * np.pi - 6.28125 - 0.0019340515136718750)
            V.tensor_scalar(em1, zz, 1.0 / 9.0, 1.0, ALU.mult, ALU.add)
            for i, part in enumerate(turn_parts):
                V.scalar_tensor_tensor(th, kk_, -float(part), th, ALU.mult, ALU.add)
                fence()
            V.tensor_scalar(th, th, -float(np.float32(3.1415925)), float(np.float32(3.1415925)), ALU.max, ALU.min)
            fence()
            V.scalar_tensor_tensor(c2, th, -1.0, th, ALU.mult, ALU.max)
            V.tensor_scalar(s2, th, 0.5, None, ALU.mult)
            fence()
            V.tensor_scalar(c2, c2, -0.5, float(np.float32(np.pi / 2)), ALU.mult, ALU.add).then_inc(half_angle.sem, 1)
            for n in range(8, 0, -1):
                V.tensor_tensor(em1, em1, zz, ALU.mult)
                fence()
                if n > 1:
                    V.tensor_scalar(em1, em1, 1.0 / n, 1.0, ALU.mult, ALU.add)
                    fence()
            for _ in range(7):
                V.scalar_tensor_tensor(em1, em1, 2.0, em1, ALU.add, ALU.mult)
                fence()
            V.tensor_scalar(mag, em1, 1.0, None, ALU.add)
            dve.wait_ge(*sines_ready(layer, 1))
            V.scalar_tensor_tensor(sin1, s2, 2.0, c2, ALU.mult, ALU.mult)
            V.scalar_tensor_tensor(cosm1, s2, -2.0, s2, ALU.mult, ALU.mult)
            V.tensor_tensor(t2, col("lre"), col("lre"), ALU.mult)
            V.tensor_tensor(t1, col("lim"), col("lim"), ALU.mult)
            fence()
            V.tensor_scalar(pw[0][0], cosm1, 1.0, None, ALU.add)
            V.tensor_copy(pw[0][1], sin1)
            V.tensor_tensor(t2, t2, t1, ALU.add)
            V.tensor_tensor(aim, mag, sin1, ALU.mult)
            fence()
            V.tensor_tensor(are, em1, pw[0][0], ALU.mult)
            V.reciprocal(t2, t2)
            fence()
            V.tensor_tensor(are, are, cosm1, ALU.add)
            fence()
            V.tensor_tensor(kre, are, col("lre"), ALU.mult)
            V.tensor_tensor(t0, aim, col("lim"), ALU.mult)
            V.tensor_tensor(kim, aim, col("lre"), ALU.mult)
            V.tensor_tensor(t1, are, col("lim"), ALU.mult)
            fence()
            V.tensor_tensor(kre, kre, t0, ALU.add)
            V.tensor_tensor(kim, kim, t1, ALU.subtract)
            fence()
            V.tensor_tensor(kre, kre, t2, ALU.mult)
            V.tensor_tensor(kim, kim, t2, ALU.mult)
            V.memset(phase_c[:, :, 0:1], 1.0)
            V.memset(phase_s[:, :, 0:1], 0.0)
            fence()
            n = 1
            while n < SEQ:
                pc, psn = pw[0] if n in (1, 4, 16, 64) else pw[1]
                nc_, ns_ = pw[1] if n in (1, 4, 16, 64) else pw[0]
                A = s5a.rearrange("p (m t) -> p m t", m=MT)[:, :, 0:n]
                B = s5b.rearrange("p (m t) -> p m t", m=MT)[:, :, 0:n]
                pcb, psb = bc(pc[:, :, None], [P, MT, n]), bc(psn[:, :, None], [P, MT, n])
                V.tensor_tensor(A, phase_c[:, :, 0:n], pcb, ALU.mult)
                V.tensor_tensor(B, phase_s[:, :, 0:n], psb, ALU.mult)
                V.tensor_tensor(t0, pc, pc, ALU.mult)
                V.tensor_tensor(t1, psn, psn, ALU.mult)
                V.scalar_tensor_tensor(ns_, pc, 2.0, psn, ALU.mult, ALU.mult)
                fence()
                V.tensor_tensor(phase_c[:, :, n:2 * n], A, B, ALU.subtract)
                V.tensor_tensor(nc_, t0, t1, ALU.subtract)
                fence()
                V.tensor_tensor(A, phase_c[:, :, 0:n], psb, ALU.mult)
                V.tensor_tensor(B, phase_s[:, :, 0:n], pcb, ALU.mult)
                fence()
                V.tensor_tensor(phase_s[:, :, n:2 * n], A, B, ALU.add)
                fence()
                n *= 2
            cre, cim = (col(x).rearrange("p (m c) -> p m c", m=MT) for x in ("cre", "cim"))
            krb, kib = bc(kre[:, :, None], [P, MT, 32]), bc(kim[:, :, None], [P, MT, 32])
            A, B, A2, B2 = (s5a[:, i * 256:(i + 1) * 256].rearrange("p (m c) -> p m c", m=MT) for i in range(4))
            V.memset(reg[:, 4096:6144], 0.0)
            V.tensor_tensor(A, cre, krb, ALU.mult)
            V.tensor_tensor(B, cim, kib, ALU.mult)
            V.tensor_tensor(A2, cre, kib, ALU.mult)
            V.tensor_tensor(B2, cim, krb, ALU.mult)
            fence()
            for j in range(4):
                c = slice(32 * j, 32 * j + 32)
                V.tensor_tensor(cz_re[:, j:MT:4, c], A[:, j:MT:4, :], B[:, j:MT:4, :], ALU.subtract)
                V.scalar_tensor_tensor(cz_im[:, j:MT:4, c], A2[:, j:MT:4, :], -1.0, B2[:, j:MT:4, :],
                                       ALU.mult, ALU.subtract)
            V.drain().then_inc(cz_ready.sem, 1)
            for m in range(MT):
                dve.wait_ge(*bu_done(layer, m + 1))
                o = bank(m % 3).rearrange("p (r t) -> p r t", r=2)
                A = s5a[:, 0:512].rearrange("p (r t) -> p r t", r=2)
                B = s5b[:, 0:512].rearrange("p (r t) -> p r t", r=2)
                R = s5a[:, 512:1024].rearrange("p (r t) -> p r t", r=2)
                S = s5b[:, 512:1024].rearrange("p (r t) -> p r t", r=2)
                c_ = bc(phase_c[:, m:m + 1, :], [P, 2, SEQ])
                s_ = bc(phase_s[:, m:m + 1, :], [P, 2, SEQ])
                V.tensor_tensor(A, o, c_, ALU.mult)
                V.tensor_tensor(B, o, s_, ALU.mult)
                V.drain().then_inc(bu_used.sem, 1)
                V.tensor_tensor(R[:, 0, :], A[:, 0, :], B[:, 1, :], ALU.add)
                V.tensor_tensor(R[:, 1, :], A[:, 1, :], B[:, 0, :], ALU.subtract)
                fence()
                for r in range(2):
                    V.tensor_tensor_scan(S[:, r, :], bc(mag[:, m:m + 1], [P, SEQ]), R[:, r, :], 0.0, ALU.mult, ALU.add)
                fence()
                V.tensor_tensor(A, S, c_, ALU.mult)
                V.tensor_tensor(B, S, s_, ALU.mult)
                fence()
                if m >= 2:
                    dve.wait_ge(*y_acc(layer, m - 1))
                V.tensor_tensor(s5st[:, m % 2, 0, :], A[:, 0, :], B[:, 1, :], ALU.subtract)
                V.tensor_tensor(s5st[:, m % 2, 1, :], A[:, 1, :], B[:, 0, :], ALU.add)
                V.drain().then_inc(state_ready.sem, 1)
                if m < CT:
                    conv(layer, m)
                if m >= 2:
                    silu(layer, m - 2)
                if m == 5:
                    dve.wait_ge(*fill_act(layer, 5))
                    V.tensor_tensor(ga, ab[:, :, 0:4], bc(row("dt")[:, None, :], [P, TB, 4]), ALU.add)
                    fence()
                    V.scalar_tensor_tensor(gb_, ga, -1.0, ga, ALU.mult, ALU.max)
                    V.tensor_scalar(ga, ga, 0.0, None, ALU.max)
                    V.drain().then_inc(a_pre.sem, 1)
            dve.wait_ge(*a_ln(layer, 1))
            V.tensor_tensor(ga, ga, gb_, ALU.add)
            V.tensor_scalar(beta, beta, 0.5, 0.5, ALU.mult, ALU.add)
            fence()
            V.scalar_tensor_tensor(gg, ga, -1.0, bc(ea[:, None, :], [P, TB, 4]), ALU.mult, ALU.mult)
            fence()
            for c in range(TB):
                V.tensor_copy(XM[c], bc(gg[:, c, :][:, :, None], [P, HEADS, P]))
            V.drain().then_inc(g_ready.sem, 1)
            dve.wait_ge(*y_acc(layer, MT))
            for j in range(2):
                V.scalar_tensor_tensor(s5y[:, j, :], uT[:, j, :], col("dsk")[:, j:j + 1],
                                       bank(3)[:, 256 * j:256 * j + 256], ALU.mult, ALU.add)
            fence()
            V.tensor_tensor(s5w, s5y, s5y, ALU.mult)
            fence()
            V.tensor_scalar(s5w, s5w, 0.044715, 1.0, ALU.mult, ALU.add)
            fence()
            V.tensor_tensor(s5w, s5w, s5y, ALU.mult).then_inc(y_arg.sem, 1)
            V.tensor_scalar(s5y, s5y, 0.5, None, ALU.mult)
            dve.wait_ge(*gcum_done(layer, 1))
            V.tensor_copy(gc, bank(0)[:, 0:8].rearrange("p (b c) -> p b c", b=TB))
            fence()
            for c in range(TB):
                for hd in range(HEADS):
                    V.scalar_tensor_tensor(dec[c][:, hd, :], bank(1 + c)[:, hd * P:(hd + 1) * P], gc[:, c, hd:hd + 1],
                                           negT, ALU.subtract, ALU.add)
                V.drain().then_inc(dec_pre.sem, 1)
            dve.wait_ge(*y_tanh(layer, 1))
            V.scalar_tensor_tensor(s5w, s5w, 1.0, s5y, ALU.add, ALU.mult).then_inc(yT_ready.sem, 1)
            dve.wait_ge(*nat_ready(layer, TB))
            V.tensor_tensor(sreg[:, 0:1024].rearrange("p (b c) -> p b c", b=TB), nat[:, :, 0:512], nat[:, :, 0:512], ALU.mult)
            fence()
            V.tensor_reduce(qkn, sreg[:, 0:1024].rearrange("p (b h c) -> p b h c", b=TB, h=8), AX, ALU.add)
            fence()
            V.tensor_scalar(qkn, qkn, 1e-6, None, ALU.add)
            fence()
            V.reciprocal(qkn, qkn).then_inc(qk_inv.sem, 1)
            dve.wait_ge(*qk_root(layer, 1))
            V.tensor_scalar(qkn[:, :, 0:4], qkn[:, :, 0:4], DK ** -0.5, None, ALU.mult)
            fence()
            for c in range(TB):
                n8 = nat[:, c, 0:512].rearrange("p (h d) -> p h d", h=8)
                V.tensor_tensor(n8, n8, bc(qkn[:, c, :][:, :, None], [P, 8, DK]), ALU.mult)
                fence()
                bb = bc(beta[:, c, :][:, :, None], [P, HEADS, DK])
                V.tensor_tensor(kb[:, c, :].rearrange("p (h d) -> p h d", h=HEADS),
                                nat[:, c, 256:512].rearrange("p (h d) -> p h d", h=HEADS), bb, ALU.mult)
                n4 = nat[:, c, 512:768].rearrange("p (h d) -> p h d", h=HEADS)
                V.tensor_tensor(n4, n4, bb, ALU.mult)
                V.drain().then_inc(qkb_ready.sem, 1)
            dve.wait_ge(*glu_done(layer, 1))
            V.tensor_tensor(s5a[:, 0:512], bank(3), row("glb"), ALU.add).then_inc(glu_pre.sem, 1)
            dve.wait_ge(*z_tanh(layer, 1))
            V.scalar_tensor_tensor(glu_t, glu_t, 1.0, zbuf, ALU.add, ALU.mult)
            V.tensor_tensor_reduce(s5b[:, 512:576], row("lq1"), row("lk1"), 1.0, 0.0, ALU.mult, ALU.add, lsum[:, 0:1])
            V.tensor_tensor_reduce(s5b[:, 576:640], row("lq2"), row("lk2"), 1.0, 0.0, ALU.mult, ALU.add, lsum[:, 1:2])
            V.drain().then_inc(lam_sum.sem, 1)
            idb = bc(ident[:, None, :], [P, HEADS, P])
            for c in range(TB):
                dve.wait_ge(*kk_done(layer, c + 1))
                dve.wait_ge(*dec_ready(layer, c + 1))
                for r in range(2):
                    o = bank(4 * c + r).rearrange("p (k g i) -> p k g i", k=2, g=2)
                    V.tensor_tensor(LT[c][:, r:HEADS:2, :], o[:, 0], dec[c][:, r:HEADS:2, :], ALU.mult)
                    V.tensor_tensor(QK[c][:, r:HEADS:2, :], o[:, 1], dec[c][:, r:HEADS:2, :], ALU.mult)
                fence()
                V.tensor_tensor(TIT[c], LT[c], bc(lev[:, 0:1, :], [P, HEADS, P]), ALU.mult)
                V.tensor_tensor(ML[c], LT[c], bc(lev[:, 1:2, :], [P, HEADS, P]), ALU.mult)
                fence()
                V.tensor_tensor(TIT[c], idb, TIT[c], ALU.subtract).then_inc(t1T_ready.sem, 1)
            for c in range(TB):
                dve.wait_ge(*t1_done(layer, c + 1))
                V.tensor_copy(TI[c], bank(4 * c + 2).rearrange("p (h i) -> p h i", h=HEADS)).then_inc(t_ready.sem, 1)

            def glu_second():
                dve.wait_ge(*glu_done(layer, 2))
                V.tensor_tensor(s5b[:, 0:512], bank(7), row("glb"), ALU.add).then_inc(glu_pre.sem, 1)

            def glu_out():
                for t in range(TB):
                    s = s5a if t == 0 else s5b
                    dve.wait_ge(*glu_tanh(layer, t + 1))
                    V.tensor_scalar(s[:, 256:512], s[:, 256:512], 0.5, 0.5, ALU.mult, ALU.add)
                    fence()
                    V.tensor_tensor(hn[:, t, 256:512], s[:, 0:256], s[:, 256:512], ALU.mult)
                fence()

            def probs_of(r):
                return prob0 if r == 0 else prob1[:, 2 * r - 2:2 * r]

            def att_mask(r):
                t = min(r, 1)
                nk = (t + 1) * P
                pr = probs_of(r)
                nh = HEADS if r == 0 else 2
                dve.wait_ge(*att_done(layer, r + 1))
                for m in range(2):
                    o = bank(3 + 4 * m).rearrange("p (h k) -> p h k", k=nk)
                    if t == 1:
                        V.tensor_copy(pr[:, :, m, 0:P], o[:, :, 0:P])
                    V.tensor_tensor(pr[:, :, m, t * P:nk], o[:, :, t * P:nk], bc(negq[:, None, :], [P, nh, P]), ALU.add)
                fence()
                mr = mx[:, MX[r]:MX[r + 1]]
                V.tensor_reduce(mr, pr.rearrange("p h m k -> p (h m) k"), AX, ALU.max)
                fence()
                V.tensor_scalar(mr, mr, -(DK ** -0.5), None, ALU.mult).then_inc(att_max.sem, 1)

            def att_diff(r):
                if r == 0:
                    dve.wait_ge(*lam_exp(layer, 1))
                    V.tensor_tensor(lam, lsum[:, 0:1], lsum[:, 1:2], ALU.subtract)
                    fence()
                    V.tensor_tensor(lam, lam, row("laminit"), ALU.add)
                    fence()
                dve.wait_ge(*att_exp(layer, r + 1))
                z = rz[:, MX[r]:MX[r + 1]]
                V.reciprocal(z, zsum[:, MX[r]:MX[r + 1]])
                fence()
                zl = lrz[:, MX[r] // 2:MX[r + 1] // 2]
                V.tensor_scalar(zl, z.rearrange("p (h m) -> p h m", m=2)[:, :, 1], lam, -1.0, ALU.mult, ALU.mult)
                fence()
                pr = probs_of(r)
                nh = HEADS if r == 0 else 2
                for i in range(nh):
                    V.tensor_scalar(pr[:, i, 1, :], pr[:, i, 1, :], zl[:, i:i + 1], None, ALU.mult)
                fence()
                for i in range(nh):
                    V.scalar_tensor_tensor(pr[:, i, 0, :], pr[:, i, 0, :], z[:, 2 * i:2 * i + 1], pr[:, i, 1, :],
                                           ALU.mult, ALU.add)
                V.drain().then_inc(pd_ready.sem, 1)

            between = {1: [lambda: att_mask(0), glu_out], 2: [lambda: att_mask(1)],
                       3: [lambda: att_mask(2), lambda: att_diff(0)], 4: [lambda: att_diff(1)],
                       5: [lambda: att_diff(2)], 6: []}
            glu_second()
            for lv in range(1, LEVELS):
                for c in range(TB):
                    b4 = [bank(4 * c + i).rearrange("p (h i) -> p h i", h=HEADS) for i in range(3)]
                    dve.wait_ge(*upd_done(layer, TB * (lv - 1) + c + 1))
                    V.tensor_tensor(TIT[c], TIT[c], b4[1], ALU.subtract)
                    if lv < LEVELS - 1:
                        V.tensor_tensor(TI[c], TI[c], b4[2], ALU.subtract)
                        V.tensor_tensor(ML[c], LT[c], bc(lev[:, lv + 1:lv + 2, :], [P, HEADS, P]), ALU.mult)
                    V.drain().then_inc(t_ready.sem, 1)
                for step in between[lv]:
                    step()
            V.sem_inc(rhs_ready.sem, 1)
            V.tensor_tensor(kd.rearrange("p (h d) -> p h d", h=HEADS),
                            nat[:, 0, 256:512].rearrange("p (h d) -> p h d", h=HEADS),
                            bc(dec[0][:, :, P - 1:P], [P, HEADS, DK]), ALU.mult)
            V.memset(XM[0][:, :, :], 0.0)
            V.drain().then_inc(kd_ready.sem, 1)
            ao = hn[:, :, 512:1024]
            dve.wait_ge(*ao_done(layer, 1))
            V.tensor_copy(ao[:, 0, :], bank(7))
            dve.wait_ge(*state_done(layer, 1))
            for g in range(2):
                for i in range(2):
                    r = slice(64 * i, 64 * i + 64)
                    V.tensor_copy(XM[0][r, g, r], bank(1)[r, g * P + 64 * i:g * P + 64 * i + 64])
            V.drain().then_inc(sbd_ready.sem, 1)
            dve.wait_ge(*ao_done(layer, 2))
            V.tensor_copy(ao[:, 1, :], bank(3))
            dve.wait_ge(*inter_done(layer, 1))
            egb = bc(eg[:, 1, :][:, :, None], [P, HEADS, DK])
            inter = [s5a[:, i * 256:(i + 1) * 256] for i in range(2)]
            for i in range(2):
                V.tensor_tensor(inter[i].rearrange("p (h d) -> p h d", h=HEADS),
                                bank(5)[:, 256 * i:256 * i + 256].rearrange("p (h d) -> p h d", h=HEADS), egb, ALU.mult)
            fence()
            V.tensor_tensor(nat[:, 1, 512:768], nat[:, 1, 512:768], inter[0], ALU.subtract).then_inc(rhs_ready.sem, 1)
            sq = sreg[:, 2048:3072].rearrange("p (b c) -> p b c", b=TB)
            V.tensor_tensor(sq, ao, ao, ALU.mult)
            fence()
            V.tensor_reduce(dss.rearrange("p (b h) -> p b h", b=TB), sq.rearrange("p b (h e) -> p b h e", h=HEADS), AX, ALU.add)
            fence()
            V.tensor_scalar(dss, dss, 1.0 / DV2, EPS, ALU.mult, ALU.add)
            fence()
            V.reciprocal(dss, dss).then_inc(ao_inv.sem, 1)
            og = s5b[:, 0:512].rearrange("p (b c) -> p b c", b=TB)
            og2 = s5b[:, 512:1024].rearrange("p (b c) -> p b c", b=TB)
            dve.wait_ge(*gout_done(layer, 1))
            V.tensor_copy(og[:, 0, :], bank(2)[:, 0:256])
            dve.wait_ge(*gout_done(layer, 2))
            V.tensor_tensor(og[:, 1, :], inter[1], bank(6)[:, 0:256], ALU.add)
            fence()
            V.tensor_tensor(og2, og, og, ALU.mult)
            fence()
            V.tensor_reduce(gss, og2.rearrange("p b (h d) -> p b h d", h=HEADS), AX, ALU.add)
            fence()
            V.tensor_scalar(gss, gss, 1.0 / DK, EPS, ALU.mult, ALU.add)
            fence()
            V.reciprocal(gss, gss).then_inc(go_inv.sem, 1)
            dve.wait_ge(*ao_root(layer, 1))
            V.tensor_scalar(dss, dss, row("lamrest"), None, ALU.mult)
            fence()
            for t in range(TB):
                for hd in range(HEADS):
                    a = ao[:, t, hd * P:(hd + 1) * P]
                    V.scalar_tensor_tensor(a, a, dss[:, 4 * t + hd:4 * t + hd + 1], row("dng"), ALU.mult, ALU.mult)
            dve.wait_ge(*go_root(layer, 1))
            for t in range(TB):
                o4 = og[:, t, :].rearrange("p (h d) -> p h d", h=HEADS)
                V.tensor_tensor(o4, o4, bc(gss[:, t, :][:, :, None], [P, HEADS, DK]), ALU.mult)
                fence()
                V.tensor_tensor(o4, o4, bc(row("gng")[:, None, :], [P, HEADS, DK]), ALU.mult)
            fence()
            V.tensor_tensor(hn[:, :, 0:256], og, glu_t, ALU.mult)
            V.drain().then_inc(mix_ready.sem, 1)
            for i in range(4):
                dve.wait_ge(*proj_done(layer, i + 1))
                hh = h[:, :, 256 * i:256 * i + 256]
                V.tensor_tensor(hh, hh, bank(4 + i).rearrange("p (b c) -> p b c", b=TB), ALU.add).then_inc(resid.sem, 1)
            norm_tokens(layer, 2)
            dve.wait_ge(*trT_ready(layer, 8))
            for t in range(TB):
                V.scalar_tensor_tensor(hn[:, t, :], h[:, t, :], rstd[:, t:t + 1], row("g2"), ALU.mult, ALU.mult)
            V.drain().then_inc(hn_ready.sem, 1)

            def top(layer, head, t, n_wait=True):
                if n_wait:
                    dve.wait_ge(*v_used(layer, (head * TB + t - 1) * TOPK))
                V.tensor_copy(scur, scores[:, t, bass.ds(head, 1), :].rearrange("p o (a n) -> p (o a) n", a=2))
                fence()
                for a in range(2):
                    V.max(sv[:, a, 0:8], scur[:, a, :])
                fence()
                for a in range(2):
                    V.max_index(si[:, a, 0:8], sv[:, a, 0:8], scur[:, a, :])
                    V.match_replace(scur2[:, a, :], sv[:, a, 0:8], scur[:, a, :], LOWEST)
                fence()
                for a in range(2):
                    V.max(sv[:, a, 8:16], scur2[:, a, :])
                fence()
                for a in range(2):
                    V.max_index(si[:, a, 8:16], sv[:, a, 8:16], scur2[:, a, :])
                c2d = cand.rearrange("p (a b) -> p a b", a=TOPK)
                V.tensor_tensor(c2d, bc(sv[:, 0, :][:, :, None], [P, TOPK, TOPK]),
                                bc(sv[:, 1, :][:, None, :], [P, TOPK, TOPK]), ALU.add)
                fence()
                V.tensor_copy(sif, si)
                V.max(tv[:, 0:8], cand)
                fence()
                V.max_index(tp[:, 0:8], tv[:, 0:8], cand)
                V.match_replace(cand2, tv[:, 0:8], cand, LOWEST)
                fence()
                V.max(tv[:, 8:16], cand2)
                fence()
                V.max_index(tp[:, 8:16], tv[:, 8:16], cand2)
                V.tensor_scalar(gate[:, t, :], tv, tv[:, 0:1], None, ALU.subtract).then_inc(top_ready.sem, 1)
                fence()
                V.tensor_scalar(ab_u[:, 0, :], tp, 4, None, ALU.logical_shift_right)
                V.tensor_scalar(ab_u[:, 1, :], tp, 15, None, ALU.bitwise_and)
                fence()
                V.tensor_copy(ab_f, ab_u)
                fence()
                V.tensor_tensor(onehot.rearrange("p a k n -> p (a k) n"),
                                bc(ab_f.rearrange("p a k -> p (a k)")[:, :, None], [P, 2 * TOPK, TOPK]),
                                bc(iota[:, None, :], [P, 2 * TOPK, TOPK]), ALU.is_equal)
                fence()
                for a in range(2):
                    V.tensor_tensor(onehot[:, a, :, :], onehot[:, a, :, :],
                                    bc(sif[:, a, :][:, None, :], [P, TOPK, TOPK]), ALU.mult)
                fence()
                V.tensor_reduce(eij.rearrange("p a k -> p (a k)"), onehot.rearrange("p a k n -> p (a k) n"), AX, ALU.add)
                fence()
                V.scalar_tensor_tensor(eij[:, 0, :], eij[:, 0, :], float(NKEY), eij[:, 1, :], ALU.mult, ALU.add)
                fence()
                V.tensor_scalar(ids[:, t, :], eij[:, 0, :], expoff, None, ALU.add).then_inc(ids_ready.sem, 1)

            def use(layer, head, t):
                n = head * TB + t
                xt = ps[:, 2 * t:2 * t + 2, :].rearrange("p b n -> p (b n)")
                for k in range(TOPK):
                    dve.wait_ge(*u_in[k](layer, n * 16 + 16))
                    V.tensor_tensor_reduce(uring[:, k, :], uring[:, k, :], xt, 1.0, 0.0, ALU.mult, ALU.add,
                                           dots[:, t, k:k + 1]).then_inc(dot_done.sem, 1)
                fence()
                dt_ = dots[:, t, :]
                V.tensor_tensor(ge[:, 0, :], dt_, dt_, ALU.mult)
                fence()
                V.tensor_scalar(ge[:, 0, :], ge[:, 0, :], 0.044715, 1.0, ALU.mult, ALU.add)
                fence()
                V.tensor_tensor(gt[:, t, :], ge[:, 0, :], dt_, ALU.mult).then_inc(gelu_arg.sem, 1)
                dve.wait_ge(*gexp_ready(layer, n + 1))
                V.reciprocal(nmax[:, t:t + 1], gz[:, t:t + 1])
                fence()
                V.tensor_scalar(dt_, dt_, nmax[:, t:t + 1], 0.5, ALU.mult, ALU.mult)
                fence()
                V.tensor_tensor(dt_, dt_, gate[:, t, :], ALU.mult)
                fence()
                dve.wait_ge(*gelu_tanh(layer, n + 1))
                V.scalar_tensor_tensor(pk[:, t, :], gt[:, t, :], 1.0, dt_, ALU.add, ALU.mult).then_inc(p_ready.sem, 1)

            V.tensor_copy(expoff, row("expoff"))
            dve.wait_ge(*sc_ready(layer, 1))
            top(layer, 0, 0, False)
            dve.wait_ge(*xy_ready(layer, 2))
            dve.wait_ge(*sc_ready(layer, 4))
            V.sem_inc(params_free.sem, 1)
            with dve.Fori(0, PH - 1) as head:
                use(layer, head, 0)
                top(layer, head, 1)
                use(layer, head, 1)
                top(layer, head + 1, 0)
            use(layer, PH - 1, 0)
            top(layer, PH - 1, 1)
            use(layer, PH - 1, 1)
            dve.wait_ge(*v_used(layer, NG * TOPK))
            for t in range(TB):
                ins = V.tensor_copy(h[:, t, :], ps[:, 4 + 2 * t:6 + 2 * t, :].rearrange("p b n -> p (b n)"))
            V.drain().then_inc(h_ready.sem, 1)
        dve.wait_ge(final_ss.sem, 1)
        V.tensor_scalar(rstd, ss, 1.0 / D, EPS, ALU.mult, ALU.add)
        fence()
        V.reciprocal(rstd, rstd).then_inc(final_inv.sem, 1)
        dve.wait_ge(final_root.sem, 1)
        dve.wait_ge(fin_in.sem, 16)
        for t in range(TB):
            V.scalar_tensor_tensor(hn[:, t, :], h[:, t, :], rstd[:, t:t + 1], row("g2"), ALU.mult, ALU.mult)
        V.drain().then_inc(final_ready.sem, 1)

    @block.scalar
    def _(act):
        S = nc.scalar
        fence = S.drain

        def squares(sig):
            for t in range(TB):
                S.activation(hn[:, t, :], h[:, t, :], ACT.Square, accum_out=ss[:, t:t + 1])
            S.drain().then_inc(sig.sem, 1)

        def copy_turned(layer, turn_no, banks, gain):
            for b in range(4):
                act.wait_ge(*tr_done(layer, 4 * turn_no + b + 1))
                for k in range(2):
                    src = bank(banks[b])[:, 256 * k:256 * k + 256]
                    dst = hnT[:, 2 * b + k, :]
                    if gain:
                        S.activation(dst, src, ACT.Copy, scale=col("g1")[:, 2 * b + k:2 * b + k + 1])
                    else:
                        S.activation(dst, src, ACT.Copy)
                S.drain().then_inc(trT_ready.sem, 1)

        act.wait_ge(cst_in.sem, 16)
        act.wait_ge(x_in.sem, 16)
        with act.Fori(0, DEPTH) as layer:
            act.wait_ge(*h_ready(layer, 0))
            squares(ss_ready)
            act.wait_ge(*inv_ready(layer, 1))
            S.activation(rstd, rstd, ACT.Sqrt).then_inc(rstd_ready.sem, 1)
            act.wait_ge(*params_in(layer, 48))
            S.activation(stp, col("lst"), ACT.Exp).then_inc(step_ready.sem, 1)
            act.wait_ge(*half_angle(layer, 1))
            S.activation(s2, s2, ACT.Sin)
            S.activation(c2, c2, ACT.Sin)
            S.drain().then_inc(sines_ready.sem, 1)
            copy_turned(layer, 0, (4, 5, 6, 7), True)
            act.wait_ge(*pads_ready(layer, 1))
            dests = {f"qkv{i}": raw[:, 2 * i:2 * i + 2, 3:3 + SEQ] for i in range(3)}
            dests |= {"u": uT, "z": zbuf, "v0": vbuf[:, :, 0:256], "v1": vbuf[:, :, 256:512],
                     "q0": qT[:, 0:2, :], "q1": qT[:, 2:4, :], "k0": kT[:, 0:2, :], "k1": kT[:, 2:4, :]}
            for f, name in enumerate(FILLS):
                act.wait_ge(*fill_done(layer, f + 1))
                o = bank(4 + f % 4)
                if name == "ab":
                    S.activation(ab, o[:, 0:16].rearrange("p (b c) -> p b c", b=TB), ACT.Copy).then_inc(fill_act.sem, 1)
                else:
                    S.activation(dests[name], o.rearrange("p (b c) -> p b c", b=2), ACT.Copy).then_inc(fill_act.sem, 1)
                j = f - 5
                if 0 <= j < CT:
                    act.wait_ge(*conv_done(layer, j + 1))
                    S.activation(nat_tanh(j), convd[:, j, :], ACT.Tanh).then_inc(conv_tanh.sem, 1)
                if f == 10:
                    act.wait_ge(*a_pre(layer, 1))
                    S.activation(beta, ab[:, :, 4:8], ACT.Tanh, scale=0.5)
                    S.activation(gb_, gb_, ACT.Exp, scale=-1.0)
                    S.activation(ea, row("alog"), ACT.Exp)
                    fence()
                    S.activation(gb_, gb_, ACT.Ln, bias=1.0)
                    S.drain().then_inc(a_ln.sem, 1)
            act.wait_ge(*y_arg(layer, 1))
            S.activation(s5w, s5w, ACT.Tanh, scale=float(np.sqrt(2.0 / np.pi))).then_inc(y_tanh.sem, 1)
            S.activation(glu_t, zbuf, ACT.Tanh, scale=0.5)
            S.activation(zbuf, zbuf, ACT.Copy, scale=0.5)
            S.drain().then_inc(z_tanh.sem, 1)
            for c in range(TB):
                act.wait_ge(*nat_done(layer, c + 1))
                S.activation(nat[:, c, 0:512], bank(4 + 2 * c), ACT.Copy)
                S.activation(nat[:, c, 512:768], bank(5 + 2 * c)[:, 0:256], ACT.Copy)
                S.drain().then_inc(nat_ready.sem, 1)
            for c in range(TB):
                act.wait_ge(*dec_pre(layer, c + 1))
                S.activation(dec[c], dec[c], ACT.Exp)
                S.drain().then_inc(dec_ready.sem, 1)
            S.activation(eg, gc, ACT.Exp)
            act.wait_ge(*qk_inv(layer, 1))
            S.activation(qkn, qkn, ACT.Sqrt).then_inc(qk_root.sem, 1)
            for c in range(TB):
                act.wait_ge(*keyT_done(layer, c + 1))
                S.activation(keyT[c][:, 0:2, :, :], bank(4 + 2 * c).rearrange("p (k g t) -> p k g t", k=2, g=2), ACT.Copy)
                S.activation(keyT[c][:, 2, :, :], bank(5 + 2 * c)[:, 0:256].rearrange("p (g t) -> p g t", g=2), ACT.Copy)
                S.drain().then_inc(keyT_ready.sem, 1)
            act.wait_ge(*lam_sum(layer, 1))
            S.activation(lsum, lsum, ACT.Exp).then_inc(lam_exp.sem, 1)

            def glu_gates():
                for t in range(TB):
                    s = s5a if t == 0 else s5b
                    act.wait_ge(*glu_pre(layer, t + 1))
                    S.activation(s[:, 256:512], s[:, 256:512], ACT.Tanh, scale=0.5).then_inc(glu_tanh.sem, 1)

            def att_exps(r):
                prob = (prob0 if r == 0 else prob1[:, 2 * r - 2:2 * r]).rearrange("p h m k -> p (h m) k")
                act.wait_ge(*att_max(layer, r + 1))
                for i in range(MX[r + 1] - MX[r]):
                    at = MX[r] + i
                    S.activation(prob[:, i, :], prob[:, i, :], ACT.Exp, bias=mx[:, at:at + 1],
                                 scale=DK ** -0.5, accum_out=zsum[:, at:at + 1])
                S.drain().then_inc(att_exp.sem, 1)

            def att_copy(r):
                act.wait_ge(*pT_done(layer, r + 1))
                if r == 0:
                    S.activation(pT0, bank(3).rearrange("p (b g q) -> p b g q", b=2, g=2), ACT.Copy).then_inc(pT_ready.sem, 1)
                else:
                    S.activation(pT1.rearrange("p h c q -> p (h c q)")[:, 512 * (r - 1):512 * r],
                                 bank(7 if r == 1 else 3), ACT.Copy).then_inc(pT_ready.sem, 1)

            between = {1: [glu_gates], 2: [lambda: att_exps(0)], 3: [lambda: att_exps(1)],
                       4: [lambda: att_exps(2)], 5: [lambda: att_copy(0)], 6: [lambda: att_copy(1), lambda: att_copy(2)]}
            for lv in range(1, LEVELS):
                for c in range(TB):
                    act.wait_ge(*x_done(layer, TB * (lv - 1) + c + 1))
                    S.activation(XM[c], bank(4 * c).rearrange("p (h i) -> p h i", h=HEADS), ACT.Copy).then_inc(x_ready.sem, 1)
                for step in between[lv]:
                    step()
            for c in range(TB):
                act.wait_ge(*vnew_done(layer, c + 1))
                S.activation(unew[:, c, :], bank(4 * c)[:, 0:256], ACT.Copy).then_inc(vnew_ready.sem, 1)
            act.wait_ge(*ao_inv(layer, 1))
            S.activation(dss, dss, ACT.Sqrt).then_inc(ao_root.sem, 1)
            act.wait_ge(*go_inv(layer, 1))
            S.activation(gss, gss, ACT.Sqrt).then_inc(go_root.sem, 1)
            copy_turned(layer, 1, (0, 1, 2, 3), False)
            act.wait_ge(*resid(layer, 4))
            squares(ss_ready)
            act.wait_ge(*inv_ready(layer, 2))
            S.activation(rstd, rstd, ACT.Sqrt).then_inc(rstd_ready.sem, 1)
            copy_turned(layer, 2, (0, 1, 2, 3), False)
            fence()
            for t in range(TB):
                for j in range(2):
                    S.activation(bank(2 * t + j), hn[:, t, 512 * j:512 * j + 512], ACT.Copy)
                S.drain().then_inc(xy_ready.sem, 1)
            for i in range(4):
                act.wait_ge(*pq_done(layer, i + 1))
                S.activation(qpT[:, 2 * i:2 * i + 2, :], bank(4 + i % 2).rearrange("p (b t) -> p b t", b=2), ACT.Copy).then_inc(pq_ready.sem, 1)
                act.wait_ge(*sc_done(layer, i + 1))
                for a in range(2):
                    S.activation(scores[:, :, 2 * i:2 * i + 2, a * NKEY:(a + 1) * NKEY],
                                 bank(6 + a).rearrange("p (t h n) -> p t h n", t=TB, h=2), ACT.Copy)
                S.drain().then_inc(sc_ready.sem, 1)

            def softmax(layer, head, t):
                n = head * TB + t
                act.wait_ge(*top_ready(layer, n + 1))
                S.activation(gate[:, t, :], gate[:, t, :], ACT.Exp, accum_out=gz[:, t:t + 1])
                S.drain().then_inc(gexp_ready.sem, 1)

            def gates(layer, head, t):
                n = head * TB + t
                act.wait_ge(*gelu_arg(layer, n + 1))
                S.activation(gt[:, t, :], gt[:, t, :], ACT.Tanh, scale=float(np.sqrt(2.0 / np.pi))).then_inc(gelu_tanh.sem, 1)
                act.wait_ge(*p_ready(layer, n + 1))
                for k in range(TOPK):
                    act.wait_ge(*v_used(layer, n * TOPK + (k - 3)))
                    S.activation(diag[:, k % 4, :], ident, ACT.Copy, scale=pk[:, t, k:k + 1]).then_inc(diag_ready.sem, 1)

            with act.Fori(0, PH) as head:
                for t in range(TB):
                    softmax(layer, head, t)
                    gates(layer, head, t)
        act.wait_ge(*h_ready(DEPTH, 0))
        squares(final_ss)
        act.wait_ge(final_inv.sem, 1)
        S.activation(rstd, rstd, ACT.Sqrt).then_inc(final_root.sem, 1)

    @block.gpsimd
    def _(pool):
        def gather(dst, table, index, done):
            nc.gpsimd.indirect_dma_start(dst, None, table, bass.IndirectOffsetOnAxis(ap=index, axis=0)
                                         ).then_inc(done.sem, 16)

        with pool.Fori(0, DEPTH) as layer:
            with pool.Fori(0, PH) as head:
                for t in range(TB):
                    n = head * TB + t
                    pool.wait_ge(*ids_ready(layer, n + 1))
                    pool.sem_inc(pool_gate.sem, 1)
                    for k in range(TOPK):
                        pool.wait_ge(*dot_done(layer, (n - 1) * TOPK + (k + 1)))
                        pool.sem_inc(pool_gate.sem, 1)
                        if k >= TOPK // 2 and k % 2 == 0:
                            pool.wait_ge(*w_used(layer, NB - (TOPK - k) // 2 + 1))
                            pool.sem_inc(pool_gate.sem, 1)
                        gather(uring[:, k, :], u_tab, ids[:, t, k:k + 1], u_in[k])
                    pool.wait_ge(*y_init(layer, 1))
                    pool.sem_inc(pool_gate.sem, 1)
                    for k in range(TOPK):
                        pool.wait_ge(*v_used(layer, (n - 1) * TOPK + (k + 1)))
                        pool.sem_inc(pool_gate.sem, 1)
                        gather(vring[:, k, :], v_tab, ids[:, t, k:k + 1], v_in[k])


def kernel(**inputs):
    import concourse.bacc as bacc
    from concourse.bass_utils import run_bass_kernel_spmd

    a = {k: np.asarray(v) for k, v in inputs.items()}
    L = DEPTH

    def tiles(w):
        return w.reshape(L, KT, P, -1).transpose(0, 2, 1, 3)

    w_in, w_out, w_q = tiles(a["w_in"]), tiles(a["w_out"]), tiles(a["peer_wq"])
    blocks = [w_in[..., c:c + BLK] for c in IN_COLS.values()]
    blocks += [w[..., i * BLK:(i + 1) * BLK] for w in (w_out, w_q) for i in range(4)]
    w_blocks = np.stack(blocks, 1).reshape(L * NB, P, KT * BLK)

    def states(v):
        return v.reshape(L, MT, P).transpose(0, 2, 1)

    cols = np.zeros((L, P, NCOLS), np.float32)

    def put(arr, where, name, value):
        lo, hi = where[name]
        arr[:, :, lo:hi] = value.reshape(L, -1, hi - lo)

    put(cols, COLS, "g1", a["norm1_g"].reshape(L, KT, P).transpose(0, 2, 1))
    put(cols, COLS, "conv", a["gdn_conv_w"].reshape(L, CONV, CT, P).transpose(0, 3, 2, 1))
    put(cols, COLS, "lre", states(a["s5_lambda_re"]))
    put(cols, COLS, "lim", states(a["s5_lambda_im"]))
    put(cols, COLS, "lst", states(np.repeat(a["s5_log_step"][:, :, None], NSTATE, 2)))
    put(cols, COLS, "dsk", a["s5_d"].reshape(L, 2, P).transpose(0, 2, 1))
    put(cols, COLS, "wab", w_in[..., 1024:1032])
    for name, key in (("bre", "s5_b_re"), ("bim", "s5_b_im")):
        b = np.zeros((L, 2, P, P), np.float32)
        for g in range(GROUPS):
            r = GCH * (g % 8)
            c = NSTATE * (g % 2)
            b[:, g // 8, r:r + GCH, c:c + NSTATE] = a[key][:, g].transpose(0, 2, 1)
        put(cols, COLS, name, b.transpose(0, 2, 1, 3))
    for name, key in (("cre", "s5_c_re"), ("cim", "s5_c_im")):
        c = np.zeros((L, P, MT, 32), np.float32)
        for g in range(GROUPS):
            i = g % 2
            c[:, NSTATE * i:NSTATE * (i + 1), g // 2, GCH * i:GCH * (i + 1)] = a[key][:, g].transpose(0, 2, 1)
        put(cols, COLS, name, c)
    put(cols, COLS, "glu", a["s5_glu_w"].reshape(L, 2, P, 512).transpose(0, 2, 1, 3))

    rows = np.zeros((L, 1, NROWS), np.float32)
    for name, key in (("alog", "gdn_a_log"), ("dt", "gdn_dt_bias"), ("gng", "gdn_norm_g"), ("lq1", "diff_lq1"),
                      ("lk1", "diff_lk1"), ("lq2", "diff_lq2"), ("lk2", "diff_lk2"), ("dng", "diff_norm_g"),
                      ("glb", "s5_glu_b"), ("g2", "norm2_g")):
        put(rows, ROWS, name, a[key])
    lam_init = np.array([0.8 - 0.6 * np.exp(-0.3 * i) for i in range(L)])
    put(rows, ROWS, "laminit", lam_init)
    put(rows, ROWS, "lamrest", 1.0 - lam_init)
    put(rows, ROWS, "expoff", np.arange(L) * float(NEXP))
    rows = np.repeat(rows, P, 1)

    keys = a["peer_keys"].transpose(0, 2, 4, 1, 3).reshape(L, P, PH * NKEY)

    i, j = np.arange(P)[None, :], np.arange(P)[:, None]
    cst = np.zeros((P, NCST), np.float32)
    levels = [((i >> (l + 1)) == (j >> (l + 1))) & ((i >> l) % 2 == 1) & ((j >> l) % 2 == 0) for l in range(LEVELS)]
    for name, value in (("ident", i == j), ("tri", j <= i), ("negT", np.where(j <= i, 0.0, NEG)),
                        ("negq", np.where(i <= j, 0.0, NEG)), ("lev", np.concatenate(levels, 1)),
                        ("iota", np.tile(np.arange(TOPK), (P, 1)))):
        cst[:, CST[name][0]:CST[name][1]] = value

    arrays = {
        "x": a["x"], "w_blocks": w_blocks, "cols": cols, "rows": rows, "keys": keys,
        "u_tab": a["peer_u"].reshape(L * NEXP, D), "v_tab": a["peer_v"].reshape(L * NEXP, D),
        "cst": cst, "final_g": np.repeat(a["final_g"][None, :], P, 0),
    }
    nc = bacc.Bacc("TRN2", target_bir_lowering=False, num_devices=1)
    named = {f"in_{k}": np.ascontiguousarray(v) for k, v in arrays.items()}
    args = [nc.dram_tensor(k, v.shape, F32, kind="ExternalInput").ap() for k, v in named.items()]
    args.append(nc.dram_tensor("out_0", (1, SEQ, D), F32, kind="ExternalOutput").ap())
    build(nc, *args)
    r = run_bass_kernel_spmd(nc, [named], core_ids=[0])
    return r.results[0]["out_0"]
```

```python
from contextlib import ExitStack

import numpy as np

import concourse.bass as bass
from concourse import mybir

P = 128
D = 1024
KT = D // P
SEQ = 256
TB = SEQ // P
DEPTH = 2
HEADS = 4
DK = 64
CONV = 4
QKV = 3 * HEADS * DK
CT = QKV // P
GROUPS, GCH, NSTATE = 16, 16, 64
ROUNDS = 3
MT = GROUPS * NSTATE // P
DV2 = 128
PH = 8
NKEY = 128
TOPK = 16
NEXP = NKEY * NKEY
EPS = 1e-6
BLK = 256
NEG = -1.0e30
LOWEST = -3.0e38

F32 = mybir.dt.float32
U32 = mybir.dt.uint32
ALU = mybir.AluOpType
ACT = mybir.ActivationFunctionType
AX = mybir.AxisListType.X

IN_COLS = {"u": 1032, "qkv0": 0, "qkv1": 256, "qkv2": 512, "z": 768,
           "v0": 2312, "v1": 2568, "q0": 1288, "q1": 1544, "k0": 1800, "k1": 2056}
BLOCKS = list(IN_COLS) + [f"out{i}" for i in range(4)] + [f"wq{i}" for i in range(4)]
NB = len(BLOCKS)
RING = 8
FIRST_SLOT = RING - NB % RING


def slot(n):
    return (n + FIRST_SLOT) % RING


FILLS = ["u", "qkv0", "qkv1", "qkv2", "ab", "z", "v0", "v1", "q0", "q1", "k0", "k1"]


def fields(*pairs):
    at, out = 0, {}
    for name, n in pairs:
        out[name] = (at, at + n)
        at += n
    return out, at


COLS, NCOLS = fields(("g1", KT), ("conv", CT * CONV), ("lre", MT), ("lim", MT), ("lst", MT), ("dsk", 2),
                     ("wab", KT * 8), ("bre", 2 * P), ("bim", 2 * P), ("cre", MT * 32), ("cim", MT * 32),
                     ("glu", 2 * 512))
ROWS, NROWS = fields(("alog", HEADS), ("dt", HEADS), ("gng", DK), ("lq1", 64), ("lk1", 64), ("lq2", 64),
                     ("lk2", 64), ("dng", DV2), ("glb", 512), ("g2", D), ("laminit", 1), ("lamrest", 1),
                     ("expoff", 1), ("pad", 1))
LEVELS = 7
CST, NCST = fields(("ident", P), ("tri", P), ("negT", P), ("negq", P), ("lev", LEVELS * P), ("iota", TOPK))


class Signal:

    def __init__(self, sem, per_layer, start=0):
        self.sem, self.per_layer, self.start = sem, per_layer, start

    def __call__(self, layer, k):
        return self.sem, layer * self.per_layer + (k + self.start)


def build(nc, x, w_blocks, cols_d, rows_d, keys_d, u_tab, v_tab, cst_d, fin_d, out):
    with ExitStack() as ctx:
        _build(nc, ctx, x, w_blocks, cols_d, rows_d, keys_d, u_tab, v_tab, cst_d, fin_d, out)


def _build(nc, ctx, x, w_blocks, cols_d, rows_d, keys_d, u_tab, v_tab, cst_d, fin_d, out):
    def sb(name, shape, dt=F32):
        return ctx.enter_context(nc.sbuf_tensor(name, shape, dt))

    def signal(name, per_layer, start=0):
        return Signal(ctx.enter_context(nc.semaphore(name)), per_layer, start)

    h = sb("h", [P, TB, D])
    hn = sb("hn", [P, TB, D])
    hnT = sb("hnT", [P, KT, SEQ])
    cst = sb("cst", [P, NCST])
    rows = sb("rows", [P, NROWS])
    cols = sb("cols", [P, NCOLS])
    keysT = sb("keysT", [P, PH, NKEY])
    scores = sb("scores", [P, TB, PH, 2 * NKEY])
    small = sb("small", [P, 1024])
    big = sb("big", [P, 2 * 16 * 1024])

    def col(name):
        return cols[:, COLS[name][0]:COLS[name][1]]

    def row(name):
        return rows[:, ROWS[name][0]:ROWS[name][1]]

    def const(name):
        return cst[:, CST[name][0]:CST[name][1]]

    ident, tri, negT, negq = const("ident"), const("tri"), const("negT"), const("negq")
    lev = const("lev").rearrange("p (l i) -> p l i", l=LEVELS)
    iota = const("iota")

    wring = big[:, 0:16384].rearrange("p (s k c) -> p s k c", s=RING, k=KT)
    uring = big[:, 0:16384].rearrange("p (s d) -> p s d", s=TOPK)
    vring = big[:, 16384:32768].rearrange("p (s d) -> p s d", s=TOPK)
    taken = [16384]

    def scratch(n):
        a = taken[0]
        taken[0] += n
        assert taken[0] <= 32768, taken[0]
        return big[:, a:a + n]

    reg = scratch(6144)
    phase_c = reg[:, 0:2048].rearrange("p (m t) -> p m t", m=MT)
    phase_s = reg[:, 2048:4096].rearrange("p (m t) -> p m t", m=MT)
    cz_re = reg[:, 4096:5120].rearrange("p (m c) -> p m c", m=MT)
    cz_im = reg[:, 5120:6144].rearrange("p (m c) -> p m c", m=MT)
    raw = scratch(1554).rearrange("p (c t) -> p c t", c=CT)
    convd = scratch(1536).rearrange("p (c t) -> p c t", c=CT)
    nat = scratch(1536).rearrange("p (b c) -> p b c", b=TB)
    zbuf = scratch(512).rearrange("p (b c) -> p b c", b=TB)
    vbuf = scratch(1024).rearrange("p (b c) -> p b c", b=TB)
    qT = scratch(1024).rearrange("p (c t) -> p c t", c=4)
    kT = scratch(1024).rearrange("p (c t) -> p c t", c=4)
    uT = scratch(512).rearrange("p (c t) -> p c t", c=2)
    kb = scratch(512).rearrange("p (b c) -> p b c", b=TB)
    flat_raw = big[:, 16384 + 6144:16384 + 6144 + 1554]
    places = [reg[:, 512 * i:512 * i + 512] for i in range(12)] + [flat_raw[:, 0:512], flat_raw[:, 512:1024]]
    mats = [[m.rearrange("p (h i) -> p h i", h=HEADS) for m in places[7 * c:7 * c + 7]] for c in range(TB)]
    dec, LT, ML, TI, TIT, XM, QK = (
        [mats[c][i] for c in range(TB)] for i in range(7))
    keyT = [convd[:, 3 * c:3 * c + 3, :].rearrange("p k (g t) -> p k g t", g=2) for c in range(TB)]
    sreg = scores[:, :, :, :].rearrange("p b h n -> p (b h n)")
    s5a = sreg[:, 0:1024]
    s5b = sreg[:, 1024:2048]
    s5st = sreg[:, 2048:3072].rearrange("p (b r t) -> p b r t", b=2, r=2)
    s5y = sreg[:, 3072:3584].rearrange("p (c t) -> p c t", c=2)
    s5w = sreg[:, 3584:4096].rearrange("p (c t) -> p c t", c=2)
    prob1 = sreg[:, 0:2048].rearrange("p (h m k) -> p h m k", h=HEADS, m=2)
    prob0 = sreg[:, 2048:3072].rearrange("p (h m k) -> p h m k", h=HEADS, m=2)
    pT1 = sreg[:, 3072:4096].rearrange("p (h c q) -> p h c q", h=HEADS, c=2)
    pT0 = nat[:, :, 0:256].rearrange("p b (g q) -> p b g q", g=2)
    qpT = big[:, 32768 - 2048:32768].rearrange("p (h t) -> p h t", h=PH)
    glu_t = uT
    kd = kb[:, 0, :]
    unew = zbuf
    sel = sb("sel", [P, 2048])
    scur = sel[:, 0:256].rearrange("p (a n) -> p a n", a=2)
    scur2 = sel[:, 256:512].rearrange("p (a n) -> p a n", a=2)
    cand = sel[:, 512:768]
    cand2 = sel[:, 768:1024]
    onehot = sel[:, 1024:1536].rearrange("p (a k n) -> p a k n", a=2, k=TOPK)
    diag = sel[:, 1536:2048].rearrange("p (r c) -> p r c", r=4)

    sm = [0]

    def tiny(n, dt=F32):
        a = sm[0]
        sm[0] += n
        assert sm[0] <= 1024
        return small[:, a:a + n] if dt == F32 else small[:, a:a + n].bitcast(dt)

    ss, rstd, expoff = tiny(2), tiny(2), tiny(1)
    (stp, xr, th, zz, em1, kk_, s2, c2, t0, t1, t2, sin1, cosm1, are, aim, kre, kim, mag) = (tiny(8) for _ in range(18))
    pw = [(tiny(8), tiny(8)), (tiny(8), tiny(8))]
    convh = tiny(24)
    ab = tiny(16).rearrange("p (b c) -> p b c", b=TB)
    beta = tiny(8).rearrange("p (b c) -> p b c", b=TB)
    gg = tiny(8).rearrange("p (b c) -> p b c", b=TB)
    ga, gb_, ea = tiny(8).rearrange("p (b c) -> p b c", b=TB), tiny(8).rearrange("p (b c) -> p b c", b=TB), tiny(4)
    gc = tiny(8).rearrange("p (b c) -> p b c", b=TB)
    eg = tiny(8).rearrange("p (b c) -> p b c", b=TB)
    qkn = tiny(16).rearrange("p (b c) -> p b c", b=TB)
    gss = tiny(8).rearrange("p (b c) -> p b c", b=TB)
    lam, lsum = tiny(1), tiny(2)
    mx, zsum, rz, lrz = tiny(16), tiny(16), tiny(16), tiny(8)
    dss = tiny(8)
    sv = [tiny(32).rearrange("p (a k) -> p a k", a=2) for _ in range(1)][0]
    si = tiny(32, U32).rearrange("p (a k) -> p a k", a=2)
    sif = tiny(32).rearrange("p (a k) -> p a k", a=2)
    tv, tp = tiny(16), tiny(16, U32)
    ab_u = tiny(32, U32).rearrange("p (a k) -> p a k", a=2)
    ab_f = tiny(32).rearrange("p (a k) -> p a k", a=2)
    eij = tiny(32).rearrange("p (a k) -> p a k", a=2)
    ids = tiny(32, U32).rearrange("p (b k) -> p b k", b=TB)
    nmax, gz = tiny(2), tiny(2)
    gate = tiny(32).rearrange("p (b k) -> p b k", b=TB)
    dots = tiny(32).rearrange("p (b k) -> p b k", b=TB)
    ge = tiny(32).rearrange("p (a k) -> p a k", a=2)
    gt = tiny(32).rearrange("p (b k) -> p b k", b=TB)
    pk = tiny(32).rearrange("p (b k) -> p b k", b=TB)

    MX = (0, 8, 12, 16)

    ps = ctx.enter_context(nc.psum_tensor("ps", [P, 8, 512], F32))

    def bank(i):
        return ps[:, i, :]

    cst_in = signal("cst_in", 0)
    x_in = signal("x_in", 0)
    params_in = signal("params_in", 3 * 16)
    slot_blocks = [len([n for n in range(NB) if slot(n) == s]) for s in range(RING)]
    w_in = [signal(f"w_in{s}", 16 * slot_blocks[s]) for s in range(RING)]
    w_used = signal("w_used", NB)
    u_in = [signal(f"u_in{k}", 16 * PH * TB) for k in range(TOPK)]
    v_in = [signal(f"v_in{k}", 16 * PH * TB) for k in range(TOPK)]
    fin_in = signal("fin_in", 0)
    out_done = signal("out_done", 0)

    ss_ready = signal("ss_ready", 2)
    inv_ready = signal("inv_ready", 3)
    rstd_ready = signal("rstd_ready", 3)
    hn_ready = signal("hn_ready", 3)
    tr_done = signal("tr_done", 13)
    trT_ready = signal("trT_ready", 13)
    fill_done = signal("fill_done", len(FILLS))
    fill_act = signal("fill_act", len(FILLS))
    pads_ready = signal("pads_ready", 1)
    step_ready = signal("step_ready", 1)
    half_angle = signal("half_angle", 1)
    sines_ready = signal("sines_ready", 1)
    cz_ready = signal("cz_ready", 1)
    bu_done = signal("bu_done", MT)
    bu_used = signal("bu_used", MT)
    state_ready = signal("state_ready", MT)
    y_acc = signal("y_acc", MT)
    y_arg = signal("y_arg", 1)
    y_tanh = signal("y_tanh", 1)
    yT_ready = signal("yT_ready", 1)
    glu_done = signal("glu_done", 2)
    glu_pre = signal("glu_pre", 2)
    glu_tanh = signal("glu_tanh", 2)
    a_pre = signal("a_pre", 1)
    a_ln = signal("a_ln", 1)
    g_ready = signal("g_ready", 1)
    gcum_done = signal("gcum_done", 1)
    dec_pre = signal("dec_pre", TB)
    dec_ready = signal("dec_ready", TB)
    conv_done = signal("conv_done", CT)
    conv_tanh = signal("conv_tanh", CT)
    silu_ready = signal("silu_ready", CT)
    nat_done = signal("nat_done", TB)
    nat_ready = signal("nat_ready", TB)
    qk_inv = signal("qk_inv", 1)
    qk_root = signal("qk_root", 1)
    qkb_ready = signal("qkb_ready", TB)
    keyT_done = signal("keyT_done", TB)
    keyT_ready = signal("keyT_ready", TB)
    kk_done = signal("kk_done", TB)
    t1T_ready = signal("t1T_ready", TB)
    t1_done = signal("t1_done", TB)
    t_ready = signal("t_ready", TB * LEVELS)
    x_done = signal("x_done", TB * (LEVELS - 1))
    x_ready = signal("x_ready", TB * (LEVELS - 1))
    upd_done = signal("upd_done", TB * (LEVELS - 1))
    rhs_ready = signal("rhs_ready", TB)
    vnew_done = signal("vnew_done", TB)
    vnew_ready = signal("vnew_ready", TB)
    kd_ready = signal("kd_ready", 1)
    state_done = signal("state_done", 1)
    sbd_ready = signal("sbd_ready", 1)
    inter_done = signal("inter_done", 1)
    gout_done = signal("gout_done", TB)
    go_inv = signal("go_inv", 1)
    go_root = signal("go_root", 1)
    z_tanh = signal("z_tanh", 1)
    lam_sum = signal("lam_sum", 1)
    lam_exp = signal("lam_exp", 1)
    att_done = signal("att_done", ROUNDS)
    att_max = signal("att_max", ROUNDS)
    att_exp = signal("att_exp", ROUNDS)
    pd_ready = signal("pd_ready", ROUNDS)
    pT_done = signal("pT_done", ROUNDS)
    pT_ready = signal("pT_ready", ROUNDS)
    ao_done = signal("ao_done", TB)
    ao_inv = signal("ao_inv", 1)
    ao_root = signal("ao_root", 1)
    ao_ss = signal("ao_ss", 1)
    ao_ready = signal("ao_ready", 1)
    mix_ready = signal("mix_ready", TB)
    proj_done = signal("proj_done", 4)
    resid = signal("resid", 4)
    pq_done = signal("pq_done", 5)
    pq_ready = signal("pq_ready", 5)
    sc_done = signal("sc_done", 5)
    sc_ready = signal("sc_ready", 1 + PH)
    xy_ready = signal("xy_ready", 2)
    y_init = signal("y_init", 1)
    NG = PH * TB
    params_free = signal("params_free", 1, start=1)
    ids_ready = signal("ids_ready", NG)
    top_ready = signal("top_ready", NG)
    gexp_ready = signal("gexp_ready", NG)
    dot_done = signal("dot_done", NG * TOPK, start=TOPK)
    gelu_arg = signal("gelu_arg", NG)
    gelu_tanh = signal("gelu_tanh", NG)
    p_ready = signal("p_ready", NG)
    diag_ready = signal("diag_ready", NG * TOPK)
    v_used = signal("v_used", NG * TOPK, start=TOPK)
    pool_gate = signal("pool_gate", 0)
    final_inv = signal("final_inv", 0)
    final_root = signal("final_root", 0)
    final_ready = signal("final_ready", 0)

    block = ctx.enter_context(nc.Block())

    def nat_tanh(j):
        return nat[:, :, :].rearrange("p b c -> p (b c)")[:, j * SEQ:(j + 1) * SEQ]

    @block.sync
    def _(sp):
        sp.dma_start(h[:, :, :], x.rearrange("o (b p) d -> p (o b) d", p=P)).then_inc(x_in.sem, 16)
        sp.dma_start(cst[:, :], cst_d).then_inc(cst_in.sem, 16)
        with sp.Fori(0, DEPTH) as layer:
            sp.wait_ge(*params_free(layer, 0))
            sp.dma_start(cols[:, :], cols_d[bass.ds(layer, 1), :, :].rearrange("o p c -> p (o c)")).then_inc(params_in.sem, 16)
            sp.dma_start(rows[:, :], rows_d[bass.ds(layer, 1), :, :].rearrange("o p c -> p (o c)")).then_inc(params_in.sem, 16)
            sp.dma_start(keysT[:, :, :].rearrange("p h n -> p (h n)"),
                         keys_d[bass.ds(layer, 1), :, :].rearrange("o p c -> p (o c)")).then_inc(params_in.sem, 16)
            for n in range(NB):
                if n == 0:
                    sp.wait_ge(*dot_done(layer, 0))
                elif n >= RING:
                    sp.wait_ge(*w_used(layer, n - RING + 1))
                sp.dma_start(wring[:, slot(n), :, :].rearrange("p k c -> p (k c)"),
                             w_blocks[bass.ds(layer * NB + n, 1), :, :].rearrange("o p c -> p (o c)")
                             ).then_inc(w_in[slot(n)].sem, 16)
        sp.wait_ge(*params_free(DEPTH, 0))
        sp.dma_start(row("g2"), fin_d).then_inc(fin_in.sem, 16)
        for t in range(TB):
            sp.wait_ge(final_ready.sem, t + 1)
            sp.dma_start(out[0, t * P:(t + 1) * P, :], hn[:, t, :]).then_inc(out_done.sem, 16)
        sp.wait_ge(out_done.sem, TB * 16)

    @block.tensor
    def _(pe):
        def mm(o, a, b, start=True, stop=True):
            return nc.tensor.matmul(o, a, b, start=start, stop=stop, skip_group_check=True)

        def turn(o, a):
            return nc.tensor.transpose(o, a, ident)

        def turn_block(src, t):
            for b in range(2):
                for k in range(4):
                    ins = turn(bank(2 * t + b)[:, k * P:(k + 1) * P], src[:, t, (4 * b + k) * P:(4 * b + k + 1) * P])
                ins.then_inc(tr_done.sem, 1)

        def turn_tokens(src, banks):
            for b in range(4):
                for k in range(2):
                    for t in range(TB):
                        ins = turn(bank(banks[b])[:, (2 * k + t) * P:(2 * k + t + 1) * P],
                                   src[:, t, (2 * b + k) * P:(2 * b + k + 1) * P])
                ins.then_inc(tr_done.sem, 1)

        def block_in(layer, n):
            pe.wait_ge(*w_in[slot(n)](layer, 16 * (n // RING + 1)))

        def fill_wait(layer, f):
            prev = f - 4
            if prev >= 0:
                pe.wait_ge(*fill_act(layer, prev + 1))

        def fill(layer, f):
            name = FILLS[f]
            o = bank(4 + f % 4)
            fill_wait(layer, f)
            if name == "ab":
                for t in range(TB):
                    for k in range(KT):
                        ins = mm(o[:, 8 * t:8 * t + 8], hnT[:, k, t * P:(t + 1) * P],
                                 col("wab").rearrange("p (k c) -> p k c", k=KT)[:, k, :], k == 0, k == KT - 1)
                ins.then_inc(fill_done.sem, 1)
                return
            n = BLOCKS.index(name)
            w = wring[:, slot(n), :, :]
            block_in(layer, n)
            for j in range(2):
                for k in range(KT):
                    if f == 0 and j == 0 and k % 2 == 0:
                        pe.wait_ge(*trT_ready(layer, k // 2 + 1))
                    if name[0] in "zv":
                        ins = mm(o[:, j * 256:(j + 1) * 256], hnT[:, k, j * P:(j + 1) * P], w[:, k, :],
                                 k == 0, k == KT - 1)
                    else:
                        ins = mm(o[:, j * 256:(j + 1) * 256], w[:, k, j * P:(j + 1) * P], hnT[:, k, :],
                                 k == 0, k == KT - 1)
            ins.then_inc(fill_done.sem, 1)
            pe.wait_ge(*fill_done(layer, f + 1))
            pe.sem_inc(w_used.sem, 1)

        def bu(layer, m):
            if m >= 3:
                pe.wait_ge(*bu_used(layer, m - 2))
            r = slice(32 * (m % 4), 32 * (m % 4) + 32)
            for i, name in enumerate(("bre", "bim")):
                ins = mm(bank(m % 3)[:, 256 * i:256 * i + 256],
                         col(name).rearrange("p (c n) -> p c n", c=2)[r, m // 4, :], uT[r, m // 4, :])
            ins.then_inc(bu_done.sem, 1)

        def y_part(layer, m):
            pe.wait_ge(*state_ready(layer, m + 1))
            if m == 0:
                pe.wait_ge(*cz_ready(layer, 1))
            for i, cz in enumerate((cz_re, cz_im)):
                ins = mm(bank(3)[:, 256 * (m // 4):256 * (m // 4) + 256], cz[:, m, :], s5st[:, m % 2, i, :],
                         m % 4 == 0 and i == 0, m % 4 == 3 and i == 1)
            ins.then_inc(y_acc.sem, 1)

        pe.wait_ge(cst_in.sem, 16)
        pe.sem_inc(v_used.sem, TOPK)
        pe.sem_inc(params_free.sem, 1)
        with pe.Fori(0, DEPTH) as layer:
            pe.wait_ge(*hn_ready(layer, 1))
            turn_tokens(hn, (4, 5, 6, 7))
            pe.wait_ge(*params_in(layer, 48))
            fill(layer, 0)
            pe.wait_ge(*fill_act(layer, 1))
            for m in range(3):
                bu(layer, m)
            for f in range(1, len(FILLS)):
                fill(layer, f)
                m = f - 4
                if 0 <= m < MT:
                    y_part(layer, m)
                    if m + 3 < MT:
                        bu(layer, m + 3)
            pe.wait_ge(*g_ready(layer, 1))
            for c in range(TB):
                ins = mm(bank(0)[:, 4 * c:4 * c + 4], tri, gg[:, c, :])
            for c in range(TB):
                for hd in range(HEADS):
                    ins = mm(bank(1 + c)[:, hd * P:(hd + 1) * P], XM[c][:, hd, :], tri)
            ins.then_inc(gcum_done.sem, 1)
            pe.wait_ge(*fill_act(layer, len(FILLS)))
            pe.wait_ge(*silu_ready(layer, CT))
            for c in range(TB):
                for j in range(CT):
                    o = bank(4 + 2 * c + j // 4)
                    ins = turn(o[:, (j % 4) * P:(j % 4 + 1) * P], convd[:, j, c * P:(c + 1) * P])
                ins.then_inc(nat_done.sem, 1)
            pe.wait_ge(*yT_ready(layer, 1))

            def glu(t):
                for k in range(2):
                    ins = mm(bank(3 + 4 * t), s5w[:, k, t * P:(t + 1) * P],
                             col("glu").rearrange("p (k n) -> p k n", k=2)[:, k, :], k == 0, k == 1)
                ins.then_inc(glu_done.sem, 1)

            glu(0)
            for c in range(TB):
                pe.wait_ge(*qkb_ready(layer, c + 1))
                pe.wait_ge(*nat_ready(layer, c + 1))
                for kind in range(3):
                    for g in range(2):
                        src = (nat[:, c, kind * 256 + g * P:kind * 256 + (g + 1) * P] if kind < 2
                               else kb[:, c, g * P:(g + 1) * P])
                        i = 2 * kind + g
                        ins = turn(bank(4 + 2 * c + i // 4)[:, (i % 4) * P:(i % 4 + 1) * P], src)
                ins.then_inc(keyT_done.sem, 1)
            pe.wait_ge(*dec_pre(layer, 2))
            for c in range(TB):
                pe.wait_ge(*keyT_ready(layer, c + 1))
                if c == 1:
                    glu(1)
                for hd in range(HEADS):
                    r = slice(64 * (hd % 2), 64 * (hd % 2) + 64)
                    g = hd // 2
                    k_ = keyT[c][r, 1, g, :]
                    o = bank(4 * c + hd % 2)
                    mm(o[:, g * P:(g + 1) * P], k_, keyT[c][r, 2, g, :])
                    ins = mm(o[:, 256 + g * P:256 + (g + 1) * P], k_, keyT[c][r, 0, g, :])
                ins.then_inc(kk_done.sem, 1)
            for c in range(TB):
                pe.wait_ge(*t1T_ready(layer, c + 1))
                for hd in range(HEADS):
                    ins = turn(bank(4 * c + 2)[:, hd * P:(hd + 1) * P], TIT[c][:, hd, :])
                ins.then_inc(t1_done.sem, 1)

            def att_scores(r):
                if r == 0:
                    pe.wait_ge(*glu_pre(layer, 2))
                else:
                    pe.wait_ge(*att_max(layer, r))
                t = min(r, 1)
                nk = (t + 1) * P
                heads = range(HEADS) if r == 0 else range(2 * r - 2, 2 * r)
                for i, hd in enumerate(heads):
                    for m in range(2):
                        rows_ = slice(64 * m, 64 * m + 64)
                        ins = mm(bank(3 + 4 * m)[:, i * nk:(i + 1) * nk], qT[rows_, hd, t * P:(t + 1) * P],
                                 kT[rows_, hd, 0:nk])
                ins.then_inc(att_done.sem, 1)

            def att_turn(r):
                pe.wait_ge(*pd_ready(layer, r + 1))
                if r == 0:
                    pe.wait_ge(*att_max(layer, ROUNDS))
                elif r == 2:
                    pe.wait_ge(*pT_ready(layer, 1))
                for i in range(4):
                    src = (prob0[:, i, 0, :] if r == 0 else
                           prob1[:, 2 * (r - 1) + i // 2, 0, (i % 2) * P:(i % 2 + 1) * P])
                    ins = turn(bank(7 if r == 1 else 3)[:, i * P:(i + 1) * P], src)
                ins.then_inc(pT_done.sem, 1)

            def att_values(t):
                pe.wait_ge(*pT_ready(layer, 2 if t == 0 else 3))
                for hd in range(HEADS):
                    for kb_ in range(t + 1):
                        lhs = pT0[:, hd // 2, hd % 2, :] if t == 0 else pT1[:, hd, kb_, :]
                        ins = mm(bank(7 if t == 0 else 3)[:, hd * P:(hd + 1) * P], lhs,
                                 vbuf[:, kb_, hd * P:(hd + 1) * P], kb_ == 0, kb_ == t)
                ins.then_inc(ao_done.sem, 1)

            between = {1: [lambda: att_scores(0)], 2: [lambda: att_scores(1)], 3: [lambda: att_scores(2)],
                       4: [lambda: att_turn(0)], 5: [lambda: att_turn(1), lambda: att_turn(2)],
                       6: [lambda: att_values(0)]}
            for lv in range(1, LEVELS):
                for c in range(TB):
                    pe.wait_ge(*t_ready(layer, TB * (lv - 1) + c + 1))
                    for hd in range(HEADS):
                        ins = mm(bank(4 * c)[:, hd * P:(hd + 1) * P], ML[c][:, hd, :], TI[c][:, hd, :])
                    ins.then_inc(x_done.sem, 1)
                for c in range(TB):
                    pe.wait_ge(*x_ready(layer, TB * (lv - 1) + c + 1))
                    for hd in range(HEADS):
                        ins = mm(bank(4 * c + 1)[:, hd * P:(hd + 1) * P], XM[c][:, hd, :], TIT[c][:, hd, :])
                        if lv < LEVELS - 1:
                            ins = mm(bank(4 * c + 2)[:, hd * P:(hd + 1) * P], TIT[c][:, hd, :], XM[c][:, hd, :])
                    ins.then_inc(upd_done.sem, 1)
                for step in between[lv]:
                    step()

            def solve(c, rhs):
                for hd in range(HEADS):
                    ins = mm(bank(0)[:, hd * DK:(hd + 1) * DK], TIT[c][:, hd, :], rhs[:, hd * DK:(hd + 1) * DK])
                ins.then_inc(vnew_done.sem, 1)

            def inside(c):
                for hd in range(HEADS):
                    ins = mm(bank(2 - c)[:, hd * DK:(hd + 1) * DK], QK[c][:, hd, :],
                             unew[:, c, hd * DK:(hd + 1) * DK])
                ins.then_inc(gout_done.sem, 1)

            def project(t, half, tiles=range(KT)):
                for i in (2 * half, 2 * half + 1):
                    n = BLOCKS.index(f"out{i}")
                    if t == 0:
                        block_in(layer, n)
                    for k in tiles:
                        ins = mm(bank(4 + 2 * t + half)[:, 256 * (i % 2):256 * (i % 2) + 256],
                                 hnT[:, k, t * P:(t + 1) * P], wring[:, slot(n), k, :],
                                 i % 2 == 0 and k == (2 if t == 0 else 0), k == (1 if t == 0 else KT - 1))
                return ins

            def turn_some(tiles, o):
                for i, k in enumerate(tiles):
                    ins = turn(o[:, i * P:(i + 1) * P], hn[:, 0, k * P:(k + 1) * P])
                ins.then_inc(tr_done.sem, 1)

            pe.wait_ge(*rhs_ready(layer, 1))
            pe.wait_ge(*t_ready(layer, TB * LEVELS))
            solve(0, nat[:, 0, 512:768])
            att_values(1)
            pe.wait_ge(*vnew_ready(layer, 1))
            turn_some((2, 3), bank(0)[:, 0:256])
            pe.wait_ge(*kd_ready(layer, 1))
            for g in range(2):
                ins = mm(bank(1)[:, g * P:(g + 1) * P], kd[:, g * P:(g + 1) * P], unew[:, 0, g * P:(g + 1) * P])
            ins.then_inc(state_done.sem, 1)
            inside(0)
            pe.wait_ge(*sbd_ready(layer, 1))
            for i, kind in enumerate((2, 0)):
                for g in range(2):
                    ins = mm(bank(6)[:, 256 * i + g * P:256 * i + (g + 1) * P], keyT[1][:, kind, g, :],
                             XM[0][:, g, :])
            ins.then_inc(inter_done.sem, 1)
            pe.wait_ge(*trT_ready(layer, 5))
            project(0, 0, (2, 3))
            pe.wait_ge(*rhs_ready(layer, 2))
            solve(1, nat[:, 1, 512:768])
            pe.wait_ge(*vnew_ready(layer, 2))
            inside(1)
            pe.wait_ge(*ao_ready(layer, 1))
            turn_some((4, 5, 6, 7), bank(7))
            project(0, 1, (2, 3))
            pe.wait_ge(*trT_ready(layer, 6))
            for half in range(2):
                project(0, half, (4, 5, 6, 7))
            pe.wait_ge(*mix_ready(layer, 1))
            turn_some((0, 1), bank(0)[:, 0:256])
            pe.wait_ge(*mix_ready(layer, 2))
            turn_block(hn, 1)
            pe.wait_ge(*trT_ready(layer, 7))
            for half in range(2):
                project(0, half, (0, 1)).then_inc(proj_done.sem, 1)
            pe.wait_ge(*trT_ready(layer, 9))
            project(1, 0).then_inc(proj_done.sem, 1)
            pe.wait_ge(*hn_ready(layer, 2))
            turn_block(hn, 0)
            pe.wait_ge(*trT_ready(layer, 11))
            n = BLOCKS.index("wq0")
            block_in(layer, n)
            for k in range(KT):
                ins = mm(bank(4)[:, 0:P], wring[:, slot(n), k, 0:P], hnT[:, k, 0:P], k == 0, k == KT - 1)
            ins.then_inc(pq_done.sem, 1)
            pe.wait_ge(*pq_ready(layer, 1))
            for a in range(2):
                r = slice(64 * a, 64 * a + 64)
                ins = mm(bank(4 + a)[:, 0:NKEY], diag[r, 0, :], keysT[r, 0, :])
            ins.then_inc(sc_done.sem, 1)
            project(1, 1).then_inc(proj_done.sem, 1)
            pe.wait_ge(*proj_done(layer, 4))
            pe.sem_inc(w_used.sem, 4)
            pe.wait_ge(*hn_ready(layer, 3))
            turn_block(hn, 1)
            pe.wait_ge(*trT_ready(layer, 13))
            pe.wait_ge(*sc_ready(layer, 1))
            for i in range(4):
                n = BLOCKS.index(f"wq{i}")
                if i > 0:
                    block_in(layer, n)
                for j in range(2):
                    for k in range(KT):
                        ins = mm(bank(4 + i % 2)[:, 256 * j:256 * j + 256], wring[:, slot(n), k, j * P:(j + 1) * P],
                                 hnT[:, k, :], k == 0, k == KT - 1)
                ins.then_inc(pq_done.sem, 1)
                pe.wait_ge(*pq_done(layer, i + 2))
                pe.sem_inc(w_used.sem, 1)
                pe.wait_ge(*pq_ready(layer, i + 2))
                if i >= 1:
                    pe.wait_ge(*sc_ready(layer, 1 + 2 * i))
                for j in range(2):
                    for t in range(TB):
                        for a in range(2):
                            r = slice(64 * a, 64 * a + 64)
                            ins = mm(bank(6 + a)[:, (2 * t + j) * P:(2 * t + j + 1) * P],
                                     qpT[r, 2 * i + j, t * P:(t + 1) * P], keysT[r, 2 * i + j, :])
                ins.then_inc(sc_done.sem, 1)
            pe.wait_ge(*sc_ready(layer, 1 + PH))
            pe.sem_inc(params_free.sem, 1)
            for t in range(TB):
                for j in range(2):
                    ins = mm(bank(4 + 2 * t + j), ident, h[:, t, 512 * j:512 * j + 512])
            ins.then_inc(y_init.sem, 1)
            with pe.Fori(0, PH) as head:
                for t in range(TB):
                    for k in range(TOPK):
                        n = head * (TB * TOPK) + (t * TOPK + k)
                        pe.wait_ge(*v_in[k](layer, (head * TB + t) * 16 + 16))
                        pe.wait_ge(*diag_ready(layer, n + 1))
                        for j in range(2):
                            ins = mm(bank(4 + 2 * t + j), diag[:, k % 4, :], vring[:, k, 512 * j:512 * j + 512],
                                     False, True)
                        ins.then_inc(v_used.sem, 1)

    @block.vector
    def _(dve):
        V = nc.vector
        fence = V.drain

        def norm_tokens(layer, which, c):
            if which > 1:
                dve.wait_ge(*ss_ready(layer, which - 1))
            V.tensor_scalar(rstd[:, c], ss[:, c], 1.0 / D, EPS, ALU.mult, ALU.add)
            fence()
            V.reciprocal(rstd[:, c], rstd[:, c]).then_inc(inv_ready.sem, 1)
            dve.wait_ge(*rstd_ready(layer, which))

        def square(t):
            V.tensor_tensor_reduce(hn[:, t, :], h[:, t, :], h[:, t, :], 1.0, 0.0, ALU.mult, ALU.add, ss[:, t:t + 1])

        def bc(a, shape):
            return a.broadcast_to(shape)

        def conv(layer, j):
            dve.wait_ge(*fill_act(layer, 2 + j // 2))
            V.tensor_scalar(convd[:, j, :], raw[:, j, 0:SEQ], convh[:, 4 * j:4 * j + 1], None, ALU.mult)
            for w in range(1, CONV):
                fence()
                ins = V.scalar_tensor_tensor(convd[:, j, :], raw[:, j, w:w + SEQ], convh[:, 4 * j + w:4 * j + w + 1],
                                             convd[:, j, :], ALU.mult, ALU.add)
            ins.then_inc(conv_done.sem, 1)

        def silu(layer, j):
            dve.wait_ge(*conv_tanh(layer, j + 1))
            V.scalar_tensor_tensor(convd[:, j, :], nat_tanh(j), 1.0, convd[:, j, :], ALU.add,
                                   ALU.mult).then_inc(silu_ready.sem, 1)

        dve.wait_ge(x_in.sem, 16)
        for t in range(TB):
            square(t)
        fence()
        dve.wait_ge(cst_in.sem, 16)
        dve.sem_inc(dot_done.sem, TOPK)
        with dve.Fori(0, DEPTH) as layer:
            norm_tokens(layer, 1, slice(0, TB))
            for t in range(TB):
                ins = V.tensor_scalar(hn[:, t, :], h[:, t, :], rstd[:, t:t + 1], None, ALU.mult)
            ins.then_inc(hn_ready.sem, 1)

            V.memset(raw[:, :, 0:3], 0.0).then_inc(pads_ready.sem, 1)
            dve.wait_ge(*params_in(layer, 48))
            V.tensor_scalar(convh, col("conv"), 0.5, None, ALU.mult)
            dve.wait_ge(*step_ready(layer, 1))
            V.tensor_tensor(xr, col("lre"), stp, ALU.mult)
            V.tensor_tensor(th, col("lim"), stp, ALU.mult)
            fence()
            V.tensor_scalar(xr, xr, -80.0, 80.0, ALU.max, ALU.min)
            magic = 12582912.0
            V.tensor_scalar(kk_, th, float(1.0 / (2.0 * np.pi)), magic, ALU.mult, ALU.add)
            fence()
            V.tensor_scalar(zz, xr, 1.0 / 128.0, None, ALU.mult)
            V.tensor_scalar(kk_, kk_, magic, None, ALU.subtract)
            fence()
            turn_parts = (6.28125, 0.0019340515136718750, 2.0 * np.pi - 6.28125 - 0.0019340515136718750)
            V.tensor_scalar(em1, zz, 1.0 / 9.0, 1.0, ALU.mult, ALU.add)
            for i, part in enumerate(turn_parts):
                V.scalar_tensor_tensor(th, kk_, -float(part), th, ALU.mult, ALU.add)
                fence()
            V.tensor_scalar(th, th, -float(np.float32(3.1415925)), float(np.float32(3.1415925)), ALU.max, ALU.min)
            fence()
            V.scalar_tensor_tensor(c2, th, -1.0, th, ALU.mult, ALU.max)
            V.tensor_scalar(s2, th, 0.5, None, ALU.mult)
            fence()
            V.tensor_scalar(c2, c2, -0.5, float(np.float32(np.pi / 2)), ALU.mult, ALU.add).then_inc(half_angle.sem, 1)
            for n in range(8, 0, -1):
                V.tensor_tensor(em1, em1, zz, ALU.mult)
                fence()
                if n > 1:
                    V.tensor_scalar(em1, em1, 1.0 / n, 1.0, ALU.mult, ALU.add)
                    fence()
            for _ in range(7):
                V.scalar_tensor_tensor(em1, em1, 2.0, em1, ALU.add, ALU.mult)
                fence()
            V.tensor_scalar(mag, em1, 1.0, None, ALU.add)
            dve.wait_ge(*sines_ready(layer, 1))
            V.scalar_tensor_tensor(sin1, s2, 2.0, c2, ALU.mult, ALU.mult)
            V.scalar_tensor_tensor(cosm1, s2, -2.0, s2, ALU.mult, ALU.mult)
            V.tensor_tensor(t2, col("lre"), col("lre"), ALU.mult)
            V.tensor_tensor(t1, col("lim"), col("lim"), ALU.mult)
            fence()
            V.tensor_scalar(pw[0][0], cosm1, 1.0, None, ALU.add)
            V.tensor_copy(pw[0][1], sin1)
            V.tensor_tensor(t2, t2, t1, ALU.add)
            V.tensor_tensor(aim, mag, sin1, ALU.mult)
            fence()
            V.tensor_tensor(are, em1, pw[0][0], ALU.mult)
            V.reciprocal(t2, t2)
            fence()
            V.tensor_tensor(are, are, cosm1, ALU.add)
            fence()
            V.tensor_tensor(kre, are, col("lre"), ALU.mult)
            V.tensor_tensor(t0, aim, col("lim"), ALU.mult)
            V.tensor_tensor(kim, aim, col("lre"), ALU.mult)
            V.tensor_tensor(t1, are, col("lim"), ALU.mult)
            fence()
            V.tensor_tensor(kre, kre, t0, ALU.add)
            V.tensor_tensor(kim, kim, t1, ALU.subtract)
            fence()
            V.tensor_tensor(kre, kre, t2, ALU.mult)
            V.tensor_tensor(kim, kim, t2, ALU.mult)
            V.memset(phase_c[:, :, 0:1], 1.0)
            V.memset(phase_s[:, :, 0:1], 0.0)
            fence()
            n = 1
            while n < SEQ:
                pc, psn = pw[0] if n in (1, 4, 16, 64) else pw[1]
                nc_, ns_ = pw[1] if n in (1, 4, 16, 64) else pw[0]
                A = s5a.rearrange("p (m t) -> p m t", m=MT)[:, :, 0:n]
                B = s5b.rearrange("p (m t) -> p m t", m=MT)[:, :, 0:n]
                pcb, psb = bc(pc[:, :, None], [P, MT, n]), bc(psn[:, :, None], [P, MT, n])
                V.tensor_tensor(A, phase_c[:, :, 0:n], pcb, ALU.mult)
                V.tensor_tensor(B, phase_s[:, :, 0:n], psb, ALU.mult)
                V.tensor_tensor(t0, pc, pc, ALU.mult)
                V.tensor_tensor(t1, psn, psn, ALU.mult)
                V.scalar_tensor_tensor(ns_, pc, 2.0, psn, ALU.mult, ALU.mult)
                fence()
                V.tensor_tensor(phase_c[:, :, n:2 * n], A, B, ALU.subtract)
                V.tensor_tensor(nc_, t0, t1, ALU.subtract)
                fence()
                V.tensor_tensor(A, phase_c[:, :, 0:n], psb, ALU.mult)
                V.tensor_tensor(B, phase_s[:, :, 0:n], pcb, ALU.mult)
                fence()
                V.tensor_tensor(phase_s[:, :, n:2 * n], A, B, ALU.add)
                fence()
                n *= 2
            cre, cim = (col(x).rearrange("p (m c) -> p m c", m=MT) for x in ("cre", "cim"))
            krb, kib = bc(kre[:, :, None], [P, MT, 32]), bc(kim[:, :, None], [P, MT, 32])
            A, B, A2, B2 = (s5a[:, i * 256:(i + 1) * 256].rearrange("p (m c) -> p m c", m=MT) for i in range(4))
            V.memset(reg[:, 4096:6144], 0.0)
            V.tensor_tensor(A, cre, krb, ALU.mult)
            V.tensor_tensor(B, cim, kib, ALU.mult)
            V.tensor_tensor(A2, cre, kib, ALU.mult)
            V.tensor_tensor(B2, cim, krb, ALU.mult)
            fence()
            for j in range(4):
                c = slice(32 * j, 32 * j + 32)
                V.tensor_tensor(cz_re[:, j:MT:4, c], A[:, j:MT:4, :], B[:, j:MT:4, :], ALU.subtract)
                V.scalar_tensor_tensor(cz_im[:, j:MT:4, c], A2[:, j:MT:4, :], -1.0, B2[:, j:MT:4, :],
                                       ALU.mult, ALU.subtract)
            V.drain().then_inc(cz_ready.sem, 1)
            for m in range(MT):
                dve.wait_ge(*bu_done(layer, m + 1))
                o = bank(m % 3).rearrange("p (r t) -> p r t", r=2)
                A = s5a[:, 0:512].rearrange("p (r t) -> p r t", r=2)
                B = s5b[:, 0:512].rearrange("p (r t) -> p r t", r=2)
                R = s5a[:, 512:1024].rearrange("p (r t) -> p r t", r=2)
                S = s5b[:, 512:1024].rearrange("p (r t) -> p r t", r=2)
                c_ = bc(phase_c[:, m:m + 1, :], [P, 2, SEQ])
                s_ = bc(phase_s[:, m:m + 1, :], [P, 2, SEQ])
                V.tensor_tensor(A, o, c_, ALU.mult)
                V.tensor_tensor(B, o, s_, ALU.mult)
                V.drain().then_inc(bu_used.sem, 1)
                V.tensor_tensor(R[:, 0, :], A[:, 0, :], B[:, 1, :], ALU.add)
                V.tensor_tensor(R[:, 1, :], A[:, 1, :], B[:, 0, :], ALU.subtract)
                fence()
                for r in range(2):
                    V.tensor_tensor_scan(S[:, r, :], bc(mag[:, m:m + 1], [P, SEQ]), R[:, r, :], 0.0, ALU.mult, ALU.add)
                fence()
                V.tensor_tensor(A, S, c_, ALU.mult)
                V.tensor_tensor(B, S, s_, ALU.mult)
                fence()
                if m >= 2:
                    dve.wait_ge(*y_acc(layer, m - 1))
                V.tensor_tensor(s5st[:, m % 2, 0, :], A[:, 0, :], B[:, 1, :], ALU.subtract)
                V.tensor_tensor(s5st[:, m % 2, 1, :], A[:, 1, :], B[:, 0, :], ALU.add)
                V.drain().then_inc(state_ready.sem, 1)
                if m < CT:
                    conv(layer, m)
                if m >= 2:
                    silu(layer, m - 2)
                if m == 5:
                    dve.wait_ge(*fill_act(layer, 5))
                    V.tensor_tensor(ga, ab[:, :, 0:4], bc(row("dt")[:, None, :], [P, TB, 4]), ALU.add)
                    fence()
                    V.scalar_tensor_tensor(gb_, ga, -1.0, ga, ALU.mult, ALU.max)
                    V.tensor_scalar(ga, ga, 0.0, None, ALU.max)
                    V.drain().then_inc(a_pre.sem, 1)
            dve.wait_ge(*a_ln(layer, 1))
            V.tensor_tensor(ga, ga, gb_, ALU.add)
            V.tensor_scalar(beta, beta, 0.5, 0.5, ALU.mult, ALU.add)
            fence()
            V.scalar_tensor_tensor(gg, ga, -1.0, bc(ea[:, None, :], [P, TB, 4]), ALU.mult, ALU.mult)
            fence()
            for c in range(TB):
                V.tensor_copy(XM[c], bc(gg[:, c, :][:, :, None], [P, HEADS, P]))
            V.drain().then_inc(g_ready.sem, 1)
            dve.wait_ge(*y_acc(layer, MT))
            for j in range(2):
                V.scalar_tensor_tensor(s5y[:, j, :], uT[:, j, :], col("dsk")[:, j:j + 1],
                                       bank(3)[:, 256 * j:256 * j + 256], ALU.mult, ALU.add)
            fence()
            V.tensor_tensor(s5w, s5y, s5y, ALU.mult)
            fence()
            V.tensor_scalar(s5w, s5w, 0.044715, 1.0, ALU.mult, ALU.add)
            fence()
            V.tensor_tensor(s5w, s5w, s5y, ALU.mult).then_inc(y_arg.sem, 1)
            V.tensor_scalar(s5y, s5y, 0.5, None, ALU.mult)
            dve.wait_ge(*gcum_done(layer, 1))
            V.tensor_copy(gc, bank(0)[:, 0:8].rearrange("p (b c) -> p b c", b=TB))
            fence()
            for c in range(TB):
                for hd in range(HEADS):
                    V.scalar_tensor_tensor(dec[c][:, hd, :], bank(1 + c)[:, hd * P:(hd + 1) * P], gc[:, c, hd:hd + 1],
                                           negT, ALU.subtract, ALU.add)
                V.drain().then_inc(dec_pre.sem, 1)
            dve.wait_ge(*y_tanh(layer, 1))
            V.scalar_tensor_tensor(s5w, s5w, 1.0, s5y, ALU.add, ALU.mult).then_inc(yT_ready.sem, 1)
            dve.wait_ge(*nat_ready(layer, TB))
            V.tensor_tensor(sreg[:, 0:1024].rearrange("p (b c) -> p b c", b=TB), nat[:, :, 0:512], nat[:, :, 0:512], ALU.mult)
            fence()
            V.tensor_reduce(qkn, sreg[:, 0:1024].rearrange("p (b h c) -> p b h c", b=TB, h=8), AX, ALU.add)
            fence()
            V.tensor_scalar(qkn, qkn, 1e-6, None, ALU.add)
            fence()
            V.reciprocal(qkn, qkn).then_inc(qk_inv.sem, 1)
            dve.wait_ge(*qk_root(layer, 1))
            V.tensor_scalar(qkn[:, :, 0:4], qkn[:, :, 0:4], DK ** -0.5, None, ALU.mult)
            fence()
            for c in range(TB):
                n8 = nat[:, c, 0:512].rearrange("p (h d) -> p h d", h=8)
                V.tensor_tensor(n8, n8, bc(qkn[:, c, :][:, :, None], [P, 8, DK]), ALU.mult)
                fence()
                bb = bc(beta[:, c, :][:, :, None], [P, HEADS, DK])
                V.tensor_tensor(kb[:, c, :].rearrange("p (h d) -> p h d", h=HEADS),
                                nat[:, c, 256:512].rearrange("p (h d) -> p h d", h=HEADS), bb, ALU.mult)
                n4 = nat[:, c, 512:768].rearrange("p (h d) -> p h d", h=HEADS)
                V.tensor_tensor(n4, n4, bb, ALU.mult)
                V.drain().then_inc(qkb_ready.sem, 1)
            dve.wait_ge(*glu_done(layer, 1))
            V.tensor_tensor(s5a[:, 0:512], bank(3), row("glb"), ALU.add).then_inc(glu_pre.sem, 1)
            dve.wait_ge(*z_tanh(layer, 1))
            V.scalar_tensor_tensor(glu_t, glu_t, 1.0, zbuf, ALU.add, ALU.mult)
            V.tensor_tensor_reduce(s5b[:, 512:576], row("lq1"), row("lk1"), 1.0, 0.0, ALU.mult, ALU.add, lsum[:, 0:1])
            V.tensor_tensor_reduce(s5b[:, 576:640], row("lq2"), row("lk2"), 1.0, 0.0, ALU.mult, ALU.add, lsum[:, 1:2])
            V.drain().then_inc(lam_sum.sem, 1)
            idb = bc(ident[:, None, :], [P, HEADS, P])
            for c in range(TB):
                dve.wait_ge(*kk_done(layer, c + 1))
                dve.wait_ge(*dec_ready(layer, c + 1))
                for r in range(2):
                    o = bank(4 * c + r).rearrange("p (k g i) -> p k g i", k=2, g=2)
                    V.tensor_tensor(LT[c][:, r:HEADS:2, :], o[:, 0], dec[c][:, r:HEADS:2, :], ALU.mult)
                    V.tensor_tensor(QK[c][:, r:HEADS:2, :], o[:, 1], dec[c][:, r:HEADS:2, :], ALU.mult)
                fence()
                V.tensor_tensor(TIT[c], LT[c], bc(lev[:, 0:1, :], [P, HEADS, P]), ALU.mult)
                V.tensor_tensor(ML[c], LT[c], bc(lev[:, 1:2, :], [P, HEADS, P]), ALU.mult)
                fence()
                V.tensor_tensor(TIT[c], idb, TIT[c], ALU.subtract).then_inc(t1T_ready.sem, 1)
            for c in range(TB):
                dve.wait_ge(*t1_done(layer, c + 1))
                V.tensor_copy(TI[c], bank(4 * c + 2).rearrange("p (h i) -> p h i", h=HEADS)).then_inc(t_ready.sem, 1)

            def glu_second():
                dve.wait_ge(*glu_done(layer, 2))
                V.tensor_tensor(s5b[:, 0:512], bank(7), row("glb"), ALU.add).then_inc(glu_pre.sem, 1)

            def glu_out():
                for t in range(TB):
                    s = s5a if t == 0 else s5b
                    dve.wait_ge(*glu_tanh(layer, t + 1))
                    V.tensor_scalar(s[:, 256:512], s[:, 256:512], 0.5, 0.5, ALU.mult, ALU.add)
                    fence()
                    V.tensor_tensor(hn[:, t, 256:512], s[:, 0:256], s[:, 256:512], ALU.mult)
                fence()

            def probs_of(r):
                return prob0 if r == 0 else prob1[:, 2 * r - 2:2 * r]

            def att_mask(r):
                t = min(r, 1)
                nk = (t + 1) * P
                pr = probs_of(r)
                nh = HEADS if r == 0 else 2
                dve.wait_ge(*att_done(layer, r + 1))
                for m in range(2):
                    o = bank(3 + 4 * m).rearrange("p (h k) -> p h k", k=nk)
                    if t == 1:
                        V.tensor_copy(pr[:, :, m, 0:P], o[:, :, 0:P])
                    V.tensor_tensor(pr[:, :, m, t * P:nk], o[:, :, t * P:nk], bc(negq[:, None, :], [P, nh, P]), ALU.add)
                fence()
                mr = mx[:, MX[r]:MX[r + 1]]
                V.tensor_reduce(mr, pr.rearrange("p h m k -> p (h m) k"), AX, ALU.max)
                fence()
                V.tensor_scalar(mr, mr, -(DK ** -0.5), None, ALU.mult).then_inc(att_max.sem, 1)

            def att_diff(r):
                if r == 0:
                    dve.wait_ge(*lam_exp(layer, 1))
                    V.tensor_tensor(lam, lsum[:, 0:1], lsum[:, 1:2], ALU.subtract)
                    fence()
                    V.tensor_tensor(lam, lam, row("laminit"), ALU.add)
                    fence()
                dve.wait_ge(*att_exp(layer, r + 1))
                z = rz[:, MX[r]:MX[r + 1]]
                V.reciprocal(z, zsum[:, MX[r]:MX[r + 1]])
                fence()
                zl = lrz[:, MX[r] // 2:MX[r + 1] // 2]
                V.tensor_scalar(zl, z.rearrange("p (h m) -> p h m", m=2)[:, :, 1], lam, -1.0, ALU.mult, ALU.mult)
                fence()
                pr = probs_of(r)
                nh = HEADS if r == 0 else 2
                for i in range(nh):
                    V.tensor_scalar(pr[:, i, 1, :], pr[:, i, 1, :], zl[:, i:i + 1], None, ALU.mult)
                fence()
                for i in range(nh):
                    V.scalar_tensor_tensor(pr[:, i, 0, :], pr[:, i, 0, :], z[:, 2 * i:2 * i + 1], pr[:, i, 1, :],
                                           ALU.mult, ALU.add)
                V.drain().then_inc(pd_ready.sem, 1)

            between = {1: [lambda: att_mask(0), glu_out], 2: [lambda: att_mask(1)],
                       3: [lambda: att_mask(2), lambda: att_diff(0)], 4: [lambda: att_diff(1)],
                       5: [lambda: att_diff(2)], 6: []}
            glu_second()
            for lv in range(1, LEVELS):
                for c in range(TB):
                    b4 = [bank(4 * c + i).rearrange("p (h i) -> p h i", h=HEADS) for i in range(3)]
                    dve.wait_ge(*upd_done(layer, TB * (lv - 1) + c + 1))
                    V.tensor_tensor(TIT[c], TIT[c], b4[1], ALU.subtract)
                    if lv < LEVELS - 1:
                        V.tensor_tensor(TI[c], TI[c], b4[2], ALU.subtract)
                        V.tensor_tensor(ML[c], LT[c], bc(lev[:, lv + 1:lv + 2, :], [P, HEADS, P]), ALU.mult)
                    V.drain().then_inc(t_ready.sem, 1)
                for step in between[lv]:
                    step()
            V.sem_inc(rhs_ready.sem, 1)
            V.tensor_tensor(kd.rearrange("p (h d) -> p h d", h=HEADS),
                            nat[:, 0, 256:512].rearrange("p (h d) -> p h d", h=HEADS),
                            bc(dec[0][:, :, P - 1:P], [P, HEADS, DK]), ALU.mult)
            V.memset(XM[0][:, :, :], 0.0)
            V.drain().then_inc(kd_ready.sem, 1)
            dve.wait_ge(*state_done(layer, 1))
            for g in range(2):
                for i in range(2):
                    r = slice(64 * i, 64 * i + 64)
                    V.tensor_copy(XM[0][r, g, r], bank(1)[r, g * P + 64 * i:g * P + 64 * i + 64])
            V.drain().then_inc(sbd_ready.sem, 1)
            dve.wait_ge(*ao_ss(layer, 1))
            V.tensor_scalar(dss, dss, 1.0 / DV2, EPS, ALU.mult, ALU.add)
            fence()
            V.reciprocal(dss, dss).then_inc(ao_inv.sem, 1)
            dve.wait_ge(*inter_done(layer, 1))
            egb = bc(eg[:, 1, :][:, :, None], [P, HEADS, DK])
            inter = [s5a[:, i * 256:(i + 1) * 256] for i in range(2)]
            for i in range(2):
                V.tensor_tensor(inter[i].rearrange("p (h d) -> p h d", h=HEADS),
                                bank(6)[:, 256 * i:256 * i + 256].rearrange("p (h d) -> p h d", h=HEADS), egb, ALU.mult)
            fence()
            V.tensor_tensor(nat[:, 1, 512:768], nat[:, 1, 512:768], inter[0], ALU.subtract).then_inc(rhs_ready.sem, 1)
            dve.wait_ge(*ao_root(layer, 1))
            V.tensor_scalar(dss, dss, row("lamrest"), None, ALU.mult)
            fence()
            for t in range(TB):
                for hd in range(HEADS):
                    ins = V.scalar_tensor_tensor(hn[:, t, 512 + hd * P:512 + (hd + 1) * P],
                                                 bank(7 - 4 * t)[:, hd * P:(hd + 1) * P],
                                                 dss[:, 4 * t + hd:4 * t + hd + 1], row("dng"), ALU.mult, ALU.mult)
                if t == 0:
                    ins.then_inc(ao_ready.sem, 1)
            og = s5b[:, 0:512].rearrange("p (b c) -> p b c", b=TB)
            og2 = s5b[:, 512:1024].rearrange("p (b c) -> p b c", b=TB)
            dve.wait_ge(*gout_done(layer, 1))
            V.tensor_copy(og[:, 0, :], bank(2)[:, 0:256])
            dve.wait_ge(*gout_done(layer, 2))
            V.tensor_tensor(og[:, 1, :], inter[1], bank(1)[:, 0:256], ALU.add)
            fence()
            V.tensor_tensor(og2, og, og, ALU.mult)
            fence()
            V.tensor_reduce(gss, og2.rearrange("p b (h d) -> p b h d", h=HEADS), AX, ALU.add)
            fence()
            V.tensor_scalar(gss, gss, 1.0 / DK, EPS, ALU.mult, ALU.add)
            fence()
            V.reciprocal(gss, gss).then_inc(go_inv.sem, 1)
            dve.wait_ge(*go_root(layer, 1))
            for t in range(TB):
                o4 = og[:, t, :].rearrange("p (h d) -> p h d", h=HEADS)
                V.tensor_tensor(o4, o4, bc(gss[:, t, :][:, :, None], [P, HEADS, DK]), ALU.mult)
                fence()
                V.tensor_tensor(o4, o4, bc(row("gng")[:, None, :], [P, HEADS, DK]), ALU.mult)
                fence()
                V.tensor_tensor(hn[:, t, 0:256], og[:, t, :], glu_t[:, t, :], ALU.mult)
                V.drain().then_inc(mix_ready.sem, 1)

            def second_norm(t):
                for half in range(2):
                    dve.wait_ge(*proj_done(layer, 2 * t + half + 1))
                    hh = h[:, t, 512 * half:512 * half + 512]
                    V.tensor_tensor(hh, hh, bank(4 + 2 * t + half), ALU.add).then_inc(resid.sem, 1)
                norm_tokens(layer, 2 + t, slice(t, t + 1))
                dve.wait_ge(*trT_ready(layer, 9))
                V.scalar_tensor_tensor(hn[:, t, :], h[:, t, :], rstd[:, t:t + 1], row("g2"), ALU.mult,
                                       ALU.mult).then_inc(hn_ready.sem, 1)

            second_norm(0)

            def top(layer, head, t, lead=False):
                dve.wait_ge(*sc_ready(layer, 1 if lead else head + 2))
                if lead:
                    V.tensor_copy(expoff, row("expoff"))
                else:
                    V.tensor_copy(scur, scores[:, t, bass.ds(head, 1), :].rearrange("p o (a n) -> p (o a) n", a=2))
                fence()
                for a in range(2):
                    V.max(sv[:, a, 0:8], scur[:, a, :])
                fence()
                for a in range(2):
                    V.max_index(si[:, a, 0:8], sv[:, a, 0:8], scur[:, a, :])
                    V.match_replace(scur2[:, a, :], sv[:, a, 0:8], scur[:, a, :], LOWEST)
                fence()
                for a in range(2):
                    V.max(sv[:, a, 8:16], scur2[:, a, :])
                fence()
                for a in range(2):
                    V.max_index(si[:, a, 8:16], sv[:, a, 8:16], scur2[:, a, :])
                c2d = cand.rearrange("p (a b) -> p a b", a=TOPK)
                V.tensor_tensor(c2d, bc(sv[:, 0, :][:, :, None], [P, TOPK, TOPK]),
                                bc(sv[:, 1, :][:, None, :], [P, TOPK, TOPK]), ALU.add)
                fence()
                V.tensor_copy(sif, si)
                V.max(tv[:, 0:8], cand)
                fence()
                V.max_index(tp[:, 0:8], tv[:, 0:8], cand)
                V.match_replace(cand2, tv[:, 0:8], cand, LOWEST)
                fence()
                V.max(tv[:, 8:16], cand2)
                fence()
                V.max_index(tp[:, 8:16], tv[:, 8:16], cand2)
                V.tensor_scalar(gate[:, t, :], tv, tv[:, 0:1], None, ALU.subtract).then_inc(top_ready.sem, 1)
                fence()
                V.tensor_scalar(ab_u[:, 0, :], tp, 4, None, ALU.logical_shift_right)
                V.tensor_scalar(ab_u[:, 1, :], tp, 15, None, ALU.bitwise_and)
                fence()
                V.tensor_copy(ab_f, ab_u)
                fence()
                V.tensor_tensor(onehot.rearrange("p a k n -> p (a k) n"),
                                bc(ab_f.rearrange("p a k -> p (a k)")[:, :, None], [P, 2 * TOPK, TOPK]),
                                bc(iota[:, None, :], [P, 2 * TOPK, TOPK]), ALU.is_equal)
                fence()
                for a in range(2):
                    V.tensor_tensor(onehot[:, a, :, :], onehot[:, a, :, :],
                                    bc(sif[:, a, :][:, None, :], [P, TOPK, TOPK]), ALU.mult)
                fence()
                V.tensor_reduce(eij.rearrange("p a k -> p (a k)"), onehot.rearrange("p a k n -> p (a k) n"), AX, ALU.add)
                fence()
                V.scalar_tensor_tensor(eij[:, 0, :], eij[:, 0, :], float(NKEY), eij[:, 1, :], ALU.mult, ALU.add)
                fence()
                if not lead:
                    dve.wait_ge(*v_used(layer, (head * TB + t - 1) * TOPK))
                V.tensor_scalar(ids[:, t, :], eij[:, 0, :], expoff, None, ALU.add).then_inc(ids_ready.sem, 1)

            def use(layer, head, t, following):
                n = head * TB + t
                dve.wait_ge(*xy_ready(layer, t + 1))
                xt = ps[:, 2 * t:2 * t + 2, :].rearrange("p b n -> p (b n)")
                for k in range(TOPK):
                    if k == TOPK // 2 and following is not None:
                        following()
                    dve.wait_ge(*u_in[k](layer, n * 16 + 16))
                    V.tensor_tensor_reduce(uring[:, k, :], uring[:, k, :], xt, 1.0, 0.0, ALU.mult, ALU.add,
                                           dots[:, t, k:k + 1]).then_inc(dot_done.sem, 1)
                fence()
                dt_ = dots[:, t, :]
                V.tensor_tensor(ge[:, 0, :], dt_, dt_, ALU.mult)
                fence()
                V.tensor_scalar(ge[:, 0, :], ge[:, 0, :], 0.044715, 1.0, ALU.mult, ALU.add)
                fence()
                V.tensor_tensor(gt[:, t, :], ge[:, 0, :], dt_, ALU.mult).then_inc(gelu_arg.sem, 1)
                dve.wait_ge(*gexp_ready(layer, n + 1))
                V.reciprocal(nmax[:, t:t + 1], gz[:, t:t + 1])
                fence()
                V.tensor_scalar(dt_, dt_, nmax[:, t:t + 1], 0.5, ALU.mult, ALU.mult)
                fence()
                V.tensor_tensor(dt_, dt_, gate[:, t, :], ALU.mult)
                fence()
                dve.wait_ge(*gelu_tanh(layer, n + 1))
                V.scalar_tensor_tensor(pk[:, t, :], gt[:, t, :], 1.0, dt_, ALU.add, ALU.mult).then_inc(p_ready.sem, 1)

            top(layer, 0, 0, lead=True)
            second_norm(1)
            with dve.Fori(0, PH - 1) as head:
                use(layer, head, 0, lambda: top(layer, head, 1))
                use(layer, head, 1, lambda: top(layer, head + 1, 0))
            use(layer, PH - 1, 0, lambda: top(layer, PH - 1, 1))
            use(layer, PH - 1, 1, None)
            for t in range(TB):
                dve.wait_ge(*v_used(layer, (NG - 1 + t) * TOPK))
                V.tensor_copy(h[:, t, :], ps[:, 4 + 2 * t:6 + 2 * t, :].rearrange("p b n -> p (b n)"))
                fence()
                square(t)
            fence()
        V.tensor_scalar(rstd, ss, 1.0 / D, EPS, ALU.mult, ALU.add)
        fence()
        V.reciprocal(rstd, rstd).then_inc(final_inv.sem, 1)
        dve.wait_ge(final_root.sem, 1)
        dve.wait_ge(fin_in.sem, 16)
        for t in range(TB):
            V.scalar_tensor_tensor(hn[:, t, :], h[:, t, :], rstd[:, t:t + 1], row("g2"), ALU.mult,
                                   ALU.mult).then_inc(final_ready.sem, 1)

    @block.scalar
    def _(act):
        S = nc.scalar
        fence = S.drain

        act.wait_ge(cst_in.sem, 16)
        act.wait_ge(x_in.sem, 16)
        with act.Fori(0, DEPTH) as layer:
            act.wait_ge(*inv_ready(layer, 1))
            S.activation(rstd, rstd, ACT.Sqrt).then_inc(rstd_ready.sem, 1)
            act.wait_ge(*params_in(layer, 48))
            S.activation(stp, col("lst"), ACT.Exp).then_inc(step_ready.sem, 1)
            act.wait_ge(*half_angle(layer, 1))
            S.activation(s2, s2, ACT.Sin)
            S.activation(c2, c2, ACT.Sin)
            S.drain().then_inc(sines_ready.sem, 1)
            for b in range(4):
                act.wait_ge(*tr_done(layer, b + 1))
                for k in range(2):
                    S.activation(hnT[:, 2 * b + k, :], bank(4 + b)[:, 256 * k:256 * k + 256], ACT.Copy,
                                 scale=col("g1")[:, 2 * b + k:2 * b + k + 1])
                S.drain().then_inc(trT_ready.sem, 1)
            act.wait_ge(*pads_ready(layer, 1))
            dests = {f"qkv{i}": raw[:, 2 * i:2 * i + 2, 3:3 + SEQ] for i in range(3)}
            dests |= {"u": uT, "z": zbuf, "v0": vbuf[:, :, 0:256], "v1": vbuf[:, :, 256:512],
                     "q0": qT[:, 0:2, :], "q1": qT[:, 2:4, :], "k0": kT[:, 0:2, :], "k1": kT[:, 2:4, :]}
            for f, name in enumerate(FILLS):
                act.wait_ge(*fill_done(layer, f + 1))
                o = bank(4 + f % 4)
                if name == "ab":
                    S.activation(ab, o[:, 0:16].rearrange("p (b c) -> p b c", b=TB), ACT.Copy).then_inc(fill_act.sem, 1)
                else:
                    S.activation(dests[name], o.rearrange("p (b c) -> p b c", b=2), ACT.Copy).then_inc(fill_act.sem, 1)
                j = f - 5
                if 0 <= j < CT:
                    act.wait_ge(*conv_done(layer, j + 1))
                    S.activation(nat_tanh(j), convd[:, j, :], ACT.Tanh).then_inc(conv_tanh.sem, 1)
                if f == 10:
                    act.wait_ge(*a_pre(layer, 1))
                    S.activation(beta, ab[:, :, 4:8], ACT.Tanh, scale=0.5)
                    S.activation(gb_, gb_, ACT.Exp, scale=-1.0)
                    S.activation(ea, row("alog"), ACT.Exp)
                    fence()
                    S.activation(gb_, gb_, ACT.Ln, bias=1.0)
                    S.drain().then_inc(a_ln.sem, 1)
            act.wait_ge(*y_arg(layer, 1))
            S.activation(s5w, s5w, ACT.Tanh, scale=float(np.sqrt(2.0 / np.pi))).then_inc(y_tanh.sem, 1)
            S.activation(glu_t, zbuf, ACT.Tanh, scale=0.5)
            S.activation(zbuf, zbuf, ACT.Copy, scale=0.5)
            S.drain().then_inc(z_tanh.sem, 1)
            for c in range(TB):
                act.wait_ge(*nat_done(layer, c + 1))
                S.activation(nat[:, c, 0:512], bank(4 + 2 * c), ACT.Copy)
                S.activation(nat[:, c, 512:768], bank(5 + 2 * c)[:, 0:256], ACT.Copy)
                S.drain().then_inc(nat_ready.sem, 1)
            for c in range(TB):
                act.wait_ge(*dec_pre(layer, c + 1))
                S.activation(dec[c], dec[c], ACT.Exp)
                S.drain().then_inc(dec_ready.sem, 1)
            S.activation(eg, gc, ACT.Exp)
            act.wait_ge(*qk_inv(layer, 1))
            S.activation(qkn, qkn, ACT.Sqrt).then_inc(qk_root.sem, 1)
            for c in range(TB):
                act.wait_ge(*keyT_done(layer, c + 1))
                S.activation(keyT[c][:, 0:2, :, :], bank(4 + 2 * c).rearrange("p (k g t) -> p k g t", k=2, g=2), ACT.Copy)
                S.activation(keyT[c][:, 2, :, :], bank(5 + 2 * c)[:, 0:256].rearrange("p (g t) -> p g t", g=2), ACT.Copy)
                S.drain().then_inc(keyT_ready.sem, 1)
            act.wait_ge(*lam_sum(layer, 1))
            S.activation(lsum, lsum, ACT.Exp).then_inc(lam_exp.sem, 1)

            def glu_gates():
                for t in range(TB):
                    s = s5a if t == 0 else s5b
                    act.wait_ge(*glu_pre(layer, t + 1))
                    S.activation(s[:, 256:512], s[:, 256:512], ACT.Tanh, scale=0.5).then_inc(glu_tanh.sem, 1)

            def att_exps(r):
                prob = (prob0 if r == 0 else prob1[:, 2 * r - 2:2 * r]).rearrange("p h m k -> p (h m) k")
                act.wait_ge(*att_max(layer, r + 1))
                for i in range(MX[r + 1] - MX[r]):
                    at = MX[r] + i
                    S.activation(prob[:, i, :], prob[:, i, :], ACT.Exp, bias=mx[:, at:at + 1],
                                 scale=DK ** -0.5, accum_out=zsum[:, at:at + 1])
                S.drain().then_inc(att_exp.sem, 1)

            def att_copy(r):
                act.wait_ge(*pT_done(layer, r + 1))
                if r == 0:
                    S.activation(pT0, bank(3).rearrange("p (b g q) -> p b g q", b=2, g=2), ACT.Copy).then_inc(pT_ready.sem, 1)
                else:
                    S.activation(pT1.rearrange("p h c q -> p (h c q)")[:, 512 * (r - 1):512 * r],
                                 bank(7 if r == 1 else 3), ACT.Copy).then_inc(pT_ready.sem, 1)

            between = {1: [glu_gates], 2: [lambda: att_exps(0)], 3: [lambda: att_exps(1)],
                       4: [lambda: att_exps(2)], 5: [lambda: att_copy(0)], 6: [lambda: att_copy(1), lambda: att_copy(2)]}
            for lv in range(1, LEVELS):
                for c in range(TB):
                    act.wait_ge(*x_done(layer, TB * (lv - 1) + c + 1))
                    S.activation(XM[c], bank(4 * c).rearrange("p (h i) -> p h i", h=HEADS), ACT.Copy).then_inc(x_ready.sem, 1)
                for step in between[lv]:
                    step()
            def copy_tiles(n, first, tiles, src, t):
                act.wait_ge(*tr_done(layer, n))
                S.activation(hnT[:, first:first + tiles, t * P:(t + 1) * P],
                             src.rearrange("p (k t) -> p k t", k=tiles), ACT.Copy)
                S.drain().then_inc(trT_ready.sem, 1)

            def copy_new_values(c):
                act.wait_ge(*vnew_done(layer, c + 1))
                S.activation(unew[:, c, :], bank(0)[:, 0:256], ACT.Copy).then_inc(vnew_ready.sem, 1)

            copy_new_values(0)
            copy_tiles(5, 2, 2, bank(0)[:, 0:256], 0)
            for t in range(TB):
                act.wait_ge(*ao_done(layer, t + 1))
                for hd in range(HEADS):
                    S.activation(sreg[:, 2048 + t * 512 + hd * P:2048 + t * 512 + (hd + 1) * P],
                                 bank(7 - 4 * t)[:, hd * P:(hd + 1) * P], ACT.Square,
                                 accum_out=dss[:, 4 * t + hd:4 * t + hd + 1])
            S.drain().then_inc(ao_ss.sem, 1)
            act.wait_ge(*ao_inv(layer, 1))
            S.activation(dss, dss, ACT.Sqrt).then_inc(ao_root.sem, 1)
            copy_new_values(1)
            copy_tiles(6, 4, 4, bank(7), 0)
            act.wait_ge(*go_inv(layer, 1))
            S.activation(gss, gss, ACT.Sqrt).then_inc(go_root.sem, 1)
            copy_tiles(7, 0, 2, bank(0)[:, 0:256], 0)
            for b in range(2):
                copy_tiles(8 + b, 4 * b, 4, bank(2 + b), 1)

            def second_norm(t):
                act.wait_ge(*resid(layer, 2 * t + 2))
                S.activation(hn[:, t, :], h[:, t, :], ACT.Square, accum_out=ss[:, t:t + 1])
                S.drain().then_inc(ss_ready.sem, 1)
                act.wait_ge(*inv_ready(layer, 2 + t))
                S.activation(rstd[:, t:t + 1], rstd[:, t:t + 1], ACT.Sqrt).then_inc(rstd_ready.sem, 1)
                for b in range(2):
                    copy_tiles(10 + 2 * t + b, 4 * b, 4, bank(2 * t + b), t)
                for j in range(2):
                    S.activation(bank(2 * t + j), hn[:, t, 512 * j:512 * j + 512], ACT.Copy)
                S.drain().then_inc(xy_ready.sem, 1)

            second_norm(0)
            act.wait_ge(*pq_done(layer, 1))
            S.activation(diag[:, 0, :], bank(4)[:, 0:P], ACT.Copy).then_inc(pq_ready.sem, 1)
            act.wait_ge(*sc_done(layer, 1))
            for a in range(2):
                S.activation(scur[:, a, :], bank(4 + a)[:, 0:NKEY], ACT.Copy)
            S.drain().then_inc(sc_ready.sem, 1)
            second_norm(1)
            for i in range(4):
                act.wait_ge(*pq_done(layer, i + 2))
                S.activation(qpT[:, 2 * i:2 * i + 2, :], bank(4 + i % 2).rearrange("p (b t) -> p b t", b=2), ACT.Copy).then_inc(pq_ready.sem, 1)
                act.wait_ge(*sc_done(layer, i + 2))
                for a in range(2):
                    S.activation(scores[:, :, 2 * i:2 * i + 2, a * NKEY:(a + 1) * NKEY],
                                 bank(6 + a).rearrange("p (t h n) -> p t h n", t=TB, h=2), ACT.Copy)
                S.drain().then_inc(sc_ready.sem, 2)

            def softmax(layer, head, t):
                n = head * TB + t
                act.wait_ge(*top_ready(layer, n + 1))
                S.activation(gate[:, t, :], gate[:, t, :], ACT.Exp, accum_out=gz[:, t:t + 1])
                S.drain().then_inc(gexp_ready.sem, 1)

            def gates(layer, head, t):
                n = head * TB + t
                act.wait_ge(*gelu_arg(layer, n + 1))
                S.activation(gt[:, t, :], gt[:, t, :], ACT.Tanh, scale=float(np.sqrt(2.0 / np.pi))).then_inc(gelu_tanh.sem, 1)
                act.wait_ge(*p_ready(layer, n + 1))
                for k in range(TOPK):
                    act.wait_ge(*v_used(layer, n * TOPK + (k - 3)))
                    S.activation(diag[:, k % 4, :], ident, ACT.Copy, scale=pk[:, t, k:k + 1]).then_inc(diag_ready.sem, 1)

            with act.Fori(0, PH) as head:
                for t in range(TB):
                    softmax(layer, head, t)
                    gates(layer, head, t)
        act.wait_ge(final_inv.sem, 1)
        S.activation(rstd, rstd, ACT.Sqrt).then_inc(final_root.sem, 1)

    @block.gpsimd
    def _(pool):
        def gather(dst, table, index, done):
            nc.gpsimd.indirect_dma_start(dst, None, table, bass.IndirectOffsetOnAxis(ap=index, axis=0)
                                         ).then_inc(done.sem, 16)

        def u_rows(layer, n, t, slots, first=False):
            for k in slots:
                pool.wait_ge(*dot_done(layer, (n - 1) * TOPK + (k + 1)))
                pool.sem_inc(pool_gate.sem, 1)
                if first and k >= TOPK // 2 and k % 2 == 0:
                    pool.wait_ge(*w_used(layer, NB - (TOPK - k) // 2 + 1))
                    pool.sem_inc(pool_gate.sem, 1)
                gather(uring[:, k, :], u_tab, ids[:, t, k:k + 1], u_in[k])

        def v_rows(layer, n, t, slots):
            for k in slots:
                pool.wait_ge(*v_used(layer, (n - 1) * TOPK + (k + 1)))
                pool.sem_inc(pool_gate.sem, 1)
                gather(vring[:, k, :], v_tab, ids[:, t, k:k + 1], v_in[k])

        def group(layer, n, t):
            pool.wait_ge(*ids_ready(layer, n + 1))
            pool.sem_inc(pool_gate.sem, 1)
            u_rows(layer, n, t, range(TOPK))
            v_rows(layer, n, t, range(TOPK))

        with pool.Fori(0, DEPTH) as layer:
            pool.wait_ge(*ids_ready(layer, 1))
            pool.sem_inc(pool_gate.sem, 1)
            pool.wait_ge(*w_used(layer, NB - 4))
            pool.sem_inc(pool_gate.sem, 1)
            u_rows(layer, 0, 0, range(TOPK // 2))
            v_rows(layer, 0, 0, range(TOPK - 2))
            u_rows(layer, 0, 0, range(TOPK // 2, TOPK), first=True)
            pool.wait_ge(*sc_done(layer, 5))
            pool.sem_inc(pool_gate.sem, 1)
            v_rows(layer, 0, 0, range(TOPK - 2, TOPK))
            with pool.Fori(0, PH - 1) as head:
                for t in (1, 0):
                    group(layer, head * TB + (2 - t), t)
            group(layer, NG - 1, 1)


def kernel(**inputs):
    import concourse.bacc as bacc
    from concourse.bass_utils import run_bass_kernel_spmd

    a = {k: np.asarray(v) for k, v in inputs.items()}
    L = DEPTH

    def tiles(w):
        return w.reshape(L, KT, P, -1).transpose(0, 2, 1, 3)

    w_in, w_out, w_q = tiles(a["w_in"]), tiles(a["w_out"]), tiles(a["peer_wq"])
    blocks = [w_in[..., c:c + BLK] for c in IN_COLS.values()]
    blocks += [w[..., i * BLK:(i + 1) * BLK] for w in (w_out, w_q) for i in range(4)]
    w_blocks = np.stack(blocks, 1).reshape(L * NB, P, KT * BLK)

    def states(v):
        return v.reshape(L, MT, P).transpose(0, 2, 1)

    cols = np.zeros((L, P, NCOLS), np.float32)

    def put(arr, where, name, value):
        lo, hi = where[name]
        arr[:, :, lo:hi] = value.reshape(L, -1, hi - lo)

    put(cols, COLS, "g1", a["norm1_g"].reshape(L, KT, P).transpose(0, 2, 1))
    put(cols, COLS, "conv", a["gdn_conv_w"].reshape(L, CONV, CT, P).transpose(0, 3, 2, 1))
    put(cols, COLS, "lre", states(a["s5_lambda_re"]))
    put(cols, COLS, "lim", states(a["s5_lambda_im"]))
    put(cols, COLS, "lst", states(np.repeat(a["s5_log_step"][:, :, None], NSTATE, 2)))
    put(cols, COLS, "dsk", a["s5_d"].reshape(L, 2, P).transpose(0, 2, 1))
    put(cols, COLS, "wab", w_in[..., 1024:1032])
    for name, key in (("bre", "s5_b_re"), ("bim", "s5_b_im")):
        b = np.zeros((L, 2, P, P), np.float32)
        for g in range(GROUPS):
            r = GCH * (g % 8)
            c = NSTATE * (g % 2)
            b[:, g // 8, r:r + GCH, c:c + NSTATE] = a[key][:, g].transpose(0, 2, 1)
        put(cols, COLS, name, b.transpose(0, 2, 1, 3))
    for name, key in (("cre", "s5_c_re"), ("cim", "s5_c_im")):
        c = np.zeros((L, P, MT, 32), np.float32)
        for g in range(GROUPS):
            i = g % 2
            c[:, NSTATE * i:NSTATE * (i + 1), g // 2, GCH * i:GCH * (i + 1)] = a[key][:, g].transpose(0, 2, 1)
        put(cols, COLS, name, c)
    put(cols, COLS, "glu", a["s5_glu_w"].reshape(L, 2, P, 512).transpose(0, 2, 1, 3))

    rows = np.zeros((L, 1, NROWS), np.float32)
    for name, key in (("alog", "gdn_a_log"), ("dt", "gdn_dt_bias"), ("gng", "gdn_norm_g"), ("lq1", "diff_lq1"),
                      ("lk1", "diff_lk1"), ("lq2", "diff_lq2"), ("lk2", "diff_lk2"), ("dng", "diff_norm_g"),
                      ("glb", "s5_glu_b"), ("g2", "norm2_g")):
        put(rows, ROWS, name, a[key])
    lam_init = np.array([0.8 - 0.6 * np.exp(-0.3 * i) for i in range(L)])
    put(rows, ROWS, "laminit", lam_init)
    put(rows, ROWS, "lamrest", 1.0 - lam_init)
    put(rows, ROWS, "expoff", np.arange(L) * float(NEXP))
    rows = np.repeat(rows, P, 1)

    keys = a["peer_keys"].transpose(0, 2, 4, 1, 3).reshape(L, P, PH * NKEY)

    i, j = np.arange(P)[None, :], np.arange(P)[:, None]
    cst = np.zeros((P, NCST), np.float32)
    levels = [((i >> (l + 1)) == (j >> (l + 1))) & ((i >> l) % 2 == 1) & ((j >> l) % 2 == 0) for l in range(LEVELS)]
    for name, value in (("ident", i == j), ("tri", j <= i), ("negT", np.where(j <= i, 0.0, NEG)),
                        ("negq", np.where(i <= j, 0.0, NEG)), ("lev", np.concatenate(levels, 1)),
                        ("iota", np.tile(np.arange(TOPK), (P, 1)))):
        cst[:, CST[name][0]:CST[name][1]] = value

    arrays = {
        "x": a["x"], "w_blocks": w_blocks, "cols": cols, "rows": rows, "keys": keys,
        "u_tab": a["peer_u"].reshape(L * NEXP, D), "v_tab": a["peer_v"].reshape(L * NEXP, D),
        "cst": cst, "final_g": np.repeat(a["final_g"][None, :], P, 0),
    }
    nc = bacc.Bacc("TRN2", target_bir_lowering=False, num_devices=1)
    named = {f"in_{k}": np.ascontiguousarray(v) for k, v in arrays.items()}
    args = [nc.dram_tensor(k, v.shape, F32, kind="ExternalInput").ap() for k, v in named.items()]
    args.append(nc.dram_tensor("out_0", (1, SEQ, D), F32, kind="ExternalOutput").ap())
    build(nc, *args)
    r = run_bass_kernel_spmd(nc, [named], core_ids=[0])
    return r.results[0]["out_0"]
```
